# Optimizing a Trainium2 kernel written in Bass

```python
import math
import jax, jax.numpy as jnp
from jax import lax
import numpy as np
import jax
import jax.numpy as jnp

D_MODEL = 1024
BATCH = 1
SEQ = 256
DEPTH = 2

M_HEADS = 4
M_QK = 64
M_V = 128
M_WIDTH = M_HEADS * M_V
CONV_W = 4
A_HEADS = 8
A_HEAD_DIM = 64
A_WIDTH = A_HEADS * A_HEAD_DIM
Q_RANK = 256
KV_RANK = 128
IDX_HEADS = 8
IDX_DIM = 64
TOPK_MAX = 256
R_HEADS = 4
R_QK = 128
R_V = 128
R_WIDTH = R_HEADS * R_V
CHUNK = 128
Q_BLOCK = 128
N_BUCKETS = 32
MAX_DISTANCE = 128
ROPE_BASE = 10000.0
EPS = 1e-6
D_FF = -(((-8 * D_MODEL) // 3) // 256) * 256
IN_SPLITS = (M_HEADS * M_QK, M_HEADS * M_QK, M_WIDTH, M_HEADS, M_HEADS, M_WIDTH,
             Q_RANK, IDX_DIM, IDX_HEADS, KV_RANK,
             R_HEADS * R_QK, R_HEADS * R_QK, R_WIDTH, R_WIDTH,
             D_MODEL, D_MODEL, D_MODEL)
D_IN = sum(IN_SPLITS)


def rms_norm(x, g):
    xf = x.astype(jnp.float32)
    y = xf * lax.rsqrt(jnp.mean(xf * xf, axis=-1, keepdims=True) + EPS)
    return (y * g.astype(jnp.float32)).astype(x.dtype)

def layer_norm(x, g):
    xf = x.astype(jnp.float32)
    mu = jnp.mean(xf, axis=-1, keepdims=True)
    xc = xf - mu
    y = xc * lax.rsqrt(jnp.mean(xc * xc, axis=-1, keepdims=True) + EPS)
    return (y * g.astype(jnp.float32)).astype(x.dtype)

def head_layer_norm(x, g):
    return layer_norm(x, g.reshape(x.shape[-2:]))

def causal_conv(x, w):
    k_w, c = w.shape
    return lax.conv_general_dilated(x, w[:, None, :].astype(x.dtype), window_strides=(1,),
                                    padding=[(k_w - 1, 0)],
                                    dimension_numbers=('NWC', 'WIO', 'NWC'),
                                    feature_group_count=c)

def rotary(x, pos):
    half = x.shape[-1] // 2
    freqs = ROPE_BASE ** (-jnp.linspace(0.0, 1.0, half, dtype=jnp.float32))
    ang = pos[:, None] * freqs[None, :]
    cos = jnp.cos(ang)[:, None, :]
    sin = jnp.sin(ang)[:, None, :]
    xf = x.astype(jnp.float32)
    x1, x2 = xf[..., :half], xf[..., half:]
    return jnp.concatenate([x1 * cos - x2 * sin, x1 * sin + x2 * cos], axis=-1).astype(x.dtype)

def t5_bucket(dist):
    max_exact = N_BUCKETS // 2
    d_f = jnp.maximum(dist, 1).astype(jnp.float32)
    large = max_exact + (jnp.log(d_f / max_exact) / math.log(MAX_DISTANCE / max_exact)
                         * (N_BUCKETS - max_exact)).astype(jnp.int32)
    large = jnp.minimum(large, N_BUCKETS - 1)
    return jnp.where(dist < max_exact, dist, large)

def to_chunks(x):
    b, s, h = x.shape[:3]
    rest = x.shape[3:]
    x = x.reshape((b, s // CHUNK, CHUNK, h) + rest)
    return jnp.transpose(x, (1, 0, 3, 2) + tuple(range(4, x.ndim)))

def from_chunks(x):
    n, b, h, l, d = x.shape
    return jnp.transpose(x, (1, 0, 3, 2, 4)).reshape(b, n * l, h, d)

def mlstm(q, k, v, i_pre, f_pre):
    dtype = v.dtype
    b, s, h, dk = q.shape
    dv = v.shape[-1]
    f32 = jnp.float32
    q = q.astype(f32) * dk ** -0.5
    k = k.astype(f32)
    v = v.astype(f32)
    log_f = jax.nn.log_sigmoid(f_pre.astype(f32))
    log_i = i_pre.astype(f32)
    causal = jnp.tril(jnp.ones((CHUNK, CHUNK), dtype=bool))

    def step(carry, inp):
        c_st, n_st, m_st = carry
        qc, kc, vc, lf, li = inp
        bcum = jnp.cumsum(lf, axis=-1)
        d_log = bcum[..., :, None] - bcum[..., None, :] + li[..., None, :]
        d_log = jnp.where(causal, d_log, -jnp.inf)
        inter = bcum + m_st[..., None]
        m_row = jnp.maximum(inter, jnp.max(d_log, axis=-1))
        w_intra = jnp.exp(d_log - m_row[..., None])
        w_inter = jnp.exp(inter - m_row)
        sc = jnp.einsum('bhld,bhrd->bhlr', qc, kc) * w_intra
        num = (jnp.einsum('bhlr,bhrv->bhlv', sc, vc)
               + w_inter[..., None] * jnp.einsum('bhld,bhdv->bhlv', qc, c_st))
        den = jnp.sum(sc, axis=-1) + w_inter * jnp.einsum('bhld,bhd->bhl', qc, n_st)
        out = num / jnp.maximum(jnp.abs(den), jnp.exp(-m_row))[..., None]
        b_last = bcum[..., -1]
        g_log = b_last[..., None] - bcum + li
        m_new = jnp.maximum(b_last + m_st, jnp.max(g_log, axis=-1))
        wk = jnp.exp(g_log - m_new[..., None])
        decay = jnp.exp(b_last + m_st - m_new)
        c_new = decay[..., None, None] * c_st + jnp.einsum('bhl,bhld,bhlv->bhdv', wk, kc, vc)
        n_new = decay[..., None] * n_st + jnp.einsum('bhl,bhld->bhd', wk, kc)
        return (c_new, n_new, m_new), out

    init = (jnp.zeros((b, h, dk, dv), f32), jnp.zeros((b, h, dk), f32), jnp.zeros((b, h), f32))
    _, out = lax.scan(step, init, (to_chunks(q), to_chunks(k), to_chunks(v),
                                   to_chunks(log_f), to_chunks(log_i)))
    return from_chunks(out).astype(dtype)

def retention(q, k, v):
    dtype = v.dtype
    b, s, h, dk = q.shape
    dv = v.shape[-1]
    f32 = jnp.float32
    q = q.astype(f32)
    k = k.astype(f32) * dk ** -0.5
    v = v.astype(f32)
    log_gamma = jnp.log1p(-jnp.exp2(-5.0 - jnp.arange(h, dtype=f32)))
    pos = jnp.arange(CHUNK, dtype=f32)
    diff = pos[:, None] - pos[None, :]
    intra = jnp.where(diff >= 0, jnp.exp(jnp.maximum(diff, 0.0)[None] * log_gamma[:, None, None]), 0.0)
    q_decay = jnp.exp((pos[None, :] + 1.0) * log_gamma[:, None])
    k_decay = jnp.exp((CHUNK - 1.0 - pos[None, :]) * log_gamma[:, None])
    chunk_decay = jnp.exp(CHUNK * log_gamma)

    def step(state, inp):
        qc, kc, vc = inp
        sc = jnp.einsum('bhld,bhrd->bhlr', qc, kc) * intra
        out = (jnp.einsum('bhlr,bhrv->bhlv', sc, vc)
               + q_decay[..., None] * jnp.einsum('bhld,bhdv->bhlv', qc, state))
        state = chunk_decay[:, None, None] * state + jnp.einsum('bhrd,hr,bhrv->bhdv', kc, k_decay, vc)
        return state, out

    _, out = lax.scan(step, jnp.zeros((b, h, dk, dv), f32), (to_chunks(q), to_chunks(k), to_chunks(v)))
    return from_chunks(out).astype(dtype)

def dsa_attention(q_lat, c_kv, q_idx, k_idx, w_idx, rel_bias):
    b, s = c_kv.shape[:2]
    top_k = min(TOPK_MAX, s // 4)
    key_pos = jnp.arange(s, dtype=jnp.int32)
    f32 = jnp.float32

    def block(start):
        qb = lax.dynamic_slice_in_dim(q_lat, start, Q_BLOCK, axis=1)
        qib = lax.dynamic_slice_in_dim(q_idx, start, Q_BLOCK, axis=1)
        wb = lax.dynamic_slice_in_dim(w_idx, start, Q_BLOCK, axis=1)
        q_pos = start + jnp.arange(Q_BLOCK, dtype=jnp.int32)
        head_sc = jax.nn.relu(jnp.einsum('btgd,bsd->btgs', qib, k_idx).astype(f32))
        idx_sc = jnp.einsum('btg,btgs->bts', wb.astype(f32), head_sc)
        idx_sc = jnp.where(key_pos[None, None, :] <= q_pos[None, :, None], idx_sc, -jnp.inf)
        _, sel = lax.top_k(idx_sc, top_k)
        valid = sel <= q_pos[None, :, None]
        kv_sel = jax.vmap(lambda c, i: c[i])(c_kv, sel)
        logits = jnp.einsum('bthc,btkc->bthk', qb, kv_sel).astype(f32)
        bias = rel_bias.astype(f32)[t5_bucket(q_pos[None, :, None] - sel)]
        logits = logits + jnp.swapaxes(bias, -1, -2)
        logits = jnp.where(valid[:, :, None, :], logits, -jnp.inf)
        probs = jax.nn.softmax(logits, axis=-1).astype(c_kv.dtype)
        return jnp.einsum('bthk,btkc->bthc', probs, kv_sel)

    starts = jnp.arange(s // Q_BLOCK, dtype=jnp.int32) * Q_BLOCK
    out = lax.map(block, starts)
    return jnp.moveaxis(out, 0, 1).reshape(b, s, A_HEADS, KV_RANK)

def hybrid_layer(x, rel_bias, norm1_g, w_in, m_conv, m_ibias, m_fbias, m_norm_g,
                 a_qnorm_g, a_wuq, a_wuq_idx, a_kidx_g, a_kvnorm_g, a_wuk, a_wuv,
                 r_norm_g, p_m, p_a, p_r, w_out, norm2_g, w_gate, w_up, w_down):
    b, s, _ = x.shape
    h = rms_norm(x, norm1_g)
    z = h @ w_in
    split_points = [int(c) for c in np.cumsum(IN_SPLITS)[:-1]]
    (m_q, m_k, m_v, m_i, m_f, m_o, a_cq, a_kidx, a_widx, a_ckv,
     r_q, r_k, r_v, r_g, g_m, g_a, g_r) = jnp.split(z, split_points, axis=-1)

    qk = jax.nn.silu(causal_conv(jnp.concatenate([m_q, m_k], axis=-1), m_conv))
    mq, mk = jnp.split(qk, 2, axis=-1)
    hm = mlstm(mq.reshape(b, s, M_HEADS, M_QK), mk.reshape(b, s, M_HEADS, M_QK),
               m_v.reshape(b, s, M_HEADS, M_V), m_i + m_ibias, m_f + m_fbias)
    hm = head_layer_norm(hm, m_norm_g).reshape(b, s, M_WIDTH) * jax.nn.sigmoid(m_o)

    c_q = rms_norm(a_cq, a_qnorm_g)
    q = (c_q @ a_wuq).reshape(b, s, A_HEADS, A_HEAD_DIM)
    q_idx = (c_q @ a_wuq_idx).reshape(b, s, IDX_HEADS, IDX_DIM)
    k_idx = layer_norm(a_kidx, a_kidx_g)
    w_idx = a_widx * (IDX_HEADS ** -0.5 * IDX_DIM ** -0.5)
    c_kv = rms_norm(a_ckv, a_kvnorm_g)
    q_lat = jnp.einsum('bshd,hdc->bshc', q, a_wuk) * A_HEAD_DIM ** -0.5
    o_lat = dsa_attention(q_lat, c_kv, q_idx, k_idx, w_idx, rel_bias)
    ha = jnp.einsum('bshc,hcd->bshd', o_lat, a_wuv).reshape(b, s, A_WIDTH)

    pos = jnp.arange(s, dtype=jnp.float32)
    rq = rotary(r_q.reshape(b, s, R_HEADS, R_QK), pos)
    rk = rotary(r_k.reshape(b, s, R_HEADS, R_QK), pos)
    hr = retention(rq, rk, r_v.reshape(b, s, R_HEADS, R_V))
    hr = head_layer_norm(hr, r_norm_g).reshape(b, s, R_WIDTH) * jax.nn.silu(r_g)

    y = (jax.nn.sigmoid(g_m) * (hm @ p_m) + jax.nn.sigmoid(g_a) * (ha @ p_a)
         + jax.nn.sigmoid(g_r) * (hr @ p_r))
    x = x + y @ w_out

    h2 = rms_norm(x, norm2_g)
    return x + (jax.nn.silu(h2 @ w_gate) * (h2 @ w_up)) @ w_down

def first_inputs(seed: int = 0) -> dict:
    key = jax.random.key(seed)
    keys = iter(jax.random.split(key, 32))
    f32 = jnp.float32

    def normal(shape, scale):
        return scale * jax.random.normal(next(keys), shape, f32)

    def gain(shape):
        return 1.0 + normal(shape, 0.02)

    L = DEPTH
    return {
        'x': normal((BATCH, SEQ, D_MODEL), 1.0),
        'rel_bias': normal((N_BUCKETS, A_HEADS), 0.2),
        'final_norm_g': gain((D_MODEL,)),
        'norm1_g': gain((L, D_MODEL)),
        'w_in': normal((L, D_MODEL, D_IN), D_MODEL ** -0.5),
        'm_conv': normal((L, CONV_W, 2 * M_HEADS * M_QK), CONV_W ** -0.5),
        'm_ibias': normal((L, M_HEADS), 0.1),
        'm_fbias': jnp.linspace(3.0, 6.0, M_HEADS, dtype=f32)[None, :] + normal((L, M_HEADS), 0.01),
        'm_norm_g': gain((L, M_WIDTH)),
        'a_qnorm_g': gain((L, Q_RANK)),
        'a_wuq': normal((L, Q_RANK, A_WIDTH), Q_RANK ** -0.5),
        'a_wuq_idx': normal((L, Q_RANK, IDX_HEADS * IDX_DIM), Q_RANK ** -0.5),
        'a_kidx_g': gain((L, IDX_DIM)),
        'a_kvnorm_g': gain((L, KV_RANK)),
        'a_wuk': normal((L, A_HEADS, A_HEAD_DIM, KV_RANK), A_HEAD_DIM ** -0.5),
        'a_wuv': normal((L, A_HEADS, KV_RANK, A_HEAD_DIM), KV_RANK ** -0.5),
        'r_norm_g': gain((L, R_WIDTH)),
        'p_m': normal((L, M_WIDTH, D_MODEL), M_WIDTH ** -0.5),
        'p_a': normal((L, A_WIDTH, D_MODEL), A_WIDTH ** -0.5),
        'p_r': normal((L, R_WIDTH, D_MODEL), R_WIDTH ** -0.5),
        'w_out': normal((L, D_MODEL, D_MODEL), D_MODEL ** -0.5),
        'norm2_g': gain((L, D_MODEL)),
        'w_gate': normal((L, D_MODEL, D_FF), D_MODEL ** -0.5),
        'w_up': normal((L, D_MODEL, D_FF), D_MODEL ** -0.5),
        'w_down': normal((L, D_FF, D_MODEL), D_FF ** -0.5),
    }

def first_block(x, rel_bias, final_norm_g, norm1_g, w_in, m_conv, m_ibias, m_fbias, m_norm_g,
              a_qnorm_g, a_wuq, a_wuq_idx, a_kidx_g, a_kvnorm_g, a_wuk, a_wuv, r_norm_g,
              p_m, p_a, p_r, w_out, norm2_g, w_gate, w_up, w_down):
    for l in range(DEPTH):
        x = hybrid_layer(x, rel_bias, norm1_g[l], w_in[l], m_conv[l], m_ibias[l], m_fbias[l],
                         m_norm_g[l], a_qnorm_g[l], a_wuq[l], a_wuq_idx[l], a_kidx_g[l],
                         a_kvnorm_g[l], a_wuk[l], a_wuv[l], r_norm_g[l], p_m[l], p_a[l], p_r[l],
                         w_out[l], norm2_g[l], w_gate[l], w_up[l], w_down[l])
    return rms_norm(x, final_norm_g)


DEPTH_2 = 1

F32 = jnp.float32
PLE_DIM = 256

A_WIDTH_2 = A_HEADS * A_HEAD_DIM
MOBA_BLOCK = 256
MOBA_TOPK = 3
MOBA_QCHUNK = 16

SSD_D_INNER = D_MODEL
SSD_HEAD_DIM = 64
SSD_HEADS = SSD_D_INNER // SSD_HEAD_DIM
SSD_GROUPS = 2
SSD_D_STATE = 128
SSD_CONV = 4
SSD_CHUNK = 256
SSD_CONV_DIM = SSD_D_INNER + 2 * SSD_GROUPS * SSD_D_STATE

MOE_GROUPS = 4
MOE_EXPERTS_PER_GROUP = 4
MOE_EXPERTS = MOE_GROUPS * MOE_EXPERTS_PER_GROUP
MOE_TOPK = 2
MOE_D_FF = 512

OFF_Q = 0
OFF_K = OFF_Q + A_WIDTH_2
OFF_V = OFF_K + A_WIDTH_2
OFF_Z = OFF_V + A_WIDTH_2
OFF_XBC = OFF_Z + SSD_D_INNER
OFF_DT = OFF_XBC + SSD_CONV_DIM
OFF_GA = OFF_DT + SSD_HEADS
OFF_GB = OFF_GA + D_MODEL
IN_DIM = OFF_GB + D_MODEL


def rms_norm_2(x, g):
    xf = x.astype(F32)
    y = xf * lax.rsqrt(jnp.mean(xf * xf, axis=-1, keepdims=True) + EPS)
    return (y * g.astype(F32)).astype(x.dtype)

def alibi_slopes(n):
    return 2.0 ** (-8.0 * jnp.arange(1, n + 1, dtype=F32) / n)

def moba_attention(q, k, v):
    bsz, s, nh, hd = q.shape
    nb = -(-s // MOBA_BLOCK)
    s_pad = nb * MOBA_BLOCK
    pad = ((0, 0), (0, s_pad - s), (0, 0), (0, 0))
    q, k, v = [jnp.pad(t, pad).transpose(0, 2, 1, 3) for t in (q, k, v)]
    scale = hd ** -0.5
    kb = k.reshape(bsz, nh, nb, MOBA_BLOCK, hd)
    vb = v.reshape(bsz, nh, nb, MOBA_BLOCK, hd)
    k_mean = jnp.mean(kb.astype(F32), axis=3)
    gate = jnp.einsum('bhtd,bhnd->bhtn', q.astype(F32), k_mean)
    q_blk = jnp.arange(s_pad) // MOBA_BLOCK
    past = jnp.arange(nb)[None, :] < q_blk[:, None]
    gate = jnp.where(past[None, None], gate, -jnp.inf)
    topk = min(MOBA_TOPK, nb)
    _, top_idx = lax.top_k(gate, topk)
    sel_valid = jnp.arange(topk)[None, :] < q_blk[:, None]
    slopes = alibi_slopes(nh)[None, :, None, None]
    bi = jnp.arange(bsz)[:, None, None, None]
    hi = jnp.arange(nh)[None, :, None, None]
    offs = jnp.arange(MOBA_BLOCK)
    n_chunks = s_pad // MOBA_QCHUNK

    def chunk(c):
        t0 = c * MOBA_QCHUNK
        qc = lax.dynamic_slice_in_dim(q, t0, MOBA_QCHUNK, axis=2)
        idx = lax.dynamic_slice_in_dim(top_idx, t0, MOBA_QCHUNK, axis=2)
        valid = lax.dynamic_slice_in_dim(sel_valid, t0, MOBA_QCHUNK, axis=0)
        t = t0 + jnp.arange(MOBA_QCHUNK)
        kg = kb[bi, hi, idx]
        vg = vb[bi, hi, idx]
        s_sel = jnp.einsum('bhqd,bhqkld->bhqkl', qc, kg, preferred_element_type=F32) * scale
        kpos = idx[..., None] * MOBA_BLOCK + offs
        s_sel = s_sel - slopes[..., None] * (t[:, None, None] - kpos).astype(F32)
        s_sel = jnp.where(valid[:, :, None], s_sel, -jnp.inf)
        blk0 = (t0 // MOBA_BLOCK) * MOBA_BLOCK
        ko = lax.dynamic_slice_in_dim(k, blk0, MOBA_BLOCK, axis=2)
        vo = lax.dynamic_slice_in_dim(v, blk0, MOBA_BLOCK, axis=2)
        s_own = jnp.einsum('bhqd,bhld->bhql', qc, ko, preferred_element_type=F32) * scale
        dist = t[:, None] - (blk0 + offs)[None, :]
        s_own = jnp.where(dist >= 0, s_own - slopes * dist.astype(F32), -jnp.inf)
        sc = jnp.concatenate([s_sel.reshape(bsz, nh, MOBA_QCHUNK, topk * MOBA_BLOCK), s_own], axis=-1)
        pr = jax.nn.softmax(sc, axis=-1).astype(v.dtype)
        p_sel = pr[..., :topk * MOBA_BLOCK].reshape(bsz, nh, MOBA_QCHUNK, topk, MOBA_BLOCK)
        p_own = pr[..., topk * MOBA_BLOCK:]
        return (jnp.einsum('bhqkl,bhqkld->bhqd', p_sel, vg)
                + jnp.einsum('bhql,bhld->bhqd', p_own, vo))

    out = lax.map(chunk, jnp.arange(n_chunks))
    out = out.transpose(1, 2, 0, 3, 4).reshape(bsz, nh, s_pad, hd)[:, :, :s]
    return out.transpose(0, 2, 1, 3)

def causal_depthwise_conv(u, w, b):
    c = u.shape[-1]
    out = lax.conv_general_dilated(u, w[:, None, :].astype(u.dtype), window_strides=(1,),
                                   padding=[(SSD_CONV - 1, 0)],
                                   dimension_numbers=('NWC', 'WIO', 'NWC'),
                                   feature_group_count=c)
    return out + b

def segsum(a):
    tlen = a.shape[-1]
    cs = jnp.cumsum(a, axis=-1)
    diff = cs[..., :, None] - cs[..., None, :]
    mask = jnp.tril(jnp.ones((tlen, tlen), dtype=bool))
    return jnp.where(mask, diff, -jnp.inf)

def ssd_chunked_scan(x, dt, a, b_in, c_in):
    bsz, s, nh, hp = x.shape
    ng, ns = b_in.shape[2], b_in.shape[3]
    hpg = nh // ng
    nc = -(-s // SSD_CHUNK)
    sp = nc * SSD_CHUNK

    def padt(t):
        return jnp.pad(t.astype(F32), [(0, 0), (0, sp - s)] + [(0, 0)] * (t.ndim - 2))

    x, dt, b_in, c_in = padt(x), padt(dt), padt(b_in), padt(c_in)
    xdt = (x * dt[..., None]).reshape(bsz, nc, SSD_CHUNK, ng, hpg, hp)
    da = (dt * a.astype(F32)).reshape(bsz, nc, SSD_CHUNK, ng, hpg).transpose(0, 3, 4, 1, 2)
    bc = b_in.reshape(bsz, nc, SSD_CHUNK, ng, ns)
    cc = c_in.reshape(bsz, nc, SSD_CHUNK, ng, ns)
    da_cs = jnp.cumsum(da, axis=-1)
    decay_in = jnp.exp(segsum(da))
    cb = jnp.einsum('bclgn,bcsgn->bgcls', cc, bc)
    y_diag = jnp.einsum('bgcls,bgjcls,bcsgjp->bclgjp', cb, decay_in, xdt)
    decay_to_end = jnp.exp(da_cs[..., -1:] - da_cs)
    chunk_states = jnp.einsum('bclgn,bgjcl,bclgjp->cbgjpn', bc, decay_to_end, xdt)
    chunk_decay = jnp.exp(da_cs[..., -1]).transpose(3, 0, 1, 2)

    def carry_state(h, inp):
        st, dec = inp
        return h * dec[..., None, None] + st, h

    h0 = jnp.zeros(chunk_states.shape[1:], F32)
    _, h_in = lax.scan(carry_state, h0, (chunk_states, chunk_decay))
    y_off = jnp.einsum('bclgn,cbgjpn,bgjcl->bclgjp', cc, h_in, jnp.exp(da_cs))
    return (y_diag + y_off).reshape(bsz, sp, nh, hp)[:, :s]

def ssd_mixer(z, xbc, dt_raw, conv_w, conv_b, dt_bias, a_log, d_skip, norm_g):
    bsz, s, _ = z.shape
    xbc = jax.nn.silu(causal_depthwise_conv(xbc, conv_w, conv_b))
    xs = xbc[..., :SSD_D_INNER].reshape(bsz, s, SSD_HEADS, SSD_HEAD_DIM)
    gs = SSD_GROUPS * SSD_D_STATE
    b_in = xbc[..., SSD_D_INNER:SSD_D_INNER + gs].reshape(bsz, s, SSD_GROUPS, SSD_D_STATE)
    c_in = xbc[..., SSD_D_INNER + gs:].reshape(bsz, s, SSD_GROUPS, SSD_D_STATE)
    dt = jax.nn.softplus(dt_raw.astype(F32) + dt_bias.astype(F32))
    a = -jnp.exp(a_log.astype(F32))
    y = ssd_chunked_scan(xs, dt, a, b_in, c_in)
    y = y + d_skip.astype(F32)[:, None] * xs.astype(F32)
    u = (y.reshape(bsz, s, SSD_D_INNER) * jax.nn.silu(z.astype(F32)))
    u = u.reshape(bsz, s, SSD_GROUPS, SSD_D_INNER // SSD_GROUPS)
    u = u * lax.rsqrt(jnp.mean(u * u, axis=-1, keepdims=True) + EPS)
    return (u.reshape(bsz, s, SSD_D_INNER) * norm_g.astype(F32)).astype(z.dtype)

def hier_moe(h, w_rg, b_rg, w_re, b_re, w_gate, w_up, w_down):
    bsz, s, _ = h.shape
    hf = h.astype(F32)
    g_logits = hf @ w_rg.astype(F32) + b_rg.astype(F32)
    g_prob = jax.nn.softmax(g_logits, axis=-1)
    g_pw, g_sel = lax.top_k(g_prob, 1)
    e_logits = (hf @ w_re.astype(F32) + b_re.astype(F32)).reshape(bsz, s, MOE_GROUPS, MOE_EXPERTS_PER_GROUP)
    e_in_group = jnp.take_along_axis(e_logits, g_sel[..., None], axis=2)[:, :, 0]
    e_val, e_idx = lax.top_k(e_in_group, MOE_TOPK)
    e_w = jax.nn.softmax(e_val, axis=-1) * g_pw
    expert_id = g_sel * MOE_EXPERTS_PER_GROUP + e_idx
    combine = jnp.sum(jax.nn.one_hot(expert_id, MOE_EXPERTS, dtype=F32) * e_w[..., None], axis=-2)
    out = jnp.zeros_like(h)
    for e in range(MOE_EXPERTS):
        he = jax.nn.silu(h @ w_gate[e]) * (h @ w_up[e])
        out = out + combine[..., e:e + 1].astype(h.dtype) * (he @ w_down[e])
    return out

def second_inputs(seed: int = 0) -> dict:
    key = jax.random.key(seed)
    ks = jax.random.split(key, 24)
    nrm = jax.random.normal

    def gain(k, n):
        return 1.0 + 0.02 * nrm(k, (DEPTH_2, n), F32)

    dt0 = jnp.exp(jax.random.uniform(ks[6], (DEPTH_2, SSD_HEADS), F32)
                  * (math.log(0.1) - math.log(1e-3)) + math.log(1e-3))
    return {
        'x': nrm(ks[0], (BATCH, SEQ, D_MODEL), F32),
        'p': nrm(ks[1], (DEPTH_2, BATCH, SEQ, PLE_DIM), F32),
        'mix_norm_g': gain(ks[2], D_MODEL),
        'w_in': nrm(ks[3], (DEPTH_2, D_MODEL, IN_DIM), F32) * D_MODEL ** -0.5,
        'conv_w': nrm(ks[4], (DEPTH_2, SSD_CONV, SSD_CONV_DIM), F32) * SSD_CONV ** -0.5,
        'conv_b': 0.02 * nrm(ks[5], (DEPTH_2, SSD_CONV_DIM), F32),
        'dt_bias': dt0 + jnp.log(-jnp.expm1(-dt0)),
        'a_log': jnp.log(jax.random.uniform(ks[7], (DEPTH_2, SSD_HEADS), F32, minval=1.0, maxval=16.0)),
        'd_skip': gain(ks[8], SSD_HEADS),
        'ssd_norm_g': gain(ks[9], SSD_D_INNER),
        'w_out_a': nrm(ks[10], (DEPTH_2, A_WIDTH_2, D_MODEL), F32) * A_WIDTH_2 ** -0.5,
        'w_out_b': nrm(ks[11], (DEPTH_2, SSD_D_INNER, D_MODEL), F32) * SSD_D_INNER ** -0.5,
        'w_out': nrm(ks[12], (DEPTH_2, D_MODEL, D_MODEL), F32) * D_MODEL ** -0.5,
        'ffn_norm_g': gain(ks[13], D_MODEL),
        'w_rg': nrm(ks[14], (DEPTH_2, D_MODEL, MOE_GROUPS), F32) * D_MODEL ** -0.5,
        'b_rg': 0.01 * nrm(ks[15], (DEPTH_2, MOE_GROUPS), F32),
        'w_re': nrm(ks[16], (DEPTH_2, D_MODEL, MOE_EXPERTS), F32) * D_MODEL ** -0.5,
        'b_re': 0.01 * nrm(ks[17], (DEPTH_2, MOE_EXPERTS), F32),
        'w_gate': nrm(ks[18], (DEPTH_2, MOE_EXPERTS, D_MODEL, MOE_D_FF), F32) * D_MODEL ** -0.5,
        'w_up': nrm(ks[19], (DEPTH_2, MOE_EXPERTS, D_MODEL, MOE_D_FF), F32) * D_MODEL ** -0.5,
        'w_down': nrm(ks[20], (DEPTH_2, MOE_EXPERTS, MOE_D_FF, D_MODEL), F32) * MOE_D_FF ** -0.5,
        'w_ple_proj': nrm(ks[21], (DEPTH_2, PLE_DIM, D_MODEL), F32) * PLE_DIM ** -0.5,
        'w_ple_gate': nrm(ks[22], (DEPTH_2, D_MODEL, D_MODEL), F32) * D_MODEL ** -0.5,
        'final_norm_g': 1.0 + 0.02 * nrm(ks[23], (D_MODEL,), F32),
    }

def second_block(x, p, mix_norm_g, w_in, conv_w, conv_b, dt_bias, a_log, d_skip, ssd_norm_g,
              w_out_a, w_out_b, w_out, ffn_norm_g, w_rg, b_rg, w_re, b_re, w_gate, w_up,
              w_down, w_ple_proj, w_ple_gate, final_norm_g):
    bsz, s, _ = x.shape
    for i in range(DEPTH_2):
        h = rms_norm_2(x, mix_norm_g[i])
        proj = h @ w_in[i]
        q = proj[..., OFF_Q:OFF_K].reshape(bsz, s, A_HEADS, A_HEAD_DIM)
        k = proj[..., OFF_K:OFF_V].reshape(bsz, s, A_HEADS, A_HEAD_DIM)
        v = proj[..., OFF_V:OFF_Z].reshape(bsz, s, A_HEADS, A_HEAD_DIM)
        z = proj[..., OFF_Z:OFF_XBC]
        xbc = proj[..., OFF_XBC:OFF_DT]
        dt_raw = proj[..., OFF_DT:OFF_GA]
        gate_a = jax.nn.sigmoid(proj[..., OFF_GA:OFF_GB])
        gate_b = jax.nn.sigmoid(proj[..., OFF_GB:IN_DIM])
        y_a = moba_attention(q, k, v).reshape(bsz, s, A_WIDTH_2) @ w_out_a[i]
        y_b = ssd_mixer(z, xbc, dt_raw, conv_w[i], conv_b[i], dt_bias[i], a_log[i],
                        d_skip[i], ssd_norm_g[i]) @ w_out_b[i]
        x = x + (gate_a * y_a + gate_b * y_b) @ w_out[i]
        h2 = rms_norm_2(x, ffn_norm_g[i])
        x = x + hier_moe(h2, w_rg[i], b_rg[i], w_re[i], b_re[i], w_gate[i], w_up[i], w_down[i])
        x = x + jax.nn.sigmoid(x @ w_ple_gate[i]) * (p[i] @ w_ple_proj[i])
    return rms_norm_2(x, final_norm_g)


def setup_inputs(seed=0):
    out = dict(first_inputs(seed))
    for name, value in second_inputs(seed + 1).items():
        if name != "x":
            out[name + "_2"] = value
    return out


def reference(
    x, rel_bias, final_norm_g, norm1_g, w_in, m_conv, m_ibias, m_fbias, m_norm_g, a_qnorm_g,
    a_wuq, a_wuq_idx, a_kidx_g, a_kvnorm_g, a_wuk, a_wuv, r_norm_g, p_m, p_a, p_r, w_out,
    norm2_g, w_gate, w_up, w_down, p_2, mix_norm_g_2, w_in_2, conv_w_2, conv_b_2, dt_bias_2,
    a_log_2, d_skip_2, ssd_norm_g_2, w_out_a_2, w_out_b_2, w_out_2, ffn_norm_g_2, w_rg_2,
    b_rg_2, w_re_2, b_re_2, w_gate_2, w_up_2, w_down_2, w_ple_proj_2, w_ple_gate_2,
    final_norm_g_2,
):
    x = first_block(
        x, rel_bias, final_norm_g, norm1_g, w_in, m_conv, m_ibias, m_fbias, m_norm_g, a_qnorm_g,
        a_wuq, a_wuq_idx, a_kidx_g, a_kvnorm_g, a_wuk, a_wuv, r_norm_g, p_m, p_a, p_r, w_out,
        norm2_g, w_gate, w_up, w_down,
    )
    return second_block(
        x, p_2, mix_norm_g_2, w_in_2, conv_w_2, conv_b_2, dt_bias_2, a_log_2, d_skip_2,
        ssd_norm_g_2, w_out_a_2, w_out_b_2, w_out_2, ffn_norm_g_2, w_rg_2, b_rg_2, w_re_2,
        b_re_2, w_gate_2, w_up_2, w_down_2, w_ple_proj_2, w_ple_gate_2, final_norm_g_2,
    )


_drawn_inputs = setup_inputs


def setup_inputs(seed=0):
    import zlib

    import numpy as np

    out = dict(_drawn_inputs(seed))
    spreads = {}
    factors = {'m_ibias': 64.0,
     'm_norm_g': 2.814,
     'a_kvnorm_g': 2.682,
     'd_skip_2': 9.285,
     'ssd_norm_g_2': 3.303,
     'b_rg_2': 14.205,
     'b_re_2': 19.499,
     'final_norm_g_2': 8.099,
     'conv_b_2': 2.892,
     'ffn_norm_g_2': 3.348}
    for name, (base, spread) in spreads.items():
        noise = np.random.default_rng([zlib.crc32(name.encode()), seed]).standard_normal(out[name].shape)
        drawn = base * np.exp(spread * noise) if base else spread * noise
        out[name] = jnp.asarray(drawn.astype(out[name].dtype))
    for name, factor in factors.items():
        out[name] = (out[name] * factor).astype(out[name].dtype)
    return out
```

```python
import math
from contextlib import ExitStack, contextmanager

import numpy as np

import concourse.bass as bass
from concourse import mybir

F32 = mybir.dt.float32
F32R = mybir.dt.float32r
ALU = mybir.AluOpType
ACT = mybir.ActivationFunctionType
AX = mybir.AxisListType

P = 128
SEQ = 256
TT = SEQ // P
D = 1024
KT = D // P
LAYERS = 2
EPS = 1e-6
QK = 2
QC = 512
RING = 3
BIG = 1e30
TAKEN = -3e38
HEADS_A = 8
WIN = SEQ + P
TOPK = 64
SLOTS = 4
SSD_HEADS = 16
BUCKETS = 32
GLU = 256
D_FF = 2816
FF_GROUPS = D_FF // GLU
EXPERTS = 16
MOE_FF = 512
MOE_GROUPS_PER_EXPERT = MOE_FF // GLU
LAYER_Q = 4 * 14 + 2 + 2 * 6 + 4 * 2 + 6 * FF_GROUPS
SECOND_Q = 4 * 12 + 2 * 2 + 4 * 2 + 4 * 2 + 6 * EXPERTS * MOE_GROUPS_PER_EXPERT + 2 + 4 * 2
TOTAL_Q = LAYERS * LAYER_Q + SECOND_Q

C_ID, C_MASK, C_QMASK, C_RET = 0, 128, 384, 512
C_COS, C_SIN, C_END = C_RET + 4 * SEQ, C_RET + 4 * SEQ + 128, C_RET + 4 * SEQ + 256
L_N1, L_N2, L_QN, L_KI, L_MN, L_RN, L_CW, L_KV, L_IB, L_UK, L_UV, L_END = (
    0, 8, 16, 18, 19, 23, 27, 43, 171, 179, 179 + 512, 179 + 1024)
(S_N1, S_N2, S_NS, S_CW, S_CB, S_DTB, S_AL, S_DS, S_BR, S_SW, S_END) = (
    0, 8, 16, 24, 72, 84, 100, 116, 132, 152, 152 + 8 * 36)


class Count:

    def __init__(self, sem):
        self.sem, self.reg, self.n = sem, 0, 0

    def up(self, k=1):
        self.n += k
        return self.reg + self.n

    def back(self, k):
        return self.reg + self.n - k


class Chain(Count):

    def __init__(self, sem, eng):
        super().__init__(sem)
        self.eng = eng

    def __call__(self, ins):
        ins.then_inc(self.sem, 1)
        self.eng.wait_ge(self.sem, self.up())


@contextmanager
def repeat(eng, name, trips, counts, per):
    with eng.Fori(0, trips) as i:
        saved = [(c, c.reg, c.n) for c in counts]
        for k, c in enumerate(counts):
            c.reg = c.reg + i * per.get((name, k), 6)
        yield i
    for k, (c, reg, n) in enumerate(saved):
        per[(name, k)] = c.n - n
        c.reg = reg
        c.n += (c.n - n) * (trips - 1)


def program(nc, stream, const, layer_small, x_in, onehot, relb, scratch, second_small, alibi, gains, p_in, out, per):
    ctx = ExitStack()
    with ctx:
        def sb(name, shape, dt=F32):
            return ctx.enter_context(nc.sbuf_tensor(name, shape, dt))

        def sem(name):
            return ctx.enter_context(nc.semaphore(name))

        raw = sb("raw", [P, RING, QK * QC])
        w_hi = sb("w_hi", [P, RING, QK * QC], F32R)
        w_lo = sb("w_lo", [P, RING, QK * QC], F32R)
        cst = sb("cst", [P, C_END])
        ident = cst[:, C_ID:C_ID + P]
        mask = cst[:, C_MASK:C_MASK + SEQ]
        qmask = cst[:, C_QMASK:C_QMASK + P]
        ret_decay = cst[:, C_RET:C_RET + 4 * SEQ].rearrange("p (h t) -> p h t", h=4)
        cosv = cst[:, C_COS:C_COS + 128].rearrange("p (t d) -> p t d", t=TT)
        sinv = cst[:, C_SIN:C_SIN + 128].rearrange("p (t d) -> p t d", t=TT)
        small = sb("small", [P, L_END])
        x = sb("x", [P, TT, D])
        hT = sb("hT", [P, 2, KT, SEQ], F32R)
        xn = sb("xn", [P, TT, D])
        bias = sb("bias", [P, HEADS_A, WIN])
        mixT = sb("mixT", [P, 3, 2, 4, SEQ], F32R)
        heT = mixT[:, 0].rearrange("p a k t -> p (a k t)")[:, 0:2 * QK * SEQ].rearrange("p (a k t) -> p a k t", a=2, k=QK)
        logits = sb("logits", [P, HEADS_A, WIN])
        gates = sb("gates", [P, 2, TT, D])
        arena = sb("arena", [P, 14 * 1024 + 64])
        tiny = sb("tiny", [P, 1024])
        ones = sb("ones", [16, SEQ])
        wexp = sb("wexp", [P, SLOTS, WIN])
        prob = sb("prob", [P, SLOTS, WIN])
        sw = sb("sw", [P, 2, 8 * 36], F32R)
        rows2 = sb("rows2", [16, 2, SEQ])

        def ar(at, *shape):
            n = int(np.prod(shape))
            v = arena[:, at:at + n]
            if len(shape) == 2:
                return v.rearrange("p (a b) -> p a b", b=shape[1])
            if len(shape) == 3:
                return v.rearrange("p (a b c) -> p a b c", b=shape[1], c=shape[2])
            if len(shape) == 4:
                return v.rearrange("p (a b c d) -> p a b c d", b=shape[1], c=shape[2], d=shape[3])
            return v

        gates_flat = gates[:].rearrange("p g t d -> p (g t d)")
        windows = logits[:].rearrange("p h w -> p (h w)"), gates_flat[:, 0:HEADS_A * WIN]
        relb_sb = arena[0:BUCKETS, 0:HEADS_A * P].rearrange("p (h t) -> p h t", h=HEADS_A)
        onehot_sb = arena[0:BUCKETS, 1024:1024 + 2 * WIN].rearrange("p (t w) -> p t w", t=2)
        cqT = mixT[:, 2].rearrange("p a k t -> p (a k t)")[:, 0:2 * QK * SEQ].rearrange("p (a k t) -> p a k t", a=2, k=QK)
        gbuf, he = ar(0, TT, GLU), ar(TT * GLU, TT, GLU)
        K1 = 1024
        mqk_tok = ar(0, TT, 512)
        qkT = ar(0, 4, SEQ)
        conv_in = ar(K1, 4, SEQ + 3)
        m_out = ar(K1, TT, 4, 129)
        mv = ar(2 * K1 + 16, TT, 4, 129)
        sm = ar(3 * K1 + 64, TT, 512)
        A0 = 4 * K1 + 64
        rq = ar(A0, TT, 512)
        r_out = ar(A0, TT, 512)
        rk = ar(A0 + K1, TT, 512)
        rv = ar(A0 + 2 * K1, TT, 512)
        rg = ar(A0 + 3 * K1, TT, 512)
        mo = ar(A0 + 4 * K1, TT, 512)
        qT = ar(A0 + 5 * K1, 2, 4, SEQ)
        rqT = ar(A0 + 7 * K1, 2, 4, SEQ)
        rot = ar(A0 + 9 * K1, TT, 4, 64)
        kidxT = ar(A0 + 9 * K1 + 512, SEQ)
        ckvT = ar(A0 + 9 * K1 + 768, SEQ)
        conv_out = qkT
        tmpy = mo
        qlatA = ar(0, 4, SEQ)
        qlatB = ar(A0 + K1, 4, SEQ)

        def qlat(h):
            return (qlatA if h < 4 else qlatB)[:, h % 4, :]

        bank = [ctx.enter_context(nc.psum_tensor(f"bank{i}", [P, 512], F32)) for i in range(8)]
        LIN, TR, AB = bank[0:2], bank[2:4], bank[4:8]

        s_raw = [sem(f"raw_in{i}") for i in range(RING)]
        s_hi = sem("hi_done")
        s_lo = sem("lo_done")
        s_used = sem("quarter_used")
        s_lin = sem("lin_full")
        s_la = sem("lin_read_act")
        s_ld = sem("lin_read_dve")
        s_tr = sem("tr_full")
        s_th = sem("tr_hi")
        s_td = sem("tr_read")
        s_ab = sem("mix_full")
        s_ad = sem("mix_read")
        s_var = sem("var_ready")
        s_std = sem("std_ready")
        s_nx = sem("normed")
        s_arg = sem("exp_arg")
        s_ex2 = sem("decay_exp")
        s_pp = sem("pool_probs")
        s_sw = sem("small_weights_hi")
        s_rot = sem("rotated")
        s_pv = sem("values_summed")
        s_bf, s_bd = sem("bias_full"), sem("bias_read")
        s_exp = sem("exp_done")
        s_act = sem("act_out")
        s_x = sem("x_ready")
        s_g = sem("glu_gate")
        s_sm = sem("small_in")
        s_cst = sem("const_in")
        s_b = sem("bias_moved")
        s_ch_d = sem("dve_chain")
        s_ch_a = sem("act_chain")
        s_ch_p = sem("pool_chain")
        s_out = sem("out_written")
        s_z = sem("cleared")

        block = ctx.enter_context(nc.Block())

        @block.sync
        def _(sp):
            sp.dma_start(x[:], x_in.rearrange("(t p) d -> p t d", p=P)).then_inc(s_cst, 16)
            sp.dma_start(cst[:], const).then_inc(s_cst, 16)
            sp.dma_start(relb_sb, relb).then_inc(s_cst, 16)
            sp.dma_start(onehot_sb, onehot).then_inc(s_cst, 16)
            for i in range(RING):
                sp.dma_start(raw[:, i], stream[i]).then_inc(s_raw[i], 16)
            with sp.Fori(1, TOTAL_Q // RING) as r:
                for i in range(RING):
                    src = stream[r * RING + i]
                    sp.wait_ge(s_hi, r * RING + (i + 1 - RING))
                    sp.wait_ge(s_lo, r * RING + (i + 1 - RING))
                    sp.dma_start(raw[:, i], src).then_inc(s_raw[i], 16)
            sp.wait_ge(s_x, LAYERS + 3)
            sp.dma_start(out.rearrange("(t p) d -> p t d", p=P), xn[:]).then_inc(s_out, 16)
            sp.wait_ge(s_out, 16)

        tok = [ar(0, TT, 512), ar(K1, TT, 512)]
        yb = ar(0, TT, D)
        conv2 = ar(2 * K1, 4, SEQ + 3)
        xbcT = [ar(3 * K1 + 16 + i * K1, 4, SEQ) for i in range(3)]
        xs = ar(6 * K1 + 16, TT, D)
        xdt = ar(8 * K1 + 16, TT, D)
        qkT2 = ar(10 * K1 + 16, 2, 4, SEQ)
        v2 = ar(12 * K1 + 16, TT, 512)
        cb = ar(13 * K1 + 16, 2, WIN)
        mixT8 = mixT[:, 0:2].rearrange("p m a k t -> p (m a k t)").rearrange("p (a k t) -> p a k t", a=2, k=KT)
        bflat = bias[:].rearrange("p h w -> p (h w)")
        gain1 = gates_flat[:, 0:D]
        gain2 = bflat[:, 0:D]
        p_tok = bflat[:, D:D + 512].rearrange("p (t d) -> p t d", t=TT)
        ple = gates[:, 0]
        tmpg2 = [ar(0, TT, 512), ar(K1, TT, 512)]

        def tn(at, *shape):
            n = int(np.prod(shape))
            v = tiny[:, at:at + n]
            if len(shape) == 2:
                return v.rearrange("p (a b) -> p a b", b=shape[1])
            return v

        g16 = tn(64, TT, 16)
        gif = tn(96, TT, 8)
        acol, mcol = tn(176, TT, 4), tn(184, TT, 4)
        em = tn(192, TT, 4)
        den = tn(200, TT, 4)
        keep = tn(256, WIN)
        dt, da, cs = tn(624, TT, 16), tn(656, TT, 16), tn(688, TT, 16)
        comb = tn(740, TT, 16)
        lflat = logits[:].rearrange("p h w -> p (h w)")
        work = lflat[:, 0:WIN]
        relu_w = lflat[:, WIN:2 * WIN]
        best = lflat[:, 2 * WIN:2 * WIN + 8]
        rows = lflat[0:4, 1152:1152 + 5 * SEQ].rearrange("p (a b) -> p a b", b=SEQ)
        xflat = xn[:].rearrange("p t d -> p (t d)")

        def heads(v):
            return v.rearrange("p t (h d) -> p t h d", h=4)

        @block.tensor
        def _(pe):
            lo, tr, ab = Count(s_lo), Count(s_td), Count(s_ad)
            la, ld, nx, rot = Count(s_la), Count(s_ld), Count(s_nx), Count(s_rot)
            counts = [lo, tr, ab, la, ld, nx, rot]
            free = {}

            def quarter():
                pe.wait_ge(s_lo, lo.up())
                s = (lo.n - 1) % RING
                return (w_hi[:, s, :].rearrange("p (k n) -> p k n", k=QK),
                        w_lo[:, s, :].rearrange("p (k n) -> p k n", k=QK))

            def claim(b, reader):
                if b in free:
                    c, n = free[b]
                    pe.wait_ge(c.sem, c.reg + n)
                c = la if reader == "act" else ld
                c.up()
                free[b] = (c, c.n)

            def product(lhs, nk, reader, between=None):
                for k0 in range(0, nk, QK):
                    hi, lw = quarter()
                    for t in range(TT):
                        if k0 == 0:
                            claim(t, reader)
                        for k in range(QK):
                            for n, (a, w) in enumerate(((0, hi), (1, hi), (0, lw))):
                                mm = pe.matmul(LIN[t][:, :], lhs[:, a, k0 + k, t * P:(t + 1) * P], w[:, k, :],
                                               start=(k0 + k == 0 and n == 0), stop=(k0 + k == nk - 1 and n == 2))
                        if t == 0 and k0 + QK == nk:
                            mm.then_inc(s_lin, 1)
                    mm.then_inc(s_used, 1)
                    if between and k0 + QK == nk // 2:
                        between()

            def tr_bank():
                f = tr.up()
                if tr.n > 2:
                    pe.wait_ge(s_td, f - 2)
                return TR[(tr.n - 1) % 2]

            def ab_bank():
                f = ab.up()
                if ab.n > 4:
                    pe.wait_ge(s_ad, f - 4)
                return AB[(ab.n - 1) % 4]

            def transposed(src, nk):
                for k0 in range(0, nk, 2):
                    b = tr_bank()
                    for k in range(2):
                        for t in range(TT):
                            mm = pe.transpose(b[:, k * SEQ + t * P:k * SEQ + (t + 1) * P], src(t, k0 + k), ident)
                    mm.then_inc(s_tr, 1)

            def scores(b, at, k, q):
                pe.matmul(b[:, at:at + SEQ], k[:, 0:P], q, start=True, stop=True, skip_group_check=True)
                return pe.matmul(b[:, at + SEQ:at + WIN], k[:, P:SEQ], q[:, P:SEQ], start=True, stop=True,
                                 skip_group_check=True)

            def weighted(b, at, n, w, v):
                pe.matmul(b[:, at:at + n], w[:, 0:P], v(0), start=True, stop=True, skip_group_check=True)
                pe.matmul(b[:, at + n:at + 2 * n], w[:, P:SEQ], v(0), start=True, stop=False, skip_group_check=True)
                return pe.matmul(b[:, at + n:at + 2 * n], w[:, SEQ:WIN], v(1), start=False, stop=True,
                                 skip_group_check=True)

            def layer(l):
                pe.wait_ge(s_nx, nx.up())
                transposed(lambda t, k: xn[:, t, k * P:(k + 1) * P], KT)
                pe.wait_ge(s_td, tr.back(0))
                product(hT, KT, "act")
                product(hT, KT, "act")
                pe.wait_ge(s_nx, nx.up())
                transposed(lambda t, k: sm[:, t, k * P:(k + 1) * P], 4)
                cq_ready = tr.back(1)
                product(hT, KT, "act")
                transposed(lambda t, k: mqk_tok[:, t, k * P:(k + 1) * P], 4)
                pe.wait_ge(s_td, cq_ready)
                for i in range(2):
                    hi, lw = quarter()
                    for f in range(4):
                        if f % 2 == 0:
                            claim(f // 2, "act")
                        for k in range(QK):
                            for n, (w, a) in enumerate(((hi, 0), (lw, 0), (hi, 1))):
                                mm = pe.matmul(LIN[f // 2][:, (f % 2) * SEQ:(f % 2 + 1) * SEQ], w[:, k, f * P:(f + 1) * P],
                                               cqT[:, a, k, :], start=(k == 0 and n == 0), stop=(k == QK - 1 and n == 2),
                                               skip_group_check=True)
                        if f == 1:
                            mm.then_inc(s_lin, 1)
                    mm.then_inc(s_used, 1)
                product(hT, KT, "act")
                pe.wait_ge(s_nx, nx.up())
                b = tr_bank()
                for g in range(2):
                    for t in range(TT):
                        mm = pe.transpose(b[0:4, g * SEQ + t * P:g * SEQ + (t + 1) * P], gif[:, t, 4 * g:4 * g + 4], ident)
                mm.then_inc(s_tr, 1)
                pe.wait_ge(s_la, la.back(2))
                for g in range(8):
                    b = ab_bank()
                    r = slice(64 * (g % 2), 64 * (g % 2) + 64)
                    pe.matmul(b[:, 0:P], qT[r, 1, g // 2, 0:P], kidxT[r, 0:P], start=True, stop=True, skip_group_check=True)
                    pe.matmul(b[:, P:WIN], qT[r, 1, g // 2, P:SEQ], kidxT[r, :], start=True, stop=True,
                              skip_group_check=True).then_inc(s_ab, 1)
                product(hT, KT, "act")
                pe.wait_ge(s_nx, nx.up())
                b = tr_bank()
                for g, row in enumerate((0, 3)):
                    for t in range(TT):
                        mm = pe.matmul(b[:, 8 * g + 4 * t:8 * g + 4 * t + 4], rows[:, row, t * P:(t + 1) * P], ident[0:4, 0:4],
                                       start=True, stop=True, skip_group_check=True)
                mm.then_inc(s_tr, 1)
                product(hT, KT, "act")
                product(hT, KT, "act")
                product(hT, KT, "act")
                pe.wait_ge(s_rot, rot.up(2))
                transposed(lambda t, k: rq[:, t, k * P:(k + 1) * P], 4)
                transposed(lambda t, k: rk[:, t, k * P:(k + 1) * P], 4)
                product(hT, KT, "act")
                pe.wait_ge(s_act, acts.up())

                def m_scores(h):
                    b = ab_bank()
                    pe.matmul(b[:, 0:SEQ], ident[0:4, h:h + 1].to_broadcast([4, P]), rows[:, 2, :], start=True,
                              stop=True).then_inc(s_ab, 1)
                    b = ab_bank()
                    r = slice(64 * (h % 2), 64 * (h % 2) + 64)
                    scores(b, 0, qkT[r, 2 + h // 2, :], qkT[r, h // 2, :]).then_inc(s_ab, 1)
                    return ab.back(0)

                weights = [m_scores(0)]
                for h in range(4):
                    if h < 3:
                        weights.append(m_scores(h + 1))
                    pe.wait_ge(s_ad, weights[h])
                    b = ab_bank()
                    weighted(b, 0, 129, prob[:, h % SLOTS], lambda s: mv[:, s, h, :]).then_inc(s_ab, 1)
                product(hT, KT, "act")

                def r_scores(h):
                    scores(ab_bank(), 0, rqT[:, 1, h, :], rqT[:, 0, h, :]).then_inc(s_ab, 1)
                    return ab.back(0)

                pe.wait_ge(s_td, tr.back(0))
                weights = [r_scores(0)]
                for h in range(4):
                    if h < 3:
                        weights.append(r_scores(h + 1))
                    pe.wait_ge(s_ad, weights[h])
                    b = ab_bank()
                    weighted(b, 0, P, prob[:, h % SLOTS], lambda s: rv[:, s, h * P:(h + 1) * P]).then_inc(s_ab, 1)
                product(hT, KT, "act")
                pe.wait_ge(s_ad, ab.back(0))
                uk = small[:, L_UK:L_UK + 512].rearrange("p (a c) -> p a c", a=4)
                for j in range(4):
                    b = ab_bank()
                    r = slice(64 * (j % 2), 64 * (j % 2) + 64)
                    for i in range(2):
                        pair = 2 * (j // 2) + i
                        mm = pe.matmul(b[:, i * SEQ:(i + 1) * SEQ], uk[r, pair, :], qT[r, 0, pair, :], start=True, stop=True,
                                       skip_group_check=True)
                    mm.then_inc(s_ab, 1)
                product(hT, KT, "act")
                pe.wait_ge(s_ad, ab.back(0))
                for h in range(HEADS_A):
                    b = ab_bank()
                    pe.matmul(b[:, 0:P], qlat(h)[:, 0:P], ckvT[:, 0:P], start=True, stop=True, skip_group_check=True)
                    pe.matmul(b[:, P:WIN], qlat(h)[:, P:SEQ], ckvT, start=True, stop=True,
                              skip_group_check=True).then_inc(s_ab, 1)
                pe.wait_ge(s_nx, nx.up())
                transposed(lambda t, k: m_out[:, t, k, 0:P], 4)
                pe.wait_ge(s_nx, nx.up())
                transposed(lambda t, k: r_out[:, t, k * P:(k + 1) * P], 4)
                pe.wait_ge(s_td, tr.back(2))
                product(mixT[:, 0], 4, "dve")
                product(mixT[:, 0], 4, "dve")
                pe.wait_ge(s_td, tr.back(0))
                product(mixT[:, 1], 4, "dve")
                product(mixT[:, 1], 4, "dve")
                product(hT, KT, "act")
                product(hT, KT, "act")
                attend(lambda: pe.wait_ge(s_nx, nx.up()), latent=True)
                pe.wait_ge(s_ad, ab.back(0))
                product(mixT[:, 2], 4, "dve")
                product(mixT[:, 2], 4, "dve")
                pe.wait_ge(s_nx, nx.up())
                transposed(lambda t, k: xn[:, t, k * P:(k + 1) * P], KT)
                pe.wait_ge(s_td, tr.back(0))
                product(hT, KT, "dve")
                product(hT, KT, "dve")
                pe.wait_ge(s_nx, nx.up())
                transposed(lambda t, k: xn[:, t, k * P:(k + 1) * P], KT)
                pe.wait_ge(s_td, tr.back(0))
                seed()
                product(hT, KT, "dve")
                with repeat(pe, "ff_pe", FF_GROUPS - 1, counts, per):
                    hidden()
                    group()
                    down()
                hidden()
                down()

            def attend(ready, latent):
                ready()

                def turned(h):
                    b = tr_bank()
                    for i in range(3):
                        mm = pe.transpose(b[:, i * P:(i + 1) * P], logits[:, h, i * P:(i + 1) * P], ident)
                    mm.then_inc(s_tr, 1)

                turned(0)
                for h in range(HEADS_A):
                    if h < HEADS_A - 1:
                        turned(h + 1)
                    pe.wait_ge(s_td, tr.back(1 if h < HEADS_A - 1 else 0))
                    p = prob[:, h % SLOTS]
                    if latent and h % 2 == 0:
                        b = ab_bank()
                    if latent:
                        o = b[:, (h % 2) * SEQ:(h % 2 + 1) * SEQ]
                        v = [sm[:, s, 384:512] for s in range(2)]
                    else:
                        if h % 4 == 0:
                            b = ab_bank()
                        o = b[64 * (h % 2):64 * (h % 2) + 64, (h // 2 % 2) * SEQ:(h // 2 % 2 + 1) * SEQ]
                        v = [v2[:, s, 64 * h:64 * h + 64] for s in range(2)]
                    pe.matmul(o, v[0], p[:, 0:SEQ], start=True, stop=False, skip_group_check=True)
                    mm = pe.matmul(o[:, P:SEQ], v[1], p[:, SEQ:WIN], start=False, stop=True, skip_group_check=True)
                    mm.then_inc(s_pv, 1)
                if latent:
                    uv = small[:, L_UV:L_UV + 512]
                    pe.wait_ge(s_ad, ab.back(0))
                    for j in range(2):
                        b = ab_bank()
                        for h in range(4 * j, 4 * j + 4):
                            mm = pe.matmul(b[64 * (h % 2):64 * (h % 2) + 64, (h // 2 % 2) * SEQ:(h // 2 % 2 + 1) * SEQ],
                                           uv[:, 64 * h:64 * h + 64], qlat(h), start=True, stop=True,
                                           skip_group_check=True)
                        mm.then_inc(s_ab, 1)

            def seed():
                pe.wait_ge(s_ad, ab.back(0))
                for t in range(TT):
                    for n in range(2):
                        pe.matmul(AB[2 * t + n][:, :], ident, x[:, t, n * 512:(n + 1) * 512], start=True, stop=False,
                                  skip_group_check=True)

            def hidden():
                pe.wait_ge(s_ld, ld.back(0))
                b = tr_bank()
                for k in range(QK):
                    for t in range(TT):
                        mm = pe.transpose(b[:, k * SEQ + t * P:k * SEQ + (t + 1) * P], he[:, t, k * P:(k + 1) * P], ident)
                mm.then_inc(s_tr, 1)

            def group():
                product(hT, KT, "dve")

            def down():
                pe.wait_ge(s_td, tr.back(0))
                for n in range(2):
                    hi, lw = quarter()
                    for t in range(TT):
                        for k in range(QK):
                            for a, w in ((0, hi), (1, hi), (0, lw)):
                                mm = pe.matmul(AB[2 * t + n][:, :], heT[:, a, k, t * P:(t + 1) * P], w[:, k, :],
                                               start=False, stop=True, skip_group_check=True)
                    mm.then_inc(s_used, 1)

            def small_product(c0, n):
                b = ab_bank()
                w = sw[:].rearrange("p a (k n) -> p a k n", k=KT)
                for t in range(TT):
                    for k in range(KT):
                        for i, (a, wa) in enumerate(((0, 0), (1, 0), (0, 1))):
                            mm = pe.matmul(b[:, t * n:(t + 1) * n], hT[:, a, k, t * P:(t + 1) * P], w[:, wa, k, c0:c0 + n],
                                           start=(k == 0 and i == 0), stop=(k == KT - 1 and i == 2), skip_group_check=True)
                mm.then_inc(s_ab, 1)

            def second():
                pe.wait_ge(s_nx, nx.up())
                transposed(lambda t, k: xn[:, t, k * P:(k + 1) * P], KT)
                pe.wait_ge(s_td, tr.back(0))
                product(hT, KT, "act")
                pe.wait_ge(s_nx, nx.up())
                small_product(0, 16)
                product(hT, KT, "act")
                transposed(lambda t, k: tok[0][:, t, k * P:(k + 1) * P], 4)
                product(hT, KT, "act")
                transposed(lambda t, k: tok[1][:, t, k * P:(k + 1) * P], 4)
                product(hT, KT, "act")
                transposed(lambda t, k: tok[0][:, t, k * P:(k + 1) * P], 4)
                product(hT, KT, "act")
                transposed(lambda t, k: tok[1][:, t, k * P:(k + 1) * P], 4)
                product(hT, KT, "act")
                transposed(lambda t, k: tok[0][:, t, k * P:(k + 1) * P], 4)
                product(hT, KT, "act")
                pe.wait_ge(s_nx, nx.up())
                b = tr_bank()
                for t in range(TT):
                    mm = pe.transpose(b[0:16, t * P:(t + 1) * P], da[:, t, :], ident)
                mm.then_inc(s_tr, 1)
                product(hT, KT, "act")
                pe.wait_ge(s_nx, nx.up())
                b = tr_bank()
                for t in range(TT):
                    mm = pe.matmul(b[:, t * 16:(t + 1) * 16], rows2[:, 1, t * P:(t + 1) * P], ident[0:16, 0:16], start=True,
                                   stop=True, skip_group_check=True)
                mm.then_inc(s_tr, 1)
                pe.wait_ge(s_act, acts.up(3))
                for t in range(TT):
                    for i in range(2):
                        b = tr_bank()
                        for k in range(4):
                            mm = pe.transpose(b[:, k * P:(k + 1) * P], xbcT[i][:, k, t * P:(t + 1) * P], ident)
                        mm.then_inc(s_tr, 1)
                for g in range(2):
                    scores(ab_bank(), 0, xbcT[2][:, g, :], xbcT[2][:, 2 + g, :]).then_inc(s_ab, 1)
                pe.wait_ge(s_td, tr.back(4))
                for h in range(HEADS_A):
                    b = ab_bank()
                    r = slice(64 * (h % 2), 64 * (h % 2) + 64)
                    q, k = qkT2[r, 0, h // 2, :], qkT2[r, 1, h // 2, :]
                    pe.matmul(b[:, 0:P], q[:, 0:P], k[:, 0:P], start=True, stop=True, skip_group_check=True)
                    pe.matmul(b[:, P:WIN], q[:, P:SEQ], k, start=True, stop=True, skip_group_check=True).then_inc(s_ab, 1)

                for g in range(4):
                    for h in range(4 * g, 4 * g + 4):
                        pe.matmul(ab_bank()[:, 0:SEQ], ident[0:16, h:h + 1].to_broadcast([16, P]), rows2[:, 1, :], start=True,
                                  stop=True).then_inc(s_ab, 1)
                    product(hT, KT, "act")
                    b = ab_bank()
                    if g == 0:
                        pe.wait_ge(s_nx, nx.up())
                    for h in range(4 * g, 4 * g + 4):
                        pe.wait_ge(s_pp, pp.up())
                        weighted(b, P * (h % 4), 64, prob[:, h % SLOTS],
                                 lambda s: xdt[:, s, 64 * h:64 * h + 64]).then_inc(s_pv, 1)
                attend(lambda: pe.wait_ge(s_nx, nx.up()), latent=False)
                pe.wait_ge(s_ad, ab.back(0))
                product(mixT[:, 2], 4, "dve")
                product(mixT[:, 2], 4, "dve")
                pe.wait_ge(s_nx, nx.up())
                transposed(lambda t, k: yb[:, t, k * P:(k + 1) * P], KT)
                pe.wait_ge(s_td, tr.back(0))
                product(mixT8, KT, "dve")
                product(mixT8, KT, "dve")
                pe.wait_ge(s_nx, nx.up())
                transposed(lambda t, k: xn[:, t, k * P:(k + 1) * P], KT)
                pe.wait_ge(s_td, tr.back(0))
                product(hT, KT, "dve")
                product(hT, KT, "dve")
                pe.wait_ge(s_nx, nx.up())
                transposed(lambda t, k: xn[:, t, k * P:(k + 1) * P], KT)
                pe.wait_ge(s_td, tr.back(0))
                small_product(16, 20)
                seed()
                product(hT, KT, "dve")
                with repeat(pe, "moe_pe", EXPERTS - 1, counts, per):
                    for _ in range(2):
                        hidden()
                        group()
                        down()
                free.clear()
                hidden()
                group()
                down()
                hidden()
                down()
                pe.wait_ge(s_x, LAYERS + 2)
                pe.wait_ge(s_sm, 16 * (LAYERS + 3 + 2))
                b = tr_bank()
                for k in range(QK):
                    for t in range(TT):
                        mm = pe.transpose(b[:, k * SEQ + t * P:k * SEQ + (t + 1) * P], p_tok[:, t, k * P:(k + 1) * P], ident)
                mm.then_inc(s_tr, 1)
                transposed(lambda t, k: x[:, t, k * P:(k + 1) * P], KT)
                pe.wait_ge(s_td, tr.back(0))
                product(cqT, QK, "act")
                product(cqT, QK, "act")
                product(hT, KT, "act")
                product(hT, KT, "act")

            acts, pp = Count(s_act), Count(s_pp)
            counts.append(acts)
            pe.wait_ge(s_cst, 64)
            for i in range(2 * HEADS_A):
                if i >= 2:
                    pe.wait_ge(s_bd, i - 1)
                pe.matmul(TR[i % 2][:, 0:WIN], relb_sb[:, i // 2, :], onehot_sb[:, i % 2, :], start=True,
                          stop=True).then_inc(s_bf, 1)
            pe.wait_ge(s_bd, 2 * HEADS_A)
            with repeat(pe, "layers_pe", LAYERS, counts, per) as l:
                free.clear()
                layer(l)
            free.clear()
            second()

        @block.scalar
        def _(act):
            hi = Count(s_hi)
            used, lin, tr, ab, raws = Count(s_used), Count(s_lin), Count(s_tr), Count(s_ab), [Count(s) for s in s_raw]
            var, arg, ad, ld, xr, la, smc, pos = (Count(s_var), Count(s_arg), Count(s_ad), Count(s_ld), Count(s_x), Count(s_la),
                                             Count(s_sm), Count(s_used))
            own = Chain(s_ch_a, act)
            counts = [hi, used, lin, tr, ab, *raws, var, arg, ad, ld, xr, la, smc, pos, own]

            def high():
                if hi.n >= TOTAL_Q:
                    return
                s = hi.n % RING
                act.wait_ge(s_raw[s], raws[s].up(16))
                if hi.n >= RING:
                    act.wait_ge(s_used, used.up())
                hi.n += 1
                act.activation(w_hi[:, s, :], raw[:, s, :], ACT.Copy).then_inc(s_hi, 1)

            def unit(n, read=None):
                if read is None:
                    for _ in range(n):
                        high()
                    pos.up(n)
                    lin.up()
                    return
                for _ in range(n - 1):
                    high()
                act.wait_ge(s_lin, lin.up())
                read(0).then_inc(s_la, 1)
                act.wait_ge(s_used, pos.up(n))
                read(1).then_inc(s_la, 1)
                high()

            def roots(n, at=0):
                act.wait_ge(s_var, var.up())
                act.activation(tiny[:, 16:16 + n], tiny[:, at:at + n], ACT.Sqrt).then_inc(s_std, 1)

            def split(dst, nk, gain=None, src=None):
                for k0 in range(0, nk, 2):
                    act.wait_ge(s_tr, tr.up())
                    b = TR[(tr.n - 1) % 2]
                    if gain is None:
                        act.activation(dst[:, 0, k0:k0 + 2, :].rearrange("p k t -> p (k t)"), b[:, :], ACT.Copy).then_inc(s_th, 1)
                    else:
                        for k in range(2):
                            i = act.activation(dst[:, 0, k0 + k, :], b[:, k * SEQ:(k + 1) * SEQ], ACT.Copy,
                                               scale=small[:, gain + k0 + k:gain + k0 + k + 1])
                        i.then_inc(s_th, 1)

            def exp(dst, src, scale=1.0, func=ACT.Exp):
                act.wait_ge(s_arg, arg.up())
                act.activation(dst, src, func, scale=scale).then_inc(s_exp, 1)

            def layer(l):
                act.wait_ge(s_x, xr.up())
                act.dma_start(small[:], layer_small[l]).then_inc(s_sm, 16)
                roots(2)
                act.wait_ge(s_sm, smc.up(16))
                split(hT, KT, L_N1)
                unit(4, lambda t: act.activation(sm[:, t, :], LIN[t][:, :], ACT.Copy))
                unit(4, lambda t: act.activation(mqk_tok[:, t, :], LIN[t][:, :], ACT.Copy))
                roots(6)
                split(cqT, 2, L_QN)
                tr.up()
                unit(4, lambda t: act.activation(mv[:, t, :, 0:P], LIN[t][:, :].rearrange("p (h d) -> p h d", h=4), ACT.Copy))
                tr.up(2)
                for i in range(2):
                    unit(1, lambda t: act.activation(qT[:, i, 2 * t:2 * t + 2, :].rearrange("p a t -> p (a t)"),
                                                     LIN[t][:, :], ACT.Copy))
                exp(tn(128, 8), tn(112, 8), -1.0)
                exp(tn(144, 8), tn(136, 8), 1.0, ACT.Ln)
                act.wait_ge(s_arg, arg.up())
                act.activation(qkT.rearrange("p a t -> p (a t)"), conv_out.rearrange("p a t -> p (a t)"), ACT.Silu).then_inc(s_act, 1)
                unit(4, lambda t: act.activation(rq[:, t, :], LIN[t][:, :], ACT.Copy))
                tr.up()
                unit(4, lambda t: act.activation(rk[:, t, :], LIN[t][:, :], ACT.Copy))
                tr.up()
                unit(4, lambda t: act.activation(rv[:, t, :], LIN[t][:, :], ACT.Copy))
                exp(tn(192, 8), tn(184, 8), -1.0)
                unit(4, lambda t: act.activation(mo[:, t, :], LIN[t][:, :], ACT.Sigmoid))
                unit(4, lambda t: act.activation(rg[:, t, :], LIN[t][:, :], ACT.Silu))
                tr.up(4)
                ad.up(8)

                def gate(g, n):
                    unit(4, lambda t: act.activation(gates[:, g, t, n * 512:(n + 1) * 512], LIN[t][:, :], ACT.Sigmoid))

                gate(0, 0)
                for h in range(4):
                    act.wait_ge(s_ad, ad.up(1))
                    act.activation(wexp[:, h % SLOTS], wexp[:, h % SLOTS], ACT.Exp).then_inc(s_exp, 1)
                    ad.up(1 if h == 0 else 2)
                ad.up(1)
                gate(0, 1)
                ad.up(8)
                gate(1, 0)
                ad.up(4)
                gate(1, 1)
                ad.up(8)
                roots(8)
                split(mixT[:, 0], 4, L_MN)
                roots(8)
                split(mixT[:, 1], 4, L_RN)
                for _ in range(4):
                    unit(2)
                act.wait_ge(s_ld, ld.up(4))
                gate(0, 0)
                gate(0, 1)
                ld.up(4)
                exp(logits[:].rearrange("p h w -> p (h w)"), logits[:].rearrange("p h w -> p (h w)"))
                attend_latent()
                unit(2)
                unit(2)
                ld.up(4)
                split(hT, KT)
                unit(4)
                unit(4)
                ld.up(4)
                roots(2)
                split(hT, KT, L_N2)
                feed_forward("ff_act", FF_GROUPS)

            def attend_latent():
                tr.up(HEADS_A)
                ad.up(4)
                ab.up(40)
                for j in range(2):
                    act.wait_ge(s_ab, ab.up())
                    dst = mixT[:, 2, 0, 2 * j:2 * j + 2, :].rearrange("p k t -> p (k t)")
                    act.activation(dst, AB[ad.n % 4][:, :], ACT.Copy).then_inc(s_th, 1)
                    ad.up()

            def glu():
                for _ in range(3):
                    high()
                act.wait_ge(s_lin, lin.up())
                act.activation(gbuf[:, 0, :], LIN[0][:, 0:GLU], ACT.Silu).then_inc(s_g, 1)
                act.wait_ge(s_used, pos.up(4))
                act.activation(gbuf[:, 1, :], LIN[1][:, 0:GLU], ACT.Silu).then_inc(s_g, 1)
                high()

            def hidden_high():
                act.wait_ge(s_tr, tr.up())
                act.activation(heT[:, 0].rearrange("p k t -> p (k t)"), TR[(tr.n - 1) % 2][:, :], ACT.Copy).then_inc(s_th, 1)

            def feed_forward(name, groups):
                glu()
                with repeat(act, name, groups - 1, counts, per):
                    hidden_high()
                    glu()
                    high()
                    high()
                    pos.up(2)
                hidden_high()
                high()
                high()
                pos.up(2)

            def second():
                act.wait_ge(s_x, LAYERS + 1)
                act.dma_start(small[:, 0:S_END], second_small).then_inc(s_sm, 16)
                act.dma_start(bflat, alibi).then_inc(s_sm, 16)
                act.dma_start(gain1, gains[0]).then_inc(s_sm, 16)
                act.wait_ge(s_sm, smc.up(48))
                roots(2)
                roots(2)
                act.activation(sw[:, 0, :], small[:, S_SW:S_END], ACT.Copy).then_inc(s_sw, 1)
                split(hT, KT, S_N1)

                def by_token(i):
                    return lambda t: act.activation(tok[i][:, t, :], LIN[t][:, :], ACT.Copy)

                def silu_conv(i):
                    act.wait_ge(s_arg, arg.up())
                    v = xbcT[i].rearrange("p a t -> p (a t)")
                    act.activation(v, v, ACT.Silu).then_inc(s_act, 1)

                unit(4, by_token(0))
                exp(tn(464, 32), tn(432, 32), -1.0)
                exp(tn(528, 32), tn(496, 32), 1.0, ACT.Ln)
                act.activation(tiny[:, 720:736], small[:, S_AL:S_AL + 16], ACT.Exp).then_inc(s_exp, 1)
                unit(4, by_token(1))
                silu_conv(0)
                unit(4, by_token(0))
                silu_conv(1)
                unit(4, by_token(1))
                silu_conv(2)
                unit(4, by_token(0))
                unit(4, lambda t: act.activation(v2[:, t, :], LIN[t][:, :], ACT.Copy))
                for n in range(2):
                    unit(4, lambda t: act.activation(xn[:, t, n * 512:(n + 1) * 512], LIN[t][:, :], ACT.Silu))
                tr.up(2 * 5 + 2 + 4)
                ad.up(1 + 2 + HEADS_A)
                lv = logits[:].rearrange("p h w -> p (h w)")
                exp(lv, lv)
                act.dma_start(gain2, gains[1]).then_inc(s_sm, 16)
                act.dma_start(p_tok, p_in.rearrange("(t p) d -> p t d", p=P)).then_inc(s_sm, 16)
                for g in range(4):
                    for h in range(4 * g, 4 * g + 4):
                        act.wait_ge(s_ad, ad.up())
                        act.activation(wexp[:, h % SLOTS], wexp[:, h % SLOTS], ACT.Exp).then_inc(s_ex2, 1)
                    ad.up()
                    unit(4, lambda t: act.activation(gates[:, g // 2, t, (g % 2) * 512:(g % 2 + 1) * 512], LIN[t][:, :],
                                                     ACT.Sigmoid))
                tr.up(HEADS_A)
                for j in range(2):
                    act.wait_ge(s_pv, LAYERS * HEADS_A + SSD_HEADS + 4 * (j + 1))
                    dst = mixT[:, 2, 0, 2 * j:2 * j + 2, :].rearrange("p k t -> p (k t)")
                    act.activation(dst, AB[ad.n % 4][:, :], ACT.Copy).then_inc(s_th, 1)
                    ad.up()
                roots(4)
                unit(2)
                unit(2)
                split(mixT8, KT, S_NS)
                unit(4)
                unit(4)
                split(hT, KT)
                unit(4)
                unit(4)
                roots(2)
                split(hT, KT, S_N2)
                ad.up()
                for c in (832, 952):
                    exp(tiny[:, c:c + 8], tiny[:, c:c + 8])
                glu()
                with repeat(act, "moe_act", EXPERTS - 1, counts, per):
                    for _ in range(2):
                        hidden_high()
                        glu()
                        high()
                        high()
                        pos.up(2)
                hidden_high()
                glu()
                high()
                high()
                pos.up(2)
                hidden_high()
                high()
                high()
                pos.up(2)
                split(cqT, QK)
                split(hT, KT)
                for n in range(2):
                    unit(1, lambda t: act.activation(ple[:, t, n * 512:(n + 1) * 512], LIN[t][:, :], ACT.Copy))
                for n in range(2):
                    unit(4, lambda t: act.activation(tmpg2[n][:, t, :], LIN[t][:, :], ACT.Sigmoid))
                roots(2)

            act.wait_ge(s_bd, 2 * HEADS_A)
            for i in range(2):
                act.dma_start(scratch[i], windows[i]).then_inc(s_b, 16)
            act.wait_ge(s_b, 32)
            act.dma_start(bias[:, :, 0:P], bass.AP(scratch.tensor, P - 1, [[HEADS_A * WIN - 1, P], [WIN, HEADS_A], [1, P]])).then_inc(s_b, 16)
            act.dma_start(bias[:, :, P:WIN], bass.AP(scratch.tensor, P * HEADS_A * WIN + P - 1,
                                                     [[HEADS_A * WIN - 1, P], [WIN, HEADS_A], [1, SEQ]])).then_inc(s_b, 16)
            for _ in range(RING):
                high()
            with repeat(act, "layers_act", LAYERS, counts, per) as l:
                layer(l)
            second()

        @block.gpsimd
        def _(pool):
            nc.gpsimd.memset(ones[:], 1.0)
            nc.gpsimd.memset(mv[:, :, :, P:P + 1], 1.0).then_inc(s_z, 1)
            la = Count(s_la)
            own = Chain(s_ch_p, pool)
            with repeat(pool, "layers_pool", LAYERS, [la, own], per):
                pool.wait_ge(s_la, la.up(14))
                cos4 = cosv.unsqueeze(2).broadcast_to([P, TT, 4, 64])
                sin4 = sinv.unsqueeze(2).broadcast_to([P, TT, 4, 64])
                for src, at in ((rq, 0), (rk, 1024)):
                    v = heads(src)
                    x1, x2 = v[:, :, :, 0:64], v[:, :, :, 64:128]
                    t1 = xflat[:, at:at + 512].rearrange("p (t h d) -> p t h d", t=TT, h=4)
                    t2 = xflat[:, at + 512:at + 1024].rearrange("p (t h d) -> p t h d", t=TT, h=4)
                    nc.gpsimd.tensor_tensor(t1, x2, sin4, ALU.mult)
                    own(nc.gpsimd.tensor_tensor(t2, x1, sin4, ALU.mult))
                    nc.gpsimd.tensor_tensor(x1, x1, cos4, ALU.mult)
                    own(nc.gpsimd.tensor_tensor(x2, x2, cos4, ALU.mult))
                    nc.gpsimd.tensor_tensor(x1, x1, t1, ALU.subtract)
                    nc.gpsimd.tensor_tensor(x2, x2, t2, ALU.add).then_inc(s_rot, 1)
                la.up(18)
            ex, pv = Count(s_ex2), Count(s_pv)
            pv.n = LAYERS * HEADS_A
            for h in range(SSD_HEADS):
                pool.wait_ge(s_ex2, ex.up())
                if h >= SLOTS:
                    pool.wait_ge(s_pv, pv.n + h - SLOTS + 1)
                nc.gpsimd.tensor_tensor(prob[:, h % SLOTS], wexp[:, h % SLOTS], cb[:, h // 8, :], ALU.mult).then_inc(s_pp, 1)

        @block.vector
        def _(dve):
            lo = Count(s_hi)
            lin, pos, tr, th, ab, ad, std, exps, la, ld, g, pv, td, xr, bdd = (
                Count(s_lin), Count(s_used), Count(s_tr), Count(s_th), Count(s_ab), Count(s_ad), Count(s_std),
                Count(s_exp), Count(s_la), Count(s_ld), Count(s_g), Count(s_pv), Count(s_td), Count(s_x), Count(s_bd))
            smc = Count(s_sm)
            own = Chain(s_ch_d, dve)
            counts = [lo, lin, pos, tr, th, ab, ad, std, exps, la, ld, g, pv, smc, own]

            def low():
                if lo.n >= TOTAL_Q:
                    return
                dve.wait_ge(s_hi, lo.up())
                s = (lo.n - 1) % RING
                dve.tensor_tensor(w_lo[:, s, :], raw[:, s, :], w_hi[:, s, :].bitcast(F32), ALU.subtract).then_inc(s_lo, 1)

            def unit(n, read=None):
                for _ in range(n - 1 if read else n):
                    low()
                v = lin.up()
                if read is None:
                    pos.up(n)
                    return
                dve.wait_ge(s_lin, v)
                read(0)
                dve.wait_ge(s_used, pos.up(n))
                read(1)
                low()

            def col(at, i=0):
                return small[:, at + i:at + i + 1]

            def tc(at, i=0):
                return tiny[:, at + i:at + i + 1]

            def squares(v, junk, n, i):
                return dve.tensor_tensor_reduce(junk, v, v, 1.0 / n, 0.0, ALU.mult, ALU.add, tc(0, i))

            def rstd(n):
                v, s, r, t = (tiny[:, a:a + n] for a in (0, 16, 32, 48))
                dve.tensor_scalar(v, v, EPS, None, ALU.add).then_inc(s_var, 1)
                dve.wait_ge(s_std, std.up())
                own(dve.reciprocal(r, s))
                own(dve.tensor_tensor(t, r, r, ALU.mult))
                own(dve.tensor_tensor(t, t, v, ALU.mult))
                own(dve.tensor_scalar(t, t, -0.5, 1.5, ALU.mult, ALU.add))
                own(dve.tensor_tensor(r, r, t, ALU.mult))

            def norm_x():
                for t in range(TT):
                    i = squares(x[:, t, :], xn[:, t, :], D, t)
                own(i)
                rstd(2)
                for t in range(TT):
                    i = dve.tensor_scalar(xn[:, t, :], x[:, t, :], tc(32, t), None, ALU.mult)
                i.then_inc(s_nx, 1)

            def split(dst, nk, gain=None):
                for k0 in range(0, nk, 2):
                    dve.wait_ge(s_th, th.up())
                    tr.up()
                    b = TR[(tr.n - 1) % 2]
                    for k in range(2):
                        hi = dst[:, 0, k0 + k, :].bitcast(F32)
                        bk = b[:, k * SEQ:(k + 1) * SEQ]
                        if gain is None:
                            i = dve.tensor_tensor(dst[:, 1, k0 + k, :], bk, hi, ALU.subtract)
                        else:
                            i = dve.scalar_tensor_tensor(dst[:, 1, k0 + k, :], bk, col(gain, k0 + k), hi, ALU.mult, ALU.subtract)
                    i.then_inc(s_td, 1)

            def tr_bank():
                dve.wait_ge(s_tr, tr.up())
                return TR[(tr.n - 1) % 2]

            def ab_bank():
                ad.up()
                dve.wait_ge(s_ab, ab.up())
                return AB[(ad.n - 1) % 4]

            def log1p_exp_minus(f, n, exp_at):
                a, e, w, ln, d, z = (tiny[:, k:k + n] for k in exp_at)
                dve.scalar_tensor_tensor(a, f, -1.0, f, ALU.mult, ALU.max).then_inc(s_arg, 1)
                dve.wait_ge(s_exp, exps.up())
                dve.tensor_scalar(w, e, 1.0, None, ALU.add).then_inc(s_arg, 1)
                dve.wait_ge(s_exp, exps.up())
                own(dve.tensor_scalar(d, w, -1.0, None, ALU.add))
                own(dve.tensor_scalar(z, d, 0.0, None, ALU.is_equal))
                own(dve.tensor_tensor(d, d, z, ALU.add))
                own(dve.reciprocal(d, d))
                own(dve.tensor_tensor(ln, ln, e, ALU.mult))
                own(dve.tensor_tensor(ln, ln, d, ALU.mult))
                own(dve.tensor_tensor(z, z, e, ALU.mult))
                own(dve.tensor_tensor(ln, ln, z, ALU.add))

            def small_norms():
                dve.wait_ge(s_la, la.up(2))
                own(dve.tensor_copy(g16, sm[:, :, 320:336]))
                dve.tensor_scalar(g16[:, :, 0:8], g16[:, :, 0:8], 8 ** -0.5 * 64 ** -0.5, None, ALU.mult)
                for t in range(TT):
                    squares(sm[:, t, 0:256], xflat[:, 512 * t:512 * t + 256], 256, t)
                    squares(sm[:, t, 384:512], xflat[:, 512 * t + 256:512 * t + 384], P, 2 + t)
                own(dve.tensor_reduce(tiny[:, 52:54], sm[:, :, 256:320], AX.X, ALU.add))
                own(dve.tensor_scalar(tiny[:, 52:54], tiny[:, 52:54], 1.0 / 64, None, ALU.mult))
                for t in range(TT):
                    i = dve.tensor_scalar(sm[:, t, 256:320], sm[:, t, 256:320], tc(52, t), None, ALU.subtract)
                own(i)
                for t in range(TT):
                    i = squares(sm[:, t, 256:320], xflat[:, 64 * t:64 * t + 64], 64, 4 + t)
                own(i)
                rstd(6)
                for t in range(TT):
                    dve.tensor_scalar(sm[:, t, 0:256], sm[:, t, 0:256], tc(32, t), None, ALU.mult)
                    dve.scalar_tensor_tensor(sm[:, t, 384:512], sm[:, t, 384:512], tc(34, t), small[:, L_KV:L_KV + P],
                                             ALU.mult, ALU.mult)
                    dve.tensor_scalar(sm[:, t, 320:384], sm[:, t, 256:320], tc(36, t), None, ALU.mult)
                    i = dve.tensor_scalar(sm[:, t, 256:320], sm[:, t, 256:320], tc(36, t), None, ALU.mult)
                i.then_inc(s_nx, 1)
                split(cqT, 2, L_QN)
                b = tr_bank()
                dve.tensor_scalar(kidxT, b[:, 0:SEQ], col(L_KI), None, ALU.mult)
                dve.tensor_copy(ckvT, b[:, SEQ:2 * SEQ]).then_inc(s_td, 1)

            def gate_logs():
                ib = small[:, L_IB:L_IB + 8].rearrange("p (g h) -> p g h", g=2)
                fx = tn(120, TT, 4)
                dve.tensor_tensor(gif[:, :, 0:4], g16[:, :, 8:12], ib[:, 0:1, :].broadcast_to([P, TT, 4]), ALU.add)
                own(dve.tensor_tensor(fx, g16[:, :, 12:16], ib[:, 1:2, :].broadcast_to([P, TT, 4]), ALU.add))
                log1p_exp_minus(tiny[:, 120:128], 8, (112, 128, 136, 144, 152, 160))
                own(dve.tensor_scalar(fx, fx, 0.0, None, ALU.min))
                dve.tensor_tensor(gif[:, :, 4:8], fx, tn(144, TT, 4), ALU.subtract).then_inc(s_nx, 1)

            def conv(dst, src, tiles, taps, bias_at=None, f0=0):
                for j in range(4):
                    for f in range(tiles):
                        s, w = src[:, f, j:j + SEQ], col(taps, 4 * (f0 + f) + j)
                        if j == 0:
                            i = dve.tensor_scalar(dst[:, f, :], s, w, None if bias_at is None else col(bias_at, f0 + f),
                                                  ALU.mult, ALU.bypass if bias_at is None else ALU.add)
                        else:
                            i = dve.scalar_tensor_tensor(dst[:, f, :], s, w, dst[:, f, :], ALU.mult, ALU.add)
                    if j < 3:
                        own(i)
                i.then_inc(s_arg, 1)

            def gate_rows():
                b = tr_bank()
                dve.tensor_copy(rows[:, 0:2, :].rearrange("p a b -> p (a b)"), b[0:4, :]).then_inc(s_td, 1)
                dve.wait_ge(s_td, tr.back(0))
                own(dve.tensor_tensor_scan(rows[:, 4, :], ones[0:4, :], rows[:, 1, :], 0.0, ALU.mult, ALU.add))
                own(dve.tensor_tensor(rows[:, 0, :], rows[:, 0, :], rows[:, 4, :], ALU.subtract))
                own(dve.tensor_tensor_scan(rows[:, 1, :], ones[0:4, :], rows[:, 0, :], 0.0, ALU.mult, ALU.max))
                dve.tensor_scalar(rows[:, 2, :], rows[:, 1, :], -1.0, None, ALU.mult)
                dve.tensor_tensor(rows[:, 3, :], rows[:, 1, :], rows[:, 4, :], ALU.add).then_inc(s_nx, 1)

            def index_scores():
                for h in range(8):
                    b = ab_bank()
                    dst = work if h == 0 else relu_w
                    dve.tensor_scalar(dst[:, 0:P], b[:, 0:P], 0.0, g16[:, 0, h:h + 1], ALU.max, ALU.mult)
                    dve.tensor_scalar(dst[:, P:WIN], b[:, P:WIN], 0.0, g16[:, 1, h:h + 1], ALU.max, ALU.mult).then_inc(s_ad, 1)
                    dve.wait_ge(s_ad, ad.back(0))
                    if h:
                        own(dve.tensor_tensor(work, work, relu_w, ALU.add))
                dve.tensor_tensor(work[:, 0:P], work[:, 0:P], qmask, ALU.add)
                own(dve.tensor_tensor(work[:, SEQ:WIN], work[:, SEQ:WIN], qmask, ALU.add))

            def take(n):
                for _ in range(n):
                    for i, c in ((0, slice(0, P)), (1, slice(P, WIN))):
                        if i == 0:
                            dve.memset(tc(1001), 0.0)
                        j = dve.max(lflat[:, 2 * WIN + 8 * i:2 * WIN + 8 * i + 8], work[:, c])
                    own(j)
                    for i, c in ((0, slice(0, P)), (1, slice(P, WIN))):
                        if i == 0:
                            dve.memset(tc(1002), 0.0)
                        j = dve.match_replace(work[:, c], lflat[:, 2 * WIN + 8 * i:2 * WIN + 8 * i + 8], work[:, c], TAKEN)
                    own(j)

            def taken():
                own(dve.tensor_scalar(keep, work, TAKEN / 2, -BIG, ALU.is_gt, ALU.mult))
                dve.tensor_tensor(keep[:, 0:P], keep[:, 0:P], qmask, ALU.add)
                own(dve.tensor_tensor(keep[:, SEQ:WIN], keep[:, SEQ:WIN], qmask, ALU.add))

            def mlstm():
                def args(h):
                    b = ab_bank()
                    dve.scalar_tensor_tensor(wexp[:, h % SLOTS, 0:SEQ], b[:, 0:SEQ], acol[:, 0, h:h + 1], mask, ALU.add, ALU.add)
                    dve.scalar_tensor_tensor(wexp[:, h % SLOTS, SEQ:WIN], b[:, P:SEQ], acol[:, 1, h:h + 1], mask[:, 0:P],
                                             ALU.add, ALU.add).then_inc(s_ad, 1)
                    b = ab_bank()
                    dve.wait_ge(s_exp, exps.up())
                    dve.scalar_tensor_tensor(prob[:, h % SLOTS], b[:, 0:WIN], 64 ** -0.5, wexp[:, h % SLOTS], ALU.mult,
                                             ALU.mult).then_inc(s_ad, 1)

                args(0)
                for h in range(4):
                    if h < 3:
                        args(h + 1)
                    b = ab_bank()
                    dve.tensor_copy(m_out[:, :, h, :], b[:, 0:258].rearrange("p (t v) -> p t v", t=TT)).then_inc(s_ad, 1)

            def retain():
                def decayed(h):
                    b = ab_bank()
                    dve.tensor_tensor(prob[:, h % SLOTS, 0:SEQ], b[:, 0:SEQ], ret_decay[:, h, :], ALU.mult)
                    dve.tensor_tensor(prob[:, h % SLOTS, SEQ:WIN], b[:, SEQ:WIN], ret_decay[:, h, 0:P], ALU.mult).then_inc(s_ad, 1)

                decayed(0)
                for h in range(4):
                    if h < 3:
                        decayed(h + 1)
                    b = ab_bank()
                    dve.tensor_copy(r_out[:, :, h * P:(h + 1) * P], b[:, 0:SEQ].rearrange("p (t v) -> p t v", t=TT)).then_inc(s_ad, 1)

            def spread(v):
                return v.unsqueeze(3).broadcast_to([P, TT, 4, P])

            def head_norm(o, gate):
                sq = xflat[:, 0:1024].rearrange("p (t h d) -> p t h d", t=TT, h=4)
                mean, var, r = tn(56, TT, 4), tn(0, TT, 4), tn(32, TT, 4)
                own(dve.tensor_reduce(mean, o, AX.X, ALU.add))
                own(dve.tensor_scalar(mean, mean, 1.0 / P, None, ALU.mult))
                own(dve.tensor_tensor(o, o, spread(mean), ALU.subtract))
                own(dve.tensor_tensor(sq, o, o, ALU.mult))
                own(dve.tensor_reduce(var, sq, AX.X, ALU.add))
                own(dve.tensor_scalar(var, var, 1.0 / P, None, ALU.mult))
                rstd(8)
                own(dve.tensor_tensor(o, o, spread(r), ALU.mult))
                dve.tensor_tensor(o, o, heads(gate), ALU.mult).then_inc(s_nx, 1)

            def softmax_args():
                mx = tiny[:, 208:224].rearrange("p (t h) -> p t h", t=TT)
                parts = ((0, logits[:, :, 0:P], P), (1, logits[:, :, P:WIN], SEQ))
                for t, v, n in parts:
                    i = dve.tensor_reduce(mx[:, t, :], v, AX.X, ALU.max)
                own(i)
                for t, v, n in parts:
                    i = dve.tensor_tensor(v, v, mx[:, t, :].unsqueeze(2).broadcast_to([P, HEADS_A, n]), ALU.subtract)
                i.then_inc(s_arg, 1)

            def softmax_probs():
                mx = tiny[:, 208:224].rearrange("p (t h) -> p t h", t=TT)
                parts = ((0, logits[:, :, 0:P], P), (1, logits[:, :, P:WIN], SEQ))
                dve.wait_ge(s_exp, exps.up())
                for t, v, n in parts:
                    i = dve.tensor_reduce(mx[:, t, :], v, AX.X, ALU.add)
                own(i)
                own(dve.reciprocal(tiny[:, 208:224], tiny[:, 208:224]))
                for t, v, n in parts:
                    i = dve.tensor_tensor(v, v, mx[:, t, :].unsqueeze(2).broadcast_to([P, HEADS_A, n]), ALU.mult)
                i.then_inc(s_nx, 1)

            def by_key(h):
                b = tr_bank()
                v = pv.up()
                if h >= SLOTS:
                    dve.wait_ge(s_pv, pv.back(SLOTS))
                dve.tensor_copy(prob[:, h % SLOTS], b[:, 0:WIN]).then_inc(s_td, 1)

            def attend_latent():
                def latent(j):
                    dve.wait_ge(s_pv, pv.back(HEADS_A - 2 - 2 * j if j == 3 else 1))
                    ad.up()
                    dve.tensor_copy(two_heads(j), AB[(ad.n - 1) % 4][:, :]).then_inc(s_ad, 1)

                by_key(0)
                by_key(1)
                for j in range(4):
                    if j < 3:
                        by_key(2 * j + 2)
                        latent(j)
                        by_key(2 * j + 3)
                    else:
                        latent(j)
                for j in range(2):
                    dve.wait_ge(s_th, th.up())
                    ab.up()
                    ad.up()
                    dst = mixT[:, 2, 1, 2 * j:2 * j + 2, :].rearrange("p k t -> p (k t)")
                    hi = mixT[:, 2, 0, 2 * j:2 * j + 2, :].rearrange("p k t -> p (k t)").bitcast(F32)
                    dve.tensor_tensor(dst, AB[(ad.n - 1) % 4][:, :], hi, ALU.subtract).then_inc(s_ad, 1)

            def two_heads(j):
                return (qlatA if j < 2 else qlatB)[:, 2 * (j % 2):2 * (j % 2) + 2, :].rearrange("p a t -> p (a t)")

            def branch(g, n, first=False, last=False):
                def read(t):
                    y, gt = xn[:, t, n * 512:(n + 1) * 512], gates[:, g, t, n * 512:(n + 1) * 512]
                    if first:
                        dve.tensor_tensor(y, LIN[t][:, :], gt, ALU.mult).then_inc(s_ld, 1)
                        ld.up()
                        return
                    dve.tensor_tensor(tmpy[:, t, :], LIN[t][:, :], gt, ALU.mult).then_inc(s_ld, 1)
                    dve.wait_ge(s_ld, ld.up())
                    i = dve.tensor_tensor(y, y, tmpy[:, t, :], ALU.add)
                    if last and t == 1:
                        i.then_inc(s_nx, 1)
                return read

            def residual(n):
                def read(t):
                    v = x[:, t, n * 512:(n + 1) * 512]
                    dve.tensor_tensor(v, LIN[t][:, :], v, ALU.add).then_inc(s_ld, 1)
                    ld.up()
                return read

            def glu(scale=None):
                for _ in range(3):
                    low()
                lin.up()
                for t in range(TT):
                    dve.wait_ge(s_g, g.up())
                    if t == 1:
                        pos.up(4)
                    ld.up()
                    if scale is None:
                        i = dve.tensor_tensor(he[:, t, :], LIN[t][:, GLU:2 * GLU], gbuf[:, t, :], ALU.mult)
                    else:
                        i = dve.scalar_tensor_tensor(he[:, t, :], LIN[t][:, GLU:2 * GLU], scale(t), gbuf[:, t, :],
                                                     ALU.mult, ALU.mult)
                    i.then_inc(s_ld, 1)
                low()

            def hidden_low():
                dve.wait_ge(s_th, th.up())
                tr.up()
                b = TR[(tr.n - 1) % 2]
                dve.tensor_tensor(heT[:, 1].rearrange("p k t -> p (k t)"), b[:, :],
                                  heT[:, 0].rearrange("p k t -> p (k t)").bitcast(F32), ALU.subtract).then_inc(s_td, 1)

            def feed_forward(name, groups):
                glu()
                with repeat(dve, name, groups - 1, counts, per):
                    hidden_low()
                    glu()
                    low()
                    low()
                    pos.up(2)
                hidden_low()
                low()
                low()
                dve.wait_ge(s_used, pos.up(2))
                for t in range(TT):
                    for n in range(2):
                        ad_done = dve.tensor_copy(x[:, t, n * 512:(n + 1) * 512], AB[2 * t + n][:, :])
                ad_done.then_inc(s_x, 1)
                dve.wait_ge(s_x, xr.up())

            def layer(l):
                norm_x()
                dve.wait_ge(s_sm, smc.up(16))
                split(hT, KT, L_N1)
                unit(4)
                unit(4)
                small_norms()
                unit(4)
                dve.wait_ge(s_la, la.up(2))
                own(dve.memset(conv_in[:, :, 0:3], 0.0))
                for j in range(2):
                    b = tr_bank()
                    dve.tensor_copy(conv_in[:, 2 * j:2 * j + 2, 3:SEQ + 3],
                                    b[:, :].rearrange("p (a t) -> p a t", a=2)).then_inc(s_td, 1)
                dve.wait_ge(s_td, tr.back(0))
                unit(1)
                unit(1)
                gate_logs()
                conv(conv_out, conv_in, 4, L_CW)
                unit(4)
                gate_rows()
                index_scores()
                unit(4)
                b = tr_bank()
                dve.tensor_copy(tiny[:, 184:192], b[:, 8:16]).then_inc(s_arg, 1)
                dve.tensor_copy(tiny[:, 176:184], b[:, 0:8]).then_inc(s_td, 1)
                dve.wait_ge(s_td, tr.back(0))
                take(2)
                unit(4)
                exps.up()
                take(2)
                unit(4)
                take(2)
                unit(4)
                take(2)
                taken()
                for dst in (rqT[:, 0], rqT[:, 1]):
                    for j in range(2):
                        b = tr_bank()
                        dve.tensor_copy(dst[:, 2 * j:2 * j + 2, :].rearrange("p a t -> p (a t)"), b[:, :]).then_inc(s_td, 1)
                unit(4)
                mlstm()
                unit(4)
                retain()
                unit(4)
                for j in range(4):
                    b = ab_bank()
                    dst = (qlatA if j < 2 else qlatB)[:, j % 2:4:2, :]
                    dve.tensor_scalar(dst, b[:, :].rearrange("p (a t) -> p a t", a=2), 64 ** -0.5, None, ALU.mult).then_inc(s_ad, 1)
                unit(4)
                for h in range(HEADS_A):
                    b = ab_bank()
                    i = dve.tensor_tensor(logits[:, h, :], b[:, 0:WIN], bias[:, h, :], ALU.add)
                    i.then_inc(s_ad, 1)
                dve.wait_ge(s_ad, ad.back(0))
                total = m_out[:, :, :, P:P + 1].rearrange("p t h a -> p t (h a)")
                own(dve.scalar_tensor_tensor(den, total, -1.0, total, ALU.mult, ALU.max))
                own(dve.tensor_tensor(den, den, em, ALU.max))
                own(dve.reciprocal(den, den))
                own(dve.tensor_tensor(m_out[:, :, :, 0:P], m_out[:, :, :, 0:P], spread(den), ALU.mult))
                dve.wait_ge(s_la, la.up(24))
                head_norm(m_out[:, :, :, 0:P], mo)
                split(mixT[:, 0], 4, L_MN)
                head_norm(heads(r_out), rg)
                split(mixT[:, 1], 4, L_RN)
                own(dve.tensor_tensor(logits[:], logits[:], keep.unsqueeze(1).broadcast_to([P, HEADS_A, WIN]), ALU.add))
                softmax_args()
                unit(2, branch(0, 0, first=True))
                unit(2, branch(0, 1, first=True))
                unit(2, branch(1, 0))
                unit(2, branch(1, 1))
                unit(4)
                unit(4)
                softmax_probs()
                attend_latent()
                dve.wait_ge(s_la, la.up(4))
                unit(2, branch(0, 0))
                unit(2, branch(0, 1, last=True))
                split(hT, KT)
                unit(4, residual(0))
                unit(4, residual(1))
                dve.wait_ge(s_ld, ld.back(0))
                norm_x()
                split(hT, KT, L_N2)
                feed_forward("ff_dve", FF_GROUPS)

            def first_of(v, out, at):
                m = tn(at, TT, 1)
                own(dve.tensor_reduce(m, v, AX.X, ALU.max))
                own(dve.tensor_tensor(out, v, m.broadcast_to([P, TT, 4]), ALU.is_equal))
                own(dve.tensor_tensor(out, out, tn(772, 1, 4).broadcast_to([P, TT, 4]), ALU.mult))
                own(dve.tensor_reduce(tn(776, TT, 1), out, AX.X, ALU.max))
                own(dve.tensor_tensor(out, out, tn(776, TT, 1).broadcast_to([P, TT, 4]), ALU.is_equal))

            def route():
                for i in range(4):
                    own(dve.memset(tiny[:, 772 + i:773 + i], 4.0 - i))
                lg = tn(780, TT, 20)
                b = ab_bank()
                dve.tensor_tensor(lg, b[:, 0:40].rearrange("p (t n) -> p t n", t=TT),
                                  small[:, S_BR:S_BR + 20].unsqueeze(1).broadcast_to([P, TT, 20]), ALU.add).then_inc(s_ad, 1)
                dve.wait_ge(s_ad, ad.back(0))
                four = [P, TT, 4]
                gp, og, ei, o1, e2, o2, cig = (tn(832 + 8 * i, TT, 4) for i in range(7))
                pw, m1, m2, ex, w1, w2 = (tn(900 + 2 * i, TT, 1) for i in range(6))
                own(dve.tensor_reduce(m1, lg[:, :, 0:4], AX.X, ALU.max))
                dve.tensor_tensor(gp, lg[:, :, 0:4], m1.broadcast_to(four), ALU.subtract).then_inc(s_arg, 1)
                dve.wait_ge(s_exp, exps.up())
                own(dve.tensor_reduce(m1, gp, AX.X, ALU.add))
                own(dve.reciprocal(m1, m1))
                own(dve.tensor_tensor(gp, gp, m1.broadcast_to(four), ALU.mult))
                first_of(gp, og, 900)
                m = tn(920, TT, 16).rearrange("p t (g j) -> p t g j", g=4)
                own(dve.tensor_tensor(m, lg[:, :, 4:20].rearrange("p t (g j) -> p t g j", g=4),
                                      og.unsqueeze(3).broadcast_to([P, TT, 4, 4]), ALU.mult))
                own(dve.tensor_reduce(ei, m.rearrange("p t g j -> p t j g"), AX.X, ALU.add))
                first_of(ei, o1, 902)
                own(dve.scalar_tensor_tensor(e2, o1, -BIG, ei, ALU.mult, ALU.add))
                first_of(e2, o2, 904)
                own(dve.memset(tiny[:, 952:960], 0.0))
                dve.tensor_tensor(tn(952, TT, 4), m2.broadcast_to(four), m1.broadcast_to(four), ALU.subtract).then_inc(s_arg, 1)
                dve.wait_ge(s_exp, exps.up())
                ex = tn(952, TT, 4)[:, :, 0:1]
                own(dve.tensor_scalar(w1, ex, 1.0, None, ALU.add))
                own(dve.reciprocal(w1, w1))
                own(dve.tensor_tensor(w1, w1, pw, ALU.mult))
                own(dve.tensor_tensor(w2, w1, ex, ALU.mult))
                own(dve.tensor_tensor(o1, o1, w1.broadcast_to(four), ALU.mult))
                own(dve.tensor_tensor(o2, o2, w2.broadcast_to(four), ALU.mult))
                own(dve.tensor_tensor(cig, o1, o2, ALU.add))
                own(dve.tensor_tensor(comb.rearrange("p t (g j) -> p t g j", g=4), og.unsqueeze(3).broadcast_to([P, TT, 4, 4]),
                                      cig.unsqueeze(2).broadcast_to([P, TT, 4, 4]), ALU.mult))

            def norm_rows(gain, dst):
                for t in range(TT):
                    i = squares(x[:, t, :], xn[:, t, :], D, t)
                own(i)
                rstd(2)
                for t in range(TT):
                    i = dve.scalar_tensor_tensor(dst[:, t, :], x[:, t, :], tc(32, t), gain, ALU.mult, ALU.mult)
                return i

            def second():
                dve.wait_ge(s_sm, smc.up(48))
                own(norm_rows(gain1, x))
                own(dve.memset(conv2[:, :, 0:3], 0.0))
                norm_x()
                dve.wait_ge(s_sw, 1)
                dve.tensor_tensor(sw[:, 1, :], small[:, S_SW:S_END], sw[:, 0, :].bitcast(F32), ALU.subtract).then_inc(s_nx, 1)
                split(hT, KT, S_N1)
                unit(4)
                b = ab_bank()
                f = tn(400, TT, 16)
                dve.tensor_tensor(f, b[:, 0:32].rearrange("p (t n) -> p t n", t=TT),
                                  small[:, S_DTB:S_DTB + 16].unsqueeze(1).broadcast_to([P, TT, 16]), ALU.add).then_inc(s_ad, 1)
                dve.wait_ge(s_ad, ad.back(0))
                log1p_exp_minus(tiny[:, 400:432], 32, (432, 464, 496, 528, 560, 592))
                own(dve.tensor_scalar(f, f, 0.0, None, ALU.max))
                own(dve.tensor_tensor(dt, f, tn(528, TT, 16), ALU.add))
                dve.wait_ge(s_exp, exps.up())
                own(dve.tensor_scalar(tiny[:, 720:736], tiny[:, 720:736], -1.0, None, ALU.mult))
                dve.tensor_tensor(da, dt, tiny[:, 720:736].unsqueeze(1).broadcast_to([P, TT, 16]), ALU.mult).then_inc(s_nx, 1)

                def conv_chunk(c):
                    for j in range(2):
                        b = tr_bank()
                        dve.tensor_copy(conv2[:, 2 * j:2 * j + 2, 3:SEQ + 3],
                                        b[:, :].rearrange("p (a t) -> p a t", a=2)).then_inc(s_td, 1)
                    dve.wait_ge(s_td, tr.back(0))
                    conv(xbcT[c], conv2, 4, S_CW, S_CB, 4 * c)

                unit(4)
                conv_chunk(0)
                unit(4)
                conv_chunk(1)
                unit(4)
                conv_chunk(2)
                for i in range(2):
                    unit(4)
                    for j in range(2):
                        b = tr_bank()
                        dve.tensor_copy(qkT2[:, i, 2 * j:2 * j + 2, :].rearrange("p a t -> p (a t)"), b[:, :]).then_inc(s_td, 1)
                unit(4)
                b = tr_bank()
                dve.tensor_copy(rows2[:, 0, :], b[0:16, 0:SEQ]).then_inc(s_td, 1)
                dve.wait_ge(s_td, tr.back(0))
                dve.tensor_tensor_scan(rows2[:, 1, :], ones[:], rows2[:, 0, :], 0.0, ALU.mult, ALU.add).then_inc(s_nx, 1)
                unit(4)
                b = tr_bank()
                dve.tensor_copy(cs, b[:, 0:32].rearrange("p (t n) -> p t n", t=TT)).then_inc(s_td, 1)
                for t in range(TT):
                    for i in range(2):
                        b = tr_bank()
                        dve.tensor_copy(xs[:, t, i * 512:(i + 1) * 512], b[:, :]).then_inc(s_td, 1)
                for g in range(2):
                    b = ab_bank()
                    dve.tensor_copy(cb[:, g, :], b[:, 0:WIN]).then_inc(s_ad, 1)
                for h in range(HEADS_A):
                    b = ab_bank()
                    dve.scalar_tensor_tensor(logits[:, h, :], b[:, 0:WIN], 64 ** -0.5, bias[:, h, :], ALU.mult,
                                             ALU.add).then_inc(s_ad, 1)
                dve.wait_ge(s_ad, ad.back(0))
                softmax_args()

                def by_head(v):
                    return v.rearrange("p t (h d) -> p t h d", h=SSD_HEADS)

                def over(v):
                    return v.unsqueeze(3).broadcast_to([P, TT, SSD_HEADS, 64])

                for g in range(4):
                    for h in range(4 * g, 4 * g + 4):
                        b = ab_bank()
                        if h >= SLOTS:
                            dve.wait_ge(s_pp, h - SLOTS + 1)
                        dve.scalar_tensor_tensor(wexp[:, h % SLOTS, 0:SEQ], b[:, 0:SEQ], cs[:, 0, h:h + 1], mask,
                                                 ALU.subtract, ALU.add)
                        dve.scalar_tensor_tensor(wexp[:, h % SLOTS, SEQ:WIN], b[:, P:SEQ], cs[:, 1, h:h + 1], mask[:, 0:P],
                                                 ALU.subtract, ALU.add).then_inc(s_ad, 1)
                    if g == 0:
                        skip = small[:, S_DS:S_DS + 16].unsqueeze(1).broadcast_to([P, TT, 16])
                        dve.tensor_tensor(by_head(yb), by_head(xs), over(skip), ALU.mult)
                        dve.tensor_tensor(by_head(xdt), by_head(xs), over(dt), ALU.mult).then_inc(s_nx, 1)
                    unit(4)
                    pv.up(4)
                    dve.wait_ge(s_pv, pv.back(0))
                    ad.up()
                    yv = by_head(yb)[:, :, 4 * g:4 * g + 4, :]
                    src = AB[(ad.n - 1) % 4][:, :].rearrange("p (h t d) -> p t h d", h=4, t=TT)
                    dve.tensor_tensor(yv, src, yv, ALU.add).then_inc(s_ad, 1)
                softmax_probs()
                for h in range(HEADS_A):
                    by_key(h)
                for j in range(2):
                    dve.wait_ge(s_th, th.up())
                    ad.up()
                    dst = mixT[:, 2, 1, 2 * j:2 * j + 2, :].rearrange("p k t -> p (k t)")
                    hi = mixT[:, 2, 0, 2 * j:2 * j + 2, :].rearrange("p k t -> p (k t)").bitcast(F32)
                    dve.tensor_tensor(dst, AB[(ad.n - 1) % 4][:, :], hi, ALU.subtract).then_inc(s_ad, 1)
                dve.wait_ge(s_la, la.up(2 * 8))
                own(dve.tensor_tensor(yb, yb, xn[:], ALU.mult))
                for t in range(TT):
                    for g in range(2):
                        i = squares(yb[:, t, g * 512:(g + 1) * 512], xdt[:, t, g * 512:(g + 1) * 512], 512, 2 * t + g)
                own(i)
                rstd(4)
                for t in range(TT):
                    for g in range(2):
                        v = yb[:, t, g * 512:(g + 1) * 512]
                        i = dve.tensor_scalar(v, v, tc(32, 2 * t + g), None, ALU.mult)
                i.then_inc(s_nx, 1)
                dve.wait_ge(s_la, la.up(2 * 4))
                unit(2, branch(0, 0, first=True))
                unit(2, branch(0, 1, first=True))
                split(mixT8, KT, S_NS)
                unit(4, branch(1, 0))
                unit(4, branch(1, 1, last=True))
                split(hT, KT)
                unit(4, residual(0))
                unit(4, residual(1))
                dve.wait_ge(s_ld, ld.back(0))
                norm_x()
                split(hT, KT, S_N2)
                route()
                glu(lambda t: comb[:, t, 0:1])
                with repeat(dve, "moe_dve", EXPERTS - 1, counts, per) as e:
                    for i in range(2):
                        hidden_low()
                        glu(lambda t: comb[:, t, bass.ds(e + i, 1)])
                        low()
                        low()
                        pos.up(2)
                hidden_low()
                glu(lambda t: comb[:, t, EXPERTS - 1:EXPERTS])
                low()
                low()
                pos.up(2)
                hidden_low()
                low()
                low()
                dve.wait_ge(s_used, pos.up(2))
                for t in range(TT):
                    for n in range(2):
                        i = dve.tensor_copy(x[:, t, n * 512:(n + 1) * 512], AB[2 * t + n][:, :])
                i.then_inc(s_x, 1)
                dve.wait_ge(s_x, xr.up())
                split(cqT, QK)
                split(hT, KT)
                unit(1)
                unit(1)
                for n in range(2):
                    unit(4)
                    dve.wait_ge(s_la, la.up(6 if n == 0 else 2))
                    pl = ple[:, :, n * 512:(n + 1) * 512]
                    own(dve.tensor_tensor(pl, pl, tmpg2[n], ALU.mult))
                    v = x[:, :, n * 512:(n + 1) * 512]
                    own(dve.tensor_tensor(v, v, pl, ALU.add))
                dve.wait_ge(s_sm, smc.up(32))
                norm_rows(gain2, xn).then_inc(s_x, 1)

            dve.wait_ge(s_cst, 64)
            dve.wait_ge(s_z, 1)
            for i in range(2 * HEADS_A):
                dve.wait_ge(s_bf, i + 1)
                j = dve.tensor_copy(windows[i % 2][:, (i // 2) * WIN:(i // 2 + 1) * WIN], TR[i % 2][:, 0:WIN])
                j.then_inc(s_bd, 1)
            dve.wait_ge(s_b, 64)
            own(dve.memset(tiny[:], 0.0))
            dve.tensor_copy(tiny[:, 1000:1001], tiny[:, 1:2]).then_inc(s_x, 1)
            dve.wait_ge(s_x, xr.up())
            for _ in range(RING):
                low()
            with repeat(dve, "layers_dve", LAYERS, counts + [xr], per) as l:
                layer(l)
            second()


def split_rows(w):
    k, n = w.shape
    q = w.reshape(k // (QK * P), QK, P, n // QC, QC).transpose(3, 0, 2, 1, 4)
    return q.reshape(-1, P, QK * QC)


def glu_rows(g, u, d):
    groups = g.shape[1] // GLU
    gu = [split_rows(np.concatenate([g[:, i * GLU:(i + 1) * GLU], u[:, i * GLU:(i + 1) * GLU]], 1)) for i in range(groups)]
    dn = [split_rows(d[i * GLU:(i + 1) * GLU]) for i in range(groups)]
    out = [gu[0]]
    for i in range(1, groups):
        out += [gu[i], dn[i - 1]]
    return out + [dn[-1]]


def columns(v):
    return v.reshape(-1, P).T


def layer_stream(a, l):
    w = a["w_in"][l]
    at = np.cumsum([0, 256, 256, 512, 4, 4, 512, 256, 64, 8, 128, 512, 512, 512, 512, 1024, 1024, 1024])
    mq, mk, mv, mi, mf, mo, cq, kidx, widx, ckv, rq, rk, rv, rg, gm, ga, gr = (w[:, at[i]:at[i + 1]] for i in range(17))
    small = np.concatenate([cq, kidx, widx, mi, mf, np.zeros((D, 48), np.float32), ckv], 1)
    p = {n: a[n][l] for n in ("p_m", "p_a", "p_r")}
    parts = [split_rows(small), split_rows(np.concatenate([mq, mk], 1)), split_rows(mv), split_rows(a["a_wuq"][l]),
             split_rows(a["a_wuq_idx"][l]), split_rows(rq), split_rows(rk), split_rows(rv), split_rows(mo),
             split_rows(rg), split_rows(gm), split_rows(gr), split_rows(p["p_m"]), split_rows(p["p_r"]),
             split_rows(ga), split_rows(p["p_a"]), split_rows(a["w_out"][l])]
    return parts + glu_rows(a["w_gate"][l], a["w_up"][l], a["w_down"][l])


def second_stream(a):
    w = a["w_in_2"][0]
    at = np.cumsum([0, 512, 512, 512, 1024, 1536, 16, 1024, 1024])
    q, k, v, z, xbc, _, ga, gb = (w[:, at[i]:at[i + 1]] for i in range(8))
    wide = lambda n: np.concatenate(list(a[n][0]), 1)
    parts = [split_rows(m) for m in (xbc, q, k, v, z, ga, gb, a["w_out_a_2"][0], a["w_out_b_2"][0], a["w_out_2"][0])]
    parts += glu_rows(wide("w_gate_2"), wide("w_up_2"), np.concatenate(list(a["w_down_2"][0]), 0))
    return parts + [split_rows(a["w_ple_proj_2"][0]), split_rows(a["w_ple_gate_2"][0])]


def second_params(a):
    rep = lambda v: np.broadcast_to(v, (P, v.size))
    cw = a["conv_w_2"][0].reshape(4, 12, P).transpose(2, 1, 0).reshape(P, 48)
    dtw = a["w_in_2"][0][:, 4096:4112]
    sw = np.concatenate([dtw, a["w_rg_2"][0], a["w_re_2"][0]], 1).reshape(KT, P, 36).transpose(1, 0, 2).reshape(P, 8 * 36)
    return np.concatenate([columns(a["mix_norm_g_2"][0]), columns(a["ffn_norm_g_2"][0]), columns(a["ssd_norm_g_2"][0]), cw,
                           columns(a["conv_b_2"][0]), rep(a["dt_bias_2"][0]), rep(a["a_log_2"][0]), rep(a["d_skip_2"][0]),
                           rep(a["b_rg_2"][0]), rep(a["b_re_2"][0]), sw], 1)


def alibi_bias():
    i = np.arange(P)
    out = np.zeros((P, HEADS_A, WIN), np.float32)
    for t, c, n in ((0, 0, P), (1, P, SEQ)):
        dist = (t * P + i)[:, None] - np.arange(n)[None, :]
        for h in range(HEADS_A):
            out[:, h, c:c + n] = np.where(dist >= 0, -2.0 ** -(h + 1) * dist, -BIG)
    return out.reshape(P, HEADS_A * WIN)


def layer_params(a, l):
    rep = lambda v: np.broadcast_to(v, (P, v.size))
    cw = a["m_conv"][l].reshape(4, 4, P).transpose(2, 1, 0).reshape(P, 16)
    uk = a["a_wuk"][l].reshape(4, P, P).transpose(1, 0, 2).reshape(P, 512)
    uv = a["a_wuv"][l].transpose(1, 0, 2).reshape(P, 512)
    ki = np.concatenate([a["a_kidx_g"][l]] * 2)
    return np.concatenate([columns(a["norm1_g"][l]), columns(a["norm2_g"][l]), columns(a["a_qnorm_g"][l]), columns(ki),
                           columns(a["m_norm_g"][l]), columns(a["r_norm_g"][l]), cw, rep(a["a_kvnorm_g"][l]),
                           rep(a["m_ibias"][l]), rep(a["m_fbias"][l]), uk, uv], 1)


def constants():
    f = np.float32
    i = np.arange(P)
    pos = np.arange(SEQ)
    mask = np.where(pos[None, :] >= i[:, None], 0, -BIG).astype(f)
    qmask = np.where(i[None, :] <= i[:, None], 0, -BIG).astype(f)
    lg = np.log1p(-np.exp2(-5.0 - np.arange(4)))
    diff = pos[None, :] - i[:, None]
    ret = [np.where(diff >= 0, np.exp(np.maximum(diff, 0) * g) * P ** -0.5, 0).astype(f) for g in lg]
    ang = pos.astype(f)[:, None] * (f(10000.0) ** (-np.linspace(0, 1, 64).astype(f)))[None, :]
    by = lambda v: v.astype(f).reshape(TT, P, 64).transpose(1, 0, 2).reshape(P, 128)
    const = np.concatenate([np.eye(P, dtype=f), mask, qmask, *ret, by(np.cos(ang)), by(np.sin(ang))], 1)
    half = BUCKETS // 2
    onehot = np.zeros((BUCKETS, TT, WIN), f)
    for t in range(TT):
        for j in range(WIN):
            dist = t * P + P - 1 - j
            if dist >= 0:
                b = dist if dist < half else min(half + int(np.log(dist / half) / math.log(128 / half) * half), BUCKETS - 1)
                onehot[b, t, j] = 1
    return const, onehot


def kernel(**a):
    import concourse.bacc as bacc
    from concourse.bass_utils import run_bass_kernel_spmd

    a = {k: np.asarray(v) for k, v in a.items()}
    const, onehot = constants()
    quarters = []
    for l in range(LAYERS):
        quarters += layer_stream(a, l)
    quarters += second_stream(a)
    assert sum(len(v) for v in quarters) == TOTAL_Q
    arrays = {
        "stream": np.concatenate(quarters),
        "const": const,
        "layer_small": np.stack([layer_params(a, l) for l in range(LAYERS)]),
        "x_in": np.ascontiguousarray(a["x"][0]),
        "onehot": onehot,
        "second_small": second_params(a),
        "alibi": alibi_bias(),
        "gains": np.stack([np.broadcast_to(a[n], (P, D)) for n in ("final_norm_g", "final_norm_g_2")]),
        "p_in": np.ascontiguousarray(a["p_2"][0, 0]),
        "relb": np.ascontiguousarray(np.broadcast_to(a["rel_bias"][:, :, None], (BUCKETS, HEADS_A, P))),
    }
    per = {}
    for trial in range(2):
        nc = bacc.Bacc("TRN2", target_bir_lowering=False, num_devices=1, dynamic_dma_scratch_size=1024)
        t = {n: nc.dram_tensor(f"in_{n}", v.shape, F32, kind="ExternalInput").ap() for n, v in arrays.items()}
        scratch = nc.dram_tensor("bias_windows", [TT, P, HEADS_A * WIN], F32, kind="Internal").ap()
        out = nc.dram_tensor("out", [SEQ, D], F32, kind="ExternalOutput").ap()
        program(nc, t["stream"], t["const"], t["layer_small"], t["x_in"], t["onehot"], t["relb"], scratch,
                t["second_small"], t["alibi"], t["gains"], t["p_in"], out, per)
    r = run_bass_kernel_spmd(nc, [{f"in_{n}": v for n, v in arrays.items()}], core_ids=[0])
    return r.results[0]["out"][None]
```

```python
import math
from contextlib import ExitStack, contextmanager

import numpy as np

import concourse.bass as bass
from concourse import mybir

F32 = mybir.dt.float32
F32R = mybir.dt.float32r
ALU = mybir.AluOpType
ACT = mybir.ActivationFunctionType
AX = mybir.AxisListType

P = 128
SEQ = 256
TT = SEQ // P
D = 1024
KT = D // P
LAYERS = 2
EPS = 1e-6
QK = 2
QC = 512
RING = 3
BIG = 1e30
TAKEN = -3e38
HEADS_A = 8
WIN = SEQ + P
TOPK = 64
SLOTS = 4
SSD_HEADS = 16
BUCKETS = 32
GLU = 256
D_FF = 2816
FF_GROUPS = D_FF // GLU
EXPERTS = 16
MOE_FF = 512
MOE_GROUPS_PER_EXPERT = MOE_FF // GLU
LAYER_Q = 4 * 14 + 2 + 2 * 6 + 4 * 2 + 6 * FF_GROUPS
SECOND_Q = 4 * 12 + 2 * 2 + 4 * 2 + 4 * 2 + 6 * EXPERTS * MOE_GROUPS_PER_EXPERT + 2 + 4 * 2
TOTAL_Q = LAYERS * LAYER_Q + SECOND_Q

C_ID, C_MASK, C_QMASK, C_RET = 0, 128, 384, 512
C_COS, C_SIN, C_END = C_RET + 4 * SEQ, C_RET + 4 * SEQ + 128, C_RET + 4 * SEQ + 256
L_N1, L_N2, L_QN, L_KI, L_MN, L_RN, L_CW, L_KV, L_IB, L_UK, L_UV, L_END = (
    0, 8, 16, 18, 19, 23, 27, 43, 171, 179, 179 + 512, 179 + 1024)
(S_N1, S_N2, S_NS, S_CW, S_CB, S_DTB, S_AL, S_DS, S_BR, S_SW, S_END) = (
    0, 8, 16, 24, 72, 84, 100, 116, 132, 152, 152 + 8 * 36)


class Count:

    def __init__(self, sem):
        self.sem, self.reg, self.n = sem, 0, 0

    def up(self, k=1):
        self.n += k
        return self.reg + self.n

    def back(self, k):
        return self.reg + self.n - k


class Chain(Count):

    def __init__(self, sem, eng):
        super().__init__(sem)
        self.eng = eng

    def __call__(self, ins):
        ins.then_inc(self.sem, 1)
        self.eng.wait_ge(self.sem, self.up())


@contextmanager
def repeat(eng, name, trips, counts, per):
    with eng.Fori(0, trips) as i:
        saved = [(c, c.reg, c.n) for c in counts]
        for k, c in enumerate(counts):
            c.reg = c.reg + i * per.get((name, k), 6)
        yield i
    for k, (c, reg, n) in enumerate(saved):
        per[(name, k)] = c.n - n
        c.reg = reg
        c.n += (c.n - n) * (trips - 1)


def program(nc, stream, const, small_in, x_in, onehot, relb, scratch, alibi, gains, p_in, out, per):
    ctx = ExitStack()
    with ctx:
        def sb(name, shape, dt=F32):
            return ctx.enter_context(nc.sbuf_tensor(name, shape, dt))

        def sem(name):
            return ctx.enter_context(nc.semaphore(name))

        raw = sb("raw", [P, RING, QK * QC])
        w_hi = sb("w_hi", [P, RING, QK * QC], F32R)
        w_lo = sb("w_lo", [P, RING, QK * QC], F32R)
        cst = sb("cst", [P, C_END])
        ident = cst[:, C_ID:C_ID + P]
        mask = cst[:, C_MASK:C_MASK + SEQ]
        qmask = cst[:, C_QMASK:C_QMASK + P]
        ret_decay = cst[:, C_RET:C_RET + 4 * SEQ].rearrange("p (h t) -> p h t", h=4)
        cosv = cst[:, C_COS:C_COS + 128].rearrange("p (t d) -> p t d", t=TT)
        sinv = cst[:, C_SIN:C_SIN + 128].rearrange("p (t d) -> p t d", t=TT)
        small = sb("small", [P, L_END])
        x = sb("x", [P, TT, D])
        hT = sb("hT", [P, 2, KT, SEQ], F32R)
        xn = sb("xn", [P, TT, D])
        bias = sb("bias", [P, HEADS_A, WIN])
        mixT = sb("mixT", [P, 3, 2, 4, SEQ], F32R)
        heT = mixT[:, 0].rearrange("p a k t -> p (a k t)")[:, 0:2 * QK * SEQ].rearrange("p (a k t) -> p a k t", a=2, k=QK)
        logits = sb("logits", [P, HEADS_A, WIN])
        gates = sb("gates", [P, 2, TT, D])
        arena = sb("arena", [P, 14 * 1024 + 64])
        tiny = sb("tiny", [P, 1024])
        ones = sb("ones", [16, SEQ])
        wexp = sb("wexp", [P, SLOTS, WIN])
        prob = sb("prob", [P, SLOTS, WIN])
        sw = sb("sw", [P, 2, 8 * 36], F32R)
        rows2 = sb("rows2", [16, 2, SEQ])

        def ar(at, *shape):
            n = int(np.prod(shape))
            v = arena[:, at:at + n]
            if len(shape) == 2:
                return v.rearrange("p (a b) -> p a b", b=shape[1])
            if len(shape) == 3:
                return v.rearrange("p (a b c) -> p a b c", b=shape[1], c=shape[2])
            if len(shape) == 4:
                return v.rearrange("p (a b c d) -> p a b c d", b=shape[1], c=shape[2], d=shape[3])
            return v

        gates_flat = gates[:].rearrange("p g t d -> p (g t d)")
        windows = logits[:].rearrange("p h w -> p (h w)"), gates_flat[:, 0:HEADS_A * WIN]
        relb_sb = arena[0:BUCKETS, 0:HEADS_A * P].rearrange("p (h t) -> p h t", h=HEADS_A)
        onehot_sb = arena[0:BUCKETS, 1024:1024 + 2 * WIN].rearrange("p (t w) -> p t w", t=2)
        cqT = mixT[:, 2].rearrange("p a k t -> p (a k t)")[:, 0:2 * QK * SEQ].rearrange("p (a k t) -> p a k t", a=2, k=QK)
        gbuf, he = ar(0, TT, GLU), ar(TT * GLU, TT, GLU)
        K1 = 1024
        mqk_tok = ar(0, TT, 512)
        qkT = ar(0, 4, SEQ)
        conv_in = ar(K1, 4, SEQ + 3)
        m_out = ar(K1, TT, 4, 129)
        mv = ar(2 * K1 + 16, TT, 4, 129)
        sm = ar(3 * K1 + 64, TT, 512)
        A0 = 4 * K1 + 64
        rq = ar(A0, TT, 512)
        r_out = ar(A0, TT, 512)
        rk = ar(A0 + K1, TT, 512)
        rv = ar(A0 + 2 * K1, TT, 512)
        rg = ar(A0 + 3 * K1, TT, 512)
        mo = ar(A0 + 4 * K1, TT, 512)
        qT = ar(A0 + 5 * K1, 2, 4, SEQ)
        rqT = ar(A0 + 7 * K1, 2, 4, SEQ)
        rot = ar(A0 + 9 * K1, TT, 4, 64)
        kidxT = ar(A0 + 9 * K1 + 512, SEQ)
        ckvT = ar(A0 + 9 * K1 + 768, SEQ)
        conv_out = qkT
        tmpy = mo
        qlatA = ar(0, 4, SEQ)
        qlatB = ar(A0 + K1, 4, SEQ)

        def qlat(h):
            return (qlatA if h < 4 else qlatB)[:, h % 4, :]

        bank = [ctx.enter_context(nc.psum_tensor(f"bank{i}", [P, 512], F32)) for i in range(8)]
        LIN, TR, AB = bank[0:2], bank[2:4], bank[4:8]

        s_raw = [sem(f"raw_in{i}") for i in range(RING)]
        s_hi = sem("hi_done")
        s_lo = sem("lo_done")
        s_used = sem("quarter_used")
        s_lin = sem("lin_full")
        s_la = sem("lin_read_act")
        s_ld = sem("lin_read_dve")
        s_tr = sem("tr_full")
        s_th = sem("tr_hi")
        s_td = sem("tr_read")
        s_ab = sem("mix_full")
        s_ad = sem("mix_read")
        s_var = sem("var_ready")
        s_std = sem("std_ready")
        s_rs = sem("rms_ready")
        s_nx = sem("normed")
        s_arg = sem("exp_arg")
        s_ex2 = sem("decay_exp")
        s_pp = sem("pool_probs")
        s_sw = sem("small_weights_hi")
        s_rot = sem("rotated")
        s_pv = sem("values_summed")
        s_bf, s_bd = sem("bias_full"), sem("bias_read")
        s_exp = sem("exp_done")
        s_act = sem("act_out")
        s_x = sem("x_ready")
        s_g = sem("glu_gate")
        s_sm = sem("small_in")
        s_alibi = sem("alibi_in")
        s_cst = sem("const_in")
        s_b = sem("bias_moved")
        s_ch_d = sem("dve_chain")
        s_ch_a = sem("act_chain")
        s_ch_p = sem("pool_chain")
        s_out = sem("out_written")
        s_z = sem("cleared")

        block = ctx.enter_context(nc.Block())

        @block.sync
        def _(sp):
            sp.dma_start(x[:], x_in.rearrange("(t p) d -> p t d", p=P)).then_inc(s_cst, 16)
            sp.dma_start(cst[:], const).then_inc(s_cst, 16)
            sp.dma_start(relb_sb, relb).then_inc(s_cst, 16)
            sp.dma_start(onehot_sb, onehot).then_inc(s_cst, 16)
            sp.dma_start(small[:], small_in[0]).then_inc(s_sm, 16)
            for i in range(RING):
                sp.dma_start(raw[:, i], stream[i]).then_inc(s_raw[i], 16)

            def load(r):
                for i in range(RING):
                    src = stream[r * RING + i]
                    sp.wait_ge(s_hi, r * RING + (i + 1 - RING))
                    sp.wait_ge(s_lo, r * RING + (i + 1 - RING))
                    sp.dma_start(raw[:, i], src).then_inc(s_raw[i], 16)

            sp.wait_ge(s_bd, 2 * HEADS_A)
            for i in range(2):
                sp.dma_start(scratch[i], windows[i]).then_inc(s_b, 16)
            load(1)
            sp.wait_ge(s_b, 32)
            sp.dma_start(bias[:, :, 0:P], bass.AP(scratch.tensor, P - 1, [[HEADS_A * WIN - 1, P], [WIN, HEADS_A], [1, P]])).then_inc(s_b, 16)
            sp.dma_start(bias[:, :, P:WIN], bass.AP(scratch.tensor, P * HEADS_A * WIN + P - 1,
                                                    [[HEADS_A * WIN - 1, P], [WIN, HEADS_A], [1, SEQ]])).then_inc(s_b, 16)
            with sp.Fori(2, TOTAL_Q // RING) as r:
                load(r)
            sp.wait_ge(s_x, LAYERS + 3)
            sp.dma_start(out.rearrange("(t p) d -> p t d", p=P), xn[:]).then_inc(s_out, 16)
            sp.wait_ge(s_out, 16)

        tok = [ar(0, TT, 512), ar(K1, TT, 512)]
        yb = ar(0, TT, D)
        conv2 = ar(2 * K1, 4, SEQ + 3)
        xbcT = [ar(3 * K1 + 16 + i * K1, 4, SEQ) for i in range(3)]
        xs = ar(6 * K1 + 16, TT, D)
        xdt = ar(8 * K1 + 16, TT, D)
        qkT2 = ar(10 * K1 + 16, 2, 4, SEQ)
        v2 = ar(12 * K1 + 16, TT, 512)
        cb = ar(13 * K1 + 16, 2, WIN)
        mixT8 = mixT[:, 0:2].rearrange("p m a k t -> p (m a k t)").rearrange("p (a k t) -> p a k t", a=2, k=KT)
        bflat = bias[:].rearrange("p h w -> p (h w)")
        gain1 = gates_flat[:, 0:D]
        gain2 = bflat[:, 0:D]
        p_tok = bflat[:, D:D + 512].rearrange("p (t d) -> p t d", t=TT)
        ple = gates[:, 0]
        tmpg2 = [ar(0, TT, 512), ar(K1, TT, 512)]

        def tn(at, *shape):
            n = int(np.prod(shape))
            v = tiny[:, at:at + n]
            if len(shape) == 2:
                return v.rearrange("p (a b) -> p a b", b=shape[1])
            return v

        g16 = tn(64, TT, 16)
        gif = tn(96, TT, 8)
        acol, mcol = tn(176, TT, 4), tn(184, TT, 4)
        em = tn(192, TT, 4)
        den = tn(200, TT, 4)
        keep = tn(256, WIN)
        dt, da, cs = tn(624, TT, 16), tn(656, TT, 16), tn(688, TT, 16)
        X_INV = 1008
        comb = tn(740, TT, 16)
        lflat = logits[:].rearrange("p h w -> p (h w)")
        work = lflat[:, 0:WIN]
        relu_w = lflat[:, WIN:2 * WIN]
        best = lflat[:, 2 * WIN:2 * WIN + 8]
        rows = lflat[0:4, 1152:1152 + 5 * SEQ].rearrange("p (a b) -> p a b", b=SEQ)
        xflat = xn[:].rearrange("p t d -> p (t d)")

        def heads(v):
            return v.rearrange("p t (h d) -> p t h d", h=4)

        @block.tensor
        def _(pe):
            lo, tr, ab = Count(s_lo), Count(s_td), Count(s_ad)
            la, ld, nx, rot = Count(s_la), Count(s_ld), Count(s_nx), Count(s_rot)
            counts = [lo, tr, ab, la, ld, nx, rot]
            free = {}

            def quarter():
                pe.wait_ge(s_lo, lo.up())
                s = (lo.n - 1) % RING
                return (w_hi[:, s, :].rearrange("p (k n) -> p k n", k=QK),
                        w_lo[:, s, :].rearrange("p (k n) -> p k n", k=QK))

            def claim(b, reader):
                if b in free:
                    c, n = free[b]
                    pe.wait_ge(c.sem, c.reg + n)
                c = la if reader == "act" else ld
                c.up()
                free[b] = (c, c.n)

            def product(lhs, nk, reader, between=None, feed=None):
                if feed:
                    for k0 in range(0, 2 * QK, QK):
                        transposed(feed, QK, k0)
                for k0 in range(0, nk, QK):
                    if feed:
                        if 0 < k0 and k0 + QK < nk:
                            transposed(feed, QK, k0 + QK)
                        pe.wait_ge(s_td, tr.back(1 if k0 + QK < nk else 0))
                    hi, lw = quarter()
                    for t in range(TT):
                        if k0 == 0:
                            claim(t, reader)
                        for k in range(QK):
                            for n, (a, w) in enumerate(((0, hi), (1, hi), (0, lw))):
                                mm = pe.matmul(LIN[t][:, :], lhs[:, a, k0 + k, t * P:(t + 1) * P], w[:, k, :],
                                               start=(k0 + k == 0 and n == 0), stop=(k0 + k == nk - 1 and n == 2))
                        if t == 0 and k0 + QK == nk:
                            mm.then_inc(s_lin, 1)
                    mm.then_inc(s_used, 1)
                    if between and k0 + QK == nk // 2:
                        between()

            def tr_bank():
                f = tr.up()
                if tr.n > 2:
                    pe.wait_ge(s_td, f - 2)
                return TR[(tr.n - 1) % 2]

            def ab_bank():
                f = ab.up()
                if ab.n > 4:
                    pe.wait_ge(s_ad, f - 4)
                return AB[(ab.n - 1) % 4]

            def transposed(src, nk, first=0):
                for k0 in range(first, first + nk, 2):
                    b = tr_bank()
                    for k in range(2):
                        for t in range(TT):
                            mm = pe.transpose(b[:, k * SEQ + t * P:k * SEQ + (t + 1) * P], src(t, k0 + k), ident)
                    mm.then_inc(s_tr, 1)

            def scores(b, at, k, q):
                pe.matmul(b[:, at:at + SEQ], k[:, 0:P], q, start=True, stop=True, skip_group_check=True)
                return pe.matmul(b[:, at + SEQ:at + WIN], k[:, P:SEQ], q[:, P:SEQ], start=True, stop=True,
                                 skip_group_check=True)

            def weighted(b, at, n, w, v):
                pe.matmul(b[:, at:at + n], w[:, 0:P], v(0), start=True, stop=True, skip_group_check=True)
                pe.matmul(b[:, at + n:at + 2 * n], w[:, P:SEQ], v(0), start=True, stop=False, skip_group_check=True)
                return pe.matmul(b[:, at + n:at + 2 * n], w[:, SEQ:WIN], v(1), start=False, stop=True,
                                 skip_group_check=True)

            def x_cols(t, k):
                return x[:, t, k * P:(k + 1) * P]

            def y_cols(t, k):
                return xn[:, t, k * P:(k + 1) * P]

            def layer(l):
                pe.wait_ge(s_x, xr.up())
                product(hT, KT, "act", feed=x_cols)
                product(hT, KT, "act")

                def qk_by_feature():
                    pe.wait_ge(s_la, la.back(2))
                    transposed(lambda t, k: mqk_tok[:, t, k * P:(k + 1) * P], 4)

                product(hT, KT, "act", between=qk_by_feature)

                def small_by_feature():
                    pe.wait_ge(s_nx, nx.up())
                    transposed(lambda t, k: sm[:, t, k * P:(k + 1) * P], 4)

                product(hT, KT, "act", between=small_by_feature)
                pe.wait_ge(s_td, tr.back(1))
                for i in range(2):
                    hi, lw = quarter()
                    for f in range(4):
                        if f % 2 == 0:
                            claim(f // 2, "act")
                        for k in range(QK):
                            for n, (w, a) in enumerate(((hi, 0), (lw, 0), (hi, 1))):
                                mm = pe.matmul(LIN[f // 2][:, (f % 2) * SEQ:(f % 2 + 1) * SEQ], w[:, k, f * P:(f + 1) * P],
                                               cqT[:, a, k, :], start=(k == 0 and n == 0), stop=(k == QK - 1 and n == 2),
                                               skip_group_check=True)
                        if f == 1:
                            mm.then_inc(s_lin, 1)
                    mm.then_inc(s_used, 1)

                def gate_rows():
                    pe.wait_ge(s_nx, nx.up())
                    b = tr_bank()
                    for g in range(2):
                        for t in range(TT):
                            mm = pe.transpose(b[0:4, g * SEQ + t * P:g * SEQ + (t + 1) * P], gif[:, t, 4 * g:4 * g + 4], ident)
                    mm.then_inc(s_tr, 1)

                product(hT, KT, "act", between=gate_rows)
                pe.wait_ge(s_td, tr.back(1))
                for g in range(8):
                    b = ab_bank()
                    r = slice(64 * (g % 2), 64 * (g % 2) + 64)
                    pe.matmul(b[:, 0:P], qT[r, 1, g // 2, 0:P], kidxT[r, 0:P], start=True, stop=True, skip_group_check=True)
                    pe.matmul(b[:, P:WIN], qT[r, 1, g // 2, P:SEQ], kidxT[r, :], start=True, stop=True,
                              skip_group_check=True).then_inc(s_ab, 1)

                def gate_columns():
                    pe.wait_ge(s_nx, nx.up())
                    b = tr_bank()
                    for g, row in enumerate((0, 3)):
                        for t in range(TT):
                            mm = pe.matmul(b[:, 8 * g + 4 * t:8 * g + 4 * t + 4], rows[:, row, t * P:(t + 1) * P],
                                           ident[0:4, 0:4], start=True, stop=True, skip_group_check=True)
                    mm.then_inc(s_tr, 1)

                def rotated(src):
                    def turn():
                        pe.wait_ge(s_rot, rot.up())
                        transposed(lambda t, k: src[:, t, k * P:(k + 1) * P], 4)
                    return turn

                product(hT, KT, "act", between=gate_columns)
                product(hT, KT, "act", between=rotated(rq))
                product(hT, KT, "act", between=rotated(rk))
                product(hT, KT, "act")
                pe.wait_ge(s_act, acts.up())

                def m_scores(h):
                    b = ab_bank()
                    pe.matmul(b[:, 0:SEQ], ident[0:4, h:h + 1].to_broadcast([4, P]), rows[:, 2, :], start=True,
                              stop=True).then_inc(s_ab, 1)
                    b = ab_bank()
                    r = slice(64 * (h % 2), 64 * (h % 2) + 64)
                    scores(b, 0, qkT[r, 2 + h // 2, :], qkT[r, h // 2, :]).then_inc(s_ab, 1)
                    return ab.back(0)

                weights = [m_scores(0)]
                for h in range(4):
                    if h < 3:
                        weights.append(m_scores(h + 1))
                    pe.wait_ge(s_ad, weights[h])
                    b = ab_bank()
                    weighted(b, 0, 129, prob[:, h % SLOTS], lambda s: mv[:, s, h, :]).then_inc(s_ab, 1)
                product(hT, KT, "act")

                def r_scores(h):
                    scores(ab_bank(), 0, rqT[:, 1, h, :], rqT[:, 0, h, :]).then_inc(s_ab, 1)
                    return ab.back(0)

                pe.wait_ge(s_td, tr.back(0))
                weights = [r_scores(0)]
                for h in range(4):
                    if h < 3:
                        weights.append(r_scores(h + 1))
                    pe.wait_ge(s_ad, weights[h])
                    b = ab_bank()
                    weighted(b, 0, P, prob[:, h % SLOTS], lambda s: rv[:, s, h * P:(h + 1) * P]).then_inc(s_ab, 1)
                product(hT, KT, "act")
                pe.wait_ge(s_ad, ab.back(0))
                uk = small[:, L_UK:L_UK + 512].rearrange("p (a c) -> p a c", a=4)
                for j in range(4):
                    b = ab_bank()
                    r = slice(64 * (j % 2), 64 * (j % 2) + 64)
                    for i in range(2):
                        pair = 2 * (j // 2) + i
                        mm = pe.matmul(b[:, i * SEQ:(i + 1) * SEQ], uk[r, pair, :], qT[r, 0, pair, :], start=True, stop=True,
                                       skip_group_check=True)
                    mm.then_inc(s_ab, 1)
                product(hT, KT, "act")
                pe.wait_ge(s_ad, ab.back(0))
                for h in range(HEADS_A):
                    b = ab_bank()
                    pe.matmul(b[:, 0:P], qlat(h)[:, 0:P], ckvT[:, 0:P], start=True, stop=True, skip_group_check=True)
                    pe.matmul(b[:, P:WIN], qlat(h)[:, P:SEQ], ckvT, start=True, stop=True,
                              skip_group_check=True).then_inc(s_ab, 1)
                pe.wait_ge(s_nx, nx.up(2))
                transposed(lambda t, k: m_out[:, t, k, 0:P], 4)
                transposed(lambda t, k: r_out[:, t, k * P:(k + 1) * P], 4)
                pe.wait_ge(s_td, tr.back(2))
                product(mixT[:, 0], 4, "dve")
                product(mixT[:, 0], 4, "dve")
                pe.wait_ge(s_td, tr.back(0))
                product(mixT[:, 1], 4, "dve")
                product(mixT[:, 1], 4, "dve")
                product(hT, KT, "act")
                product(hT, KT, "act")
                attend(lambda: pe.wait_ge(s_nx, nx.up()), latent=True)
                pe.wait_ge(s_ad, ab.back(0))
                product(mixT[:, 2], 4, "dve")
                product(mixT[:, 2], 4, "dve")
                pe.wait_ge(s_nx, nx.up())
                product(hT, KT, "dve", feed=y_cols)
                product(hT, KT, "dve")
                pe.wait_ge(s_nx, nx.up())
                product(hT, KT, "dve", feed=x_cols)
                seed()
                with repeat(pe, "ff_pe", FF_GROUPS - 1, counts, per):
                    hidden()
                    group()
                    down()
                hidden()
                down()

            def attend(ready, latent):
                ready()

                def turned(h):
                    b = tr_bank()
                    for i in range(3):
                        mm = pe.transpose(b[:, i * P:(i + 1) * P], logits[:, h, i * P:(i + 1) * P], ident)
                    mm.then_inc(s_tr, 1)

                turned(0)
                for h in range(HEADS_A):
                    if h < HEADS_A - 1:
                        turned(h + 1)
                    pe.wait_ge(s_td, tr.back(1 if h < HEADS_A - 1 else 0))
                    p = prob[:, h % SLOTS]
                    if latent and h % 2 == 0:
                        b = ab_bank()
                    if latent:
                        o = b[:, (h % 2) * SEQ:(h % 2 + 1) * SEQ]
                        v = [sm[:, s, 384:512] for s in range(2)]
                    else:
                        if h % 4 == 0:
                            b = ab_bank()
                        o = b[64 * (h % 2):64 * (h % 2) + 64, (h // 2 % 2) * SEQ:(h // 2 % 2 + 1) * SEQ]
                        v = [v2[:, s, 64 * h:64 * h + 64] for s in range(2)]
                    pe.matmul(o, v[0], p[:, 0:SEQ], start=True, stop=False, skip_group_check=True)
                    mm = pe.matmul(o[:, P:SEQ], v[1], p[:, SEQ:WIN], start=False, stop=True, skip_group_check=True)
                    mm.then_inc(s_pv, 1)
                if latent:
                    uv = small[:, L_UV:L_UV + 512]
                    pe.wait_ge(s_ad, ab.back(0))
                    for j in range(2):
                        b = ab_bank()
                        for h in range(4 * j, 4 * j + 4):
                            mm = pe.matmul(b[64 * (h % 2):64 * (h % 2) + 64, (h // 2 % 2) * SEQ:(h // 2 % 2 + 1) * SEQ],
                                           uv[:, 64 * h:64 * h + 64], qlat(h), start=True, stop=True,
                                           skip_group_check=True)
                        mm.then_inc(s_ab, 1)

            def seed():
                pe.wait_ge(s_ad, ab.back(0))
                for t in range(TT):
                    for n in range(2):
                        pe.matmul(AB[2 * t + n][:, :], ident, x[:, t, n * 512:(n + 1) * 512], start=True, stop=False,
                                  skip_group_check=True)

            def hidden():
                pe.wait_ge(s_ld, ld.back(0))
                b = tr_bank()
                for k in range(QK):
                    for t in range(TT):
                        mm = pe.transpose(b[:, k * SEQ + t * P:k * SEQ + (t + 1) * P], he[:, t, k * P:(k + 1) * P], ident)
                mm.then_inc(s_tr, 1)

            def group():
                product(hT, KT, "dve")

            def down():
                pe.wait_ge(s_td, tr.back(0))
                for n in range(2):
                    hi, lw = quarter()
                    for t in range(TT):
                        for k in range(QK):
                            for a, w in ((0, hi), (1, hi), (0, lw)):
                                mm = pe.matmul(AB[2 * t + n][:, :], heT[:, a, k, t * P:(t + 1) * P], w[:, k, :],
                                               start=False, stop=True, skip_group_check=True)
                    mm.then_inc(s_used, 1)

            def small_product(c0, n):
                b = ab_bank()
                w = sw[:].rearrange("p a (k n) -> p a k n", k=KT)
                for t in range(TT):
                    for k in range(KT):
                        for i, (a, wa) in enumerate(((0, 0), (1, 0), (0, 1))):
                            mm = pe.matmul(b[:, t * n:(t + 1) * n], hT[:, a, k, t * P:(t + 1) * P], w[:, wa, k, c0:c0 + n],
                                           start=(k == 0 and i == 0), stop=(k == KT - 1 and i == 2), skip_group_check=True)
                mm.then_inc(s_ab, 1)

            def second():
                pe.wait_ge(s_nx, nx.up())
                product(hT, KT, "act", feed=x_cols)
                small_product(0, 16)
                product(hT, KT, "act")
                transposed(lambda t, k: tok[0][:, t, k * P:(k + 1) * P], 4)
                product(hT, KT, "act")
                transposed(lambda t, k: tok[1][:, t, k * P:(k + 1) * P], 4)
                product(hT, KT, "act")
                transposed(lambda t, k: tok[0][:, t, k * P:(k + 1) * P], 4)
                product(hT, KT, "act")
                transposed(lambda t, k: tok[1][:, t, k * P:(k + 1) * P], 4)
                product(hT, KT, "act")
                transposed(lambda t, k: tok[0][:, t, k * P:(k + 1) * P], 4)
                product(hT, KT, "act")
                pe.wait_ge(s_nx, nx.up())
                b = tr_bank()
                for t in range(TT):
                    mm = pe.transpose(b[0:16, t * P:(t + 1) * P], da[:, t, :], ident)
                mm.then_inc(s_tr, 1)
                product(hT, KT, "act")
                pe.wait_ge(s_nx, nx.up())
                b = tr_bank()
                for t in range(TT):
                    mm = pe.matmul(b[:, t * 16:(t + 1) * 16], rows2[:, 1, t * P:(t + 1) * P], ident[0:16, 0:16], start=True,
                                   stop=True, skip_group_check=True)
                mm.then_inc(s_tr, 1)
                pe.wait_ge(s_act, acts.up(3))
                for t in range(TT):
                    for i in range(2):
                        b = tr_bank()
                        for k in range(4):
                            mm = pe.transpose(b[:, k * P:(k + 1) * P], xbcT[i][:, k, t * P:(t + 1) * P], ident)
                        mm.then_inc(s_tr, 1)
                for g in range(2):
                    scores(ab_bank(), 0, xbcT[2][:, g, :], xbcT[2][:, 2 + g, :]).then_inc(s_ab, 1)
                pe.wait_ge(s_td, tr.back(4))
                for h in range(HEADS_A):
                    b = ab_bank()
                    r = slice(64 * (h % 2), 64 * (h % 2) + 64)
                    q, k = qkT2[r, 0, h // 2, :], qkT2[r, 1, h // 2, :]
                    pe.matmul(b[:, 0:P], q[:, 0:P], k[:, 0:P], start=True, stop=True, skip_group_check=True)
                    pe.matmul(b[:, P:WIN], q[:, P:SEQ], k, start=True, stop=True, skip_group_check=True).then_inc(s_ab, 1)

                for g in range(4):
                    for h in range(4 * g, 4 * g + 4):
                        pe.matmul(ab_bank()[:, 0:SEQ], ident[0:16, h:h + 1].to_broadcast([16, P]), rows2[:, 1, :], start=True,
                                  stop=True).then_inc(s_ab, 1)
                    product(hT, KT, "act")
                    b = ab_bank()
                    if g == 0:
                        pe.wait_ge(s_nx, nx.up())
                    for h in range(4 * g, 4 * g + 4):
                        pe.wait_ge(s_pp, pp.up())
                        weighted(b, P * (h % 4), 64, prob[:, h % SLOTS],
                                 lambda s: xdt[:, s, 64 * h:64 * h + 64]).then_inc(s_pv, 1)
                attend(lambda: pe.wait_ge(s_nx, nx.up()), latent=False)
                pe.wait_ge(s_ad, ab.back(0))
                product(mixT[:, 2], 4, "dve")
                product(mixT[:, 2], 4, "dve")
                pe.wait_ge(s_nx, nx.up())
                transposed(lambda t, k: yb[:, t, k * P:(k + 1) * P], KT)
                pe.wait_ge(s_td, tr.back(0))
                product(mixT8, KT, "dve")
                product(mixT8, KT, "dve")
                pe.wait_ge(s_nx, nx.up())
                product(hT, KT, "dve", feed=y_cols)
                product(hT, KT, "dve")
                pe.wait_ge(s_nx, nx.up())
                transposed(x_cols, KT)
                pe.wait_ge(s_td, tr.back(0))
                small_product(16, 20)
                seed()
                product(hT, KT, "dve")
                with repeat(pe, "moe_pe", EXPERTS - 1, counts, per):
                    for _ in range(2):
                        hidden()
                        group()
                        down()
                free.clear()
                hidden()
                group()
                down()
                hidden()
                down()
                pe.wait_ge(s_x, LAYERS + 2)
                pe.wait_ge(s_sm, 16 * (1 + 2 * LAYERS + 2))
                b = tr_bank()
                for k in range(QK):
                    for t in range(TT):
                        mm = pe.transpose(b[:, k * SEQ + t * P:k * SEQ + (t + 1) * P], p_tok[:, t, k * P:(k + 1) * P], ident)
                mm.then_inc(s_tr, 1)
                transposed(lambda t, k: x[:, t, k * P:(k + 1) * P], KT)
                pe.wait_ge(s_td, tr.back(0))
                product(cqT, QK, "act")
                product(cqT, QK, "act")
                product(hT, KT, "act")
                product(hT, KT, "act")

            acts, pp, xr = Count(s_act), Count(s_pp), Count(s_x)
            counts += [acts, xr]
            pe.wait_ge(s_cst, 64)
            for i in range(2 * HEADS_A):
                if i >= 2:
                    pe.wait_ge(s_bd, i - 1)
                pe.matmul(TR[i % 2][:, 0:WIN], relb_sb[:, i // 2, :], onehot_sb[:, i % 2, :], start=True,
                          stop=True).then_inc(s_bf, 1)
            pe.wait_ge(s_bd, 2 * HEADS_A)
            with repeat(pe, "layers_pe", LAYERS, counts, per) as l:
                free.clear()
                layer(l)
            free.clear()
            second()

        @block.scalar
        def _(act):
            hi = Count(s_hi)
            used, lin, tr, ab, raws = Count(s_used), Count(s_lin), Count(s_tr), Count(s_ab), [Count(s) for s in s_raw]
            var, arg, ad, ld, rs, la, smc, pos = (Count(s_var), Count(s_arg), Count(s_ad), Count(s_ld), Count(s_rs), Count(s_la),
                                             Count(s_sm), Count(s_used))
            own = Chain(s_ch_a, act)
            smc.n = -16
            counts = [hi, used, lin, tr, ab, *raws, var, arg, ad, ld, rs, la, smc, pos, own]

            def high():
                if hi.n >= TOTAL_Q:
                    return
                s = hi.n % RING
                act.wait_ge(s_raw[s], raws[s].up(16))
                if hi.n >= RING:
                    act.wait_ge(s_used, used.up())
                hi.n += 1
                act.activation(w_hi[:, s, :], raw[:, s, :], ACT.Copy).then_inc(s_hi, 1)

            def unit(n, read=None, first=None):
                if read is None:
                    for _ in range(n):
                        high()
                    pos.up(n)
                    lin.up()
                    return
                for _ in range(n - 1):
                    high()
                if first:
                    first()
                act.wait_ge(s_lin, lin.up())
                read(0).then_inc(s_la, 1)
                act.wait_ge(s_used, pos.up(n))
                read(1).then_inc(s_la, 1)
                high()

            def roots(n, at=0):
                act.wait_ge(s_var, var.up())
                act.activation(tiny[:, 16:16 + n], tiny[:, at:at + n], ACT.Sqrt).then_inc(s_std, 1)

            def split(dst, nk, gain=None, src=None):
                for k0 in range(0, nk, 2):
                    act.wait_ge(s_tr, tr.up())
                    b = TR[(tr.n - 1) % 2]
                    if gain is None:
                        act.activation(dst[:, 0, k0:k0 + 2, :].rearrange("p k t -> p (k t)"), b[:, :], ACT.Copy).then_inc(s_th, 1)
                    else:
                        for k in range(2):
                            i = act.activation(dst[:, 0, k0 + k, :], b[:, k * SEQ:(k + 1) * SEQ], ACT.Copy,
                                               scale=small[:, gain + k0 + k:gain + k0 + k + 1])
                        i.then_inc(s_th, 1)

            def exp(dst, src, scale=1.0, func=ACT.Exp):
                act.wait_ge(s_arg, arg.up())
                act.activation(dst, src, func, scale=scale).then_inc(s_exp, 1)

            def x_root():
                roots(2)
                act.wait_ge(s_rs, rs.up())

            def inv(t):
                return tiny[:, X_INV + t:X_INV + t + 1]

            def copy(dst, t):
                return act.activation(dst, LIN[t][:, :], ACT.Copy, scale=inv(t))

            def layer(l):
                act.wait_ge(s_sm, smc.up(32))
                split(hT, KT, L_N1)
                unit(4, lambda t: copy(sm[:, t, :], t), first=x_root)
                unit(4, lambda t: copy(mqk_tok[:, t, :], t))
                roots(6)
                unit(4, lambda t: act.activation(mv[:, t, :, 0:P], LIN[t][:, :].rearrange("p (h d) -> p h d", h=4), ACT.Copy,
                                                 scale=inv(t)))
                act.wait_ge(s_arg, arg.up())
                act.activation(qkT.rearrange("p a t -> p (a t)"), conv_out.rearrange("p a t -> p (a t)"), ACT.Silu).then_inc(s_act, 1)
                exp(tn(128, 8), tn(112, 8), -1.0)
                exp(tn(144, 8), tn(136, 8), 1.0, ACT.Ln)
                tr.up(2)
                unit(4, lambda t: copy(rq[:, t, :], t), first=lambda: split(cqT, 2, L_QN))
                tr.up()
                for i in range(2):
                    unit(1, lambda t: act.activation(qT[:, i, 2 * t:2 * t + 2, :].rearrange("p a t -> p (a t)"),
                                                     LIN[t][:, :], ACT.Copy))
                unit(4, lambda t: copy(rk[:, t, :], t))
                tr.up()
                unit(4, lambda t: copy(rv[:, t, :], t))
                tr.up()
                exp(tn(192, 8), tn(184, 8), -1.0)
                unit(4, lambda t: act.activation(mo[:, t, :], LIN[t][:, :], ACT.Sigmoid, scale=inv(t)))
                unit(4, lambda t: act.activation(rg[:, t, :], LIN[t][:, :], ACT.Silu, scale=inv(t)))
                tr.up(4)
                ad.up(8)

                def gate(g, n):
                    unit(4, lambda t: act.activation(gates[:, g, t, n * 512:(n + 1) * 512], LIN[t][:, :], ACT.Sigmoid,
                                                     scale=inv(t)))

                gate(0, 0)
                for h in range(4):
                    act.wait_ge(s_ad, ad.up(1))
                    act.activation(wexp[:, h % SLOTS], wexp[:, h % SLOTS], ACT.Exp).then_inc(s_exp, 1)
                    ad.up(1 if h == 0 else 2)
                ad.up(1)
                gate(0, 1)
                roots(8)
                ad.up(8)
                gate(1, 0)
                roots(8)
                ad.up(4)
                gate(1, 1)
                ad.up(8)
                split(mixT[:, 0], 4, L_MN)
                split(mixT[:, 1], 4, L_RN)
                for i in range(3):
                    unit(2)
                exp(logits[:].rearrange("p h w -> p (h w)"), logits[:].rearrange("p h w -> p (h w)"))
                unit(2)
                act.wait_ge(s_ld, ld.up(4))
                gate(0, 0)
                gate(0, 1)
                ld.up(4)
                attend_latent()
                unit(2)
                unit(2)
                ld.up(4)
                split(hT, KT)
                unit(4)
                unit(4)
                ld.up(4)
                split(hT, KT, L_N2)
                feed_forward("ff_act", FF_GROUPS, l)

            def attend_latent():
                tr.up(HEADS_A)
                ad.up(4)
                ab.up(40)
                for j in range(2):
                    act.wait_ge(s_ab, ab.up())
                    dst = mixT[:, 2, 0, 2 * j:2 * j + 2, :].rearrange("p k t -> p (k t)")
                    act.activation(dst, AB[ad.n % 4][:, :], ACT.Copy).then_inc(s_th, 1)
                    ad.up()

            def glu(first=None):
                for _ in range(3):
                    high()
                if first:
                    first()
                act.wait_ge(s_lin, lin.up())
                act.activation(gbuf[:, 0, :], LIN[0][:, 0:GLU], ACT.Silu, scale=inv(0)).then_inc(s_g, 1)
                act.wait_ge(s_used, pos.up(4))
                act.activation(gbuf[:, 1, :], LIN[1][:, 0:GLU], ACT.Silu, scale=inv(1)).then_inc(s_g, 1)
                high()

            def hidden_high():
                act.wait_ge(s_tr, tr.up())
                act.activation(heT[:, 0].rearrange("p k t -> p (k t)"), TR[(tr.n - 1) % 2][:, :], ACT.Copy).then_inc(s_th, 1)

            def feed_forward(name, groups, l):
                glu(first=x_root)
                act.dma_start(small[:], small_in[l + 1]).then_inc(s_sm, 16)
                act.dma_start(gain1, gains[0]).then_inc(s_sm, 16)
                with repeat(act, name, groups - 1, counts, per):
                    hidden_high()
                    glu()
                    high()
                    high()
                    pos.up(2)
                hidden_high()
                high()
                high()
                pos.up(2)

            def second():
                act.wait_ge(s_sm, smc.up(32))
                act.dma_start(bflat, alibi).then_inc(s_alibi, 16)
                act.activation(sw[:, 0, :], small[:, S_SW:S_END], ACT.Copy).then_inc(s_sw, 1)
                roots(2)
                split(hT, KT, S_N1)

                def by_token(i):
                    return lambda t: copy(tok[i][:, t, :], t)

                def silu_conv(i):
                    act.wait_ge(s_arg, arg.up())
                    v = xbcT[i].rearrange("p a t -> p (a t)")
                    act.activation(v, v, ACT.Silu).then_inc(s_act, 1)

                unit(4, by_token(0), first=x_root)
                exp(tn(464, 32), tn(432, 32), -1.0)
                exp(tn(528, 32), tn(496, 32), 1.0, ACT.Ln)
                act.activation(tiny[:, 720:736], small[:, S_AL:S_AL + 16], ACT.Exp).then_inc(s_exp, 1)
                unit(4, by_token(1))
                silu_conv(0)
                unit(4, by_token(0))
                silu_conv(1)
                unit(4, by_token(1))
                silu_conv(2)
                unit(4, by_token(0))
                unit(4, lambda t: copy(v2[:, t, :], t))
                for n in range(2):
                    unit(4, lambda t: act.activation(xn[:, t, n * 512:(n + 1) * 512], LIN[t][:, :], ACT.Silu, scale=inv(t)))
                tr.up(2 * 5 + 2 + 4)
                ad.up(1 + 2 + HEADS_A)
                lv = logits[:].rearrange("p h w -> p (h w)")
                exp(lv, lv)
                act.dma_start(gain2, gains[1]).then_inc(s_sm, 16)
                act.dma_start(p_tok, p_in.rearrange("(t p) d -> p t d", p=P)).then_inc(s_sm, 16)
                for g in range(4):
                    for h in range(4 * g, 4 * g + 4):
                        act.wait_ge(s_ad, ad.up())
                        act.activation(wexp[:, h % SLOTS], wexp[:, h % SLOTS], ACT.Exp).then_inc(s_ex2, 1)
                    ad.up()
                    unit(4, lambda t: act.activation(gates[:, g // 2, t, (g % 2) * 512:(g % 2 + 1) * 512], LIN[t][:, :],
                                                     ACT.Sigmoid, scale=inv(t)))
                tr.up(HEADS_A)
                for j in range(2):
                    act.wait_ge(s_pv, LAYERS * HEADS_A + SSD_HEADS + 4 * (j + 1))
                    dst = mixT[:, 2, 0, 2 * j:2 * j + 2, :].rearrange("p k t -> p (k t)")
                    act.activation(dst, AB[ad.n % 4][:, :], ACT.Copy).then_inc(s_th, 1)
                    ad.up()
                roots(4)
                unit(2)
                unit(2)
                split(mixT8, KT, S_NS)
                unit(4)
                unit(4)
                split(hT, KT)
                unit(4)
                unit(4)
                split(hT, KT, S_N2)
                x_root()
                ad.up()
                for c in (832, 952):
                    exp(tiny[:, c:c + 8], tiny[:, c:c + 8])
                glu()
                with repeat(act, "moe_act", EXPERTS - 1, counts, per):
                    for _ in range(2):
                        hidden_high()
                        glu()
                        high()
                        high()
                        pos.up(2)
                hidden_high()
                glu()
                high()
                high()
                pos.up(2)
                hidden_high()
                high()
                high()
                pos.up(2)
                split(cqT, QK)
                split(hT, KT)
                for n in range(2):
                    unit(1, lambda t: act.activation(ple[:, t, n * 512:(n + 1) * 512], LIN[t][:, :], ACT.Copy))
                for n in range(2):
                    unit(4, lambda t: act.activation(tmpg2[n][:, t, :], LIN[t][:, :], ACT.Sigmoid))
                roots(2)

            for _ in range(RING):
                high()
            with repeat(act, "layers_act", LAYERS, counts, per) as l:
                layer(l)
            second()

        @block.gpsimd
        def _(pool):
            nc.gpsimd.memset(ones[:], 1.0)
            nc.gpsimd.memset(mv[:, :, :, P:P + 1], 1.0).then_inc(s_z, 1)
            with pool.Fori(0, TOTAL_Q // RING) as r:
                for i in range(RING):
                    pool.wait_ge(s_hi, r * RING + (i + 1))
                    nc.gpsimd.tensor_tensor(w_lo[:, i, :], raw[:, i, :], w_hi[:, i, :].bitcast(F32),
                                            ALU.subtract).then_inc(s_lo, 1)

        @block.vector
        def _(dve):
            lin, pos, tr, th, ab, ad, std, exps, la, ld, g, pv, td, xr, bdd = (
                Count(s_lin), Count(s_used), Count(s_tr), Count(s_th), Count(s_ab), Count(s_ad), Count(s_std),
                Count(s_exp), Count(s_la), Count(s_ld), Count(s_g), Count(s_pv), Count(s_td), Count(s_x), Count(s_bd))
            smc, rs = Count(s_sm), Count(s_rs)
            own = Chain(s_ch_d, dve)
            smc.n = -16
            counts = [lin, pos, tr, th, ab, ad, std, exps, la, ld, g, pv, smc, rs, own]

            def unit(n, read=None):
                v = lin.up()
                if read is None:
                    pos.up(n)
                    return
                dve.wait_ge(s_lin, v)
                read(0)
                dve.wait_ge(s_used, pos.up(n))
                read(1)

            def col(at, i=0):
                return small[:, at + i:at + i + 1]

            def tc(at, i=0):
                return tiny[:, at + i:at + i + 1]

            def squares(v, junk, n, i):
                return dve.tensor_tensor_reduce(junk, v, v, 1.0 / n, 0.0, ALU.mult, ALU.add, tc(0, i))

            def rstd(n, to=32):
                v, s, r, t = (tiny[:, a:a + n] for a in (0, 16, 32, 48))
                dve.tensor_scalar(v, v, EPS, None, ALU.add).then_inc(s_var, 1)
                dve.wait_ge(s_std, std.up())
                own(dve.reciprocal(r, s))
                own(dve.tensor_tensor(t, r, r, ALU.mult))
                own(dve.tensor_tensor(t, t, v, ALU.mult))
                own(dve.tensor_scalar(t, t, -0.5, 1.5, ALU.mult, ALU.add))
                last = dve.tensor_tensor(tiny[:, to:to + n], r, t, ALU.mult)
                if to == 32:
                    own(last)
                return last

            def x_stats():
                for t in range(TT):
                    i = squares(x[:, t, :], xn[:, t, :], D, t)
                own(i)
                rstd(2, X_INV).then_inc(s_rs, 1)
                dve.wait_ge(s_rs, rs.up())

            def split(dst, nk, gain=None):
                for k0 in range(0, nk, 2):
                    dve.wait_ge(s_th, th.up())
                    tr.up()
                    b = TR[(tr.n - 1) % 2]
                    for k in range(2):
                        hi = dst[:, 0, k0 + k, :].bitcast(F32)
                        bk = b[:, k * SEQ:(k + 1) * SEQ]
                        if gain is None:
                            i = dve.tensor_tensor(dst[:, 1, k0 + k, :], bk, hi, ALU.subtract)
                        else:
                            i = dve.scalar_tensor_tensor(dst[:, 1, k0 + k, :], bk, col(gain, k0 + k), hi, ALU.mult, ALU.subtract)
                    i.then_inc(s_td, 1)

            def tr_bank():
                dve.wait_ge(s_tr, tr.up())
                return TR[(tr.n - 1) % 2]

            def ab_bank():
                ad.up()
                dve.wait_ge(s_ab, ab.up())
                return AB[(ad.n - 1) % 4]

            def log1p_exp_minus(f, n, exp_at):
                a, e, w, ln, d, z = (tiny[:, k:k + n] for k in exp_at)
                dve.scalar_tensor_tensor(a, f, -1.0, f, ALU.mult, ALU.max).then_inc(s_arg, 1)
                dve.wait_ge(s_exp, exps.up())
                dve.tensor_scalar(w, e, 1.0, None, ALU.add).then_inc(s_arg, 1)
                dve.wait_ge(s_exp, exps.up())
                own(dve.tensor_scalar(d, w, -1.0, None, ALU.add))
                own(dve.tensor_scalar(z, d, 0.0, None, ALU.is_equal))
                own(dve.tensor_tensor(d, d, z, ALU.add))
                own(dve.reciprocal(d, d))
                own(dve.tensor_tensor(ln, ln, e, ALU.mult))
                own(dve.tensor_tensor(ln, ln, d, ALU.mult))
                own(dve.tensor_tensor(z, z, e, ALU.mult))
                own(dve.tensor_tensor(ln, ln, z, ALU.add))

            def small_norms():
                dve.wait_ge(s_la, la.up(2))
                own(dve.tensor_copy(g16, sm[:, :, 320:336]))
                dve.tensor_scalar(g16[:, :, 0:8], g16[:, :, 0:8], 8 ** -0.5 * 64 ** -0.5, None, ALU.mult)
                for t in range(TT):
                    squares(sm[:, t, 0:256], xflat[:, 512 * t:512 * t + 256], 256, t)
                    squares(sm[:, t, 384:512], xflat[:, 512 * t + 256:512 * t + 384], P, 2 + t)
                own(dve.tensor_reduce(tiny[:, 52:54], sm[:, :, 256:320], AX.X, ALU.add))
                own(dve.tensor_scalar(tiny[:, 52:54], tiny[:, 52:54], 1.0 / 64, None, ALU.mult))
                for t in range(TT):
                    i = dve.tensor_scalar(sm[:, t, 256:320], sm[:, t, 256:320], tc(52, t), None, ALU.subtract)
                own(i)
                for t in range(TT):
                    i = squares(sm[:, t, 256:320], xflat[:, 64 * t:64 * t + 64], 64, 4 + t)
                own(i)
                rstd(6)
                for t in range(TT):
                    dve.tensor_scalar(sm[:, t, 0:256], sm[:, t, 0:256], tc(32, t), None, ALU.mult)
                    dve.scalar_tensor_tensor(sm[:, t, 384:512], sm[:, t, 384:512], tc(34, t), small[:, L_KV:L_KV + P],
                                             ALU.mult, ALU.mult)
                    dve.tensor_scalar(sm[:, t, 320:384], sm[:, t, 256:320], tc(36, t), None, ALU.mult)
                    i = dve.tensor_scalar(sm[:, t, 256:320], sm[:, t, 256:320], tc(36, t), None, ALU.mult)
                i.then_inc(s_nx, 1)

            def small_by_feature():
                split(cqT, 2, L_QN)
                b = tr_bank()
                dve.tensor_scalar(kidxT, b[:, 0:SEQ], col(L_KI), None, ALU.mult)
                dve.tensor_copy(ckvT, b[:, SEQ:2 * SEQ]).then_inc(s_td, 1)

            def gate_logs():
                ib = small[:, L_IB:L_IB + 8].rearrange("p (g h) -> p g h", g=2)
                fx = tn(120, TT, 4)
                dve.tensor_tensor(gif[:, :, 0:4], g16[:, :, 8:12], ib[:, 0:1, :].broadcast_to([P, TT, 4]), ALU.add)
                own(dve.tensor_tensor(fx, g16[:, :, 12:16], ib[:, 1:2, :].broadcast_to([P, TT, 4]), ALU.add))
                log1p_exp_minus(tiny[:, 120:128], 8, (112, 128, 136, 144, 152, 160))
                own(dve.tensor_scalar(fx, fx, 0.0, None, ALU.min))
                dve.tensor_tensor(gif[:, :, 4:8], fx, tn(144, TT, 4), ALU.subtract).then_inc(s_nx, 1)

            def conv(dst, src, tiles, taps, bias_at=None, f0=0):
                for j in range(4):
                    for f in range(tiles):
                        s, w = src[:, f, j:j + SEQ], col(taps, 4 * (f0 + f) + j)
                        if j == 0:
                            i = dve.tensor_scalar(dst[:, f, :], s, w, None if bias_at is None else col(bias_at, f0 + f),
                                                  ALU.mult, ALU.bypass if bias_at is None else ALU.add)
                        else:
                            i = dve.scalar_tensor_tensor(dst[:, f, :], s, w, dst[:, f, :], ALU.mult, ALU.add)
                    if j < 3:
                        own(i)
                i.then_inc(s_arg, 1)

            def gate_rows():
                dve.wait_ge(s_b, 32)
                b = tr_bank()
                dve.tensor_copy(rows[:, 0:2, :].rearrange("p a b -> p (a b)"), b[0:4, :]).then_inc(s_td, 1)
                dve.wait_ge(s_td, tr.back(0))
                own(dve.tensor_tensor_scan(rows[:, 4, :], ones[0:4, :], rows[:, 1, :], 0.0, ALU.mult, ALU.add))
                own(dve.tensor_tensor(rows[:, 0, :], rows[:, 0, :], rows[:, 4, :], ALU.subtract))
                own(dve.tensor_tensor_scan(rows[:, 1, :], ones[0:4, :], rows[:, 0, :], 0.0, ALU.mult, ALU.max))
                dve.tensor_scalar(rows[:, 2, :], rows[:, 1, :], -1.0, None, ALU.mult)
                dve.tensor_tensor(rows[:, 3, :], rows[:, 1, :], rows[:, 4, :], ALU.add).then_inc(s_nx, 1)

            def index_scores():
                for h in range(8):
                    b = ab_bank()
                    dst = work if h == 0 else relu_w
                    dve.tensor_scalar(dst[:, 0:P], b[:, 0:P], 0.0, g16[:, 0, h:h + 1], ALU.max, ALU.mult)
                    dve.tensor_scalar(dst[:, P:WIN], b[:, P:WIN], 0.0, g16[:, 1, h:h + 1], ALU.max, ALU.mult).then_inc(s_ad, 1)
                    dve.wait_ge(s_ad, ad.back(0))
                    if h:
                        own(dve.tensor_tensor(work, work, relu_w, ALU.add))
                dve.tensor_tensor(work[:, 0:P], work[:, 0:P], qmask, ALU.add)
                own(dve.tensor_tensor(work[:, SEQ:WIN], work[:, SEQ:WIN], qmask, ALU.add))

            def take(n):
                for _ in range(n):
                    for i, c in ((0, slice(0, P)), (1, slice(P, WIN))):
                        if i == 0:
                            dve.memset(tc(1001), 0.0)
                        j = dve.max(lflat[:, 2 * WIN + 8 * i:2 * WIN + 8 * i + 8], work[:, c])
                    own(j)
                    for i, c in ((0, slice(0, P)), (1, slice(P, WIN))):
                        if i == 0:
                            dve.memset(tc(1002), 0.0)
                        j = dve.match_replace(work[:, c], lflat[:, 2 * WIN + 8 * i:2 * WIN + 8 * i + 8], work[:, c], TAKEN)
                    own(j)

            def rotate(*which):
                cos4 = cosv.unsqueeze(2).broadcast_to([P, TT, 4, 64])
                sin4 = sinv.unsqueeze(2).broadcast_to([P, TT, 4, 64])
                for src, at, copied in which:
                    dve.wait_ge(s_la, la.up(copied))
                    x1, x2 = heads(src)[:, :, :, 0:64], heads(src)[:, :, :, 64:128]
                    t1, t2 = (xflat[:, a:a + 512].rearrange("p (t h d) -> p t h d", t=TT, h=4) for a in (at, at + 512))
                    dve.tensor_tensor(t1, x2, sin4, ALU.mult)
                    own(dve.tensor_tensor(t2, x1, sin4, ALU.mult))
                    dve.tensor_tensor(x1, x1, cos4, ALU.mult)
                    own(dve.tensor_tensor(x2, x2, cos4, ALU.mult))
                    dve.tensor_tensor(x1, x1, t1, ALU.subtract)
                    dve.tensor_tensor(x2, x2, t2, ALU.add).then_inc(s_rot, 1)

            def taken():
                own(dve.tensor_scalar(keep, work, TAKEN / 2, -BIG, ALU.is_gt, ALU.mult))
                dve.tensor_tensor(keep[:, 0:P], keep[:, 0:P], qmask, ALU.add)
                own(dve.tensor_tensor(keep[:, SEQ:WIN], keep[:, SEQ:WIN], qmask, ALU.add))

            def mlstm():
                def args(h):
                    b = ab_bank()
                    dve.scalar_tensor_tensor(wexp[:, h % SLOTS, 0:SEQ], b[:, 0:SEQ], acol[:, 0, h:h + 1], mask, ALU.add, ALU.add)
                    dve.scalar_tensor_tensor(wexp[:, h % SLOTS, SEQ:WIN], b[:, P:SEQ], acol[:, 1, h:h + 1], mask[:, 0:P],
                                             ALU.add, ALU.add).then_inc(s_ad, 1)
                    b = ab_bank()
                    dve.wait_ge(s_exp, exps.up())
                    dve.scalar_tensor_tensor(prob[:, h % SLOTS], b[:, 0:WIN], 64 ** -0.5, wexp[:, h % SLOTS], ALU.mult,
                                             ALU.mult).then_inc(s_ad, 1)

                args(0)
                for h in range(4):
                    if h < 3:
                        args(h + 1)
                    b = ab_bank()
                    dve.tensor_copy(m_out[:, :, h, :], b[:, 0:258].rearrange("p (t v) -> p t v", t=TT)).then_inc(s_ad, 1)

            def retain():
                def decayed(h):
                    b = ab_bank()
                    dve.tensor_tensor(prob[:, h % SLOTS, 0:SEQ], b[:, 0:SEQ], ret_decay[:, h, :], ALU.mult)
                    dve.tensor_tensor(prob[:, h % SLOTS, SEQ:WIN], b[:, SEQ:WIN], ret_decay[:, h, 0:P], ALU.mult).then_inc(s_ad, 1)

                decayed(0)
                for h in range(4):
                    if h < 3:
                        decayed(h + 1)
                    b = ab_bank()
                    dve.tensor_copy(r_out[:, :, h * P:(h + 1) * P], b[:, 0:SEQ].rearrange("p (t v) -> p t v", t=TT)).then_inc(s_ad, 1)

            def spread(v):
                return v.unsqueeze(3).broadcast_to([P, TT, 4, P])

            def head_norm(o, gate):
                sq = xflat[:, 0:1024].rearrange("p (t h d) -> p t h d", t=TT, h=4)
                mean, var, r = tn(56, TT, 4), tn(0, TT, 4), tn(32, TT, 4)
                own(dve.tensor_reduce(mean, o, AX.X, ALU.add))
                own(dve.tensor_scalar(mean, mean, 1.0 / P, None, ALU.mult))
                own(dve.tensor_tensor(o, o, spread(mean), ALU.subtract))
                own(dve.tensor_tensor(sq, o, o, ALU.mult))
                own(dve.tensor_reduce(var, sq, AX.X, ALU.add))
                own(dve.tensor_scalar(var, var, 1.0 / P, None, ALU.mult))
                rstd(8)
                own(dve.tensor_tensor(o, o, spread(r), ALU.mult))
                dve.tensor_tensor(o, o, heads(gate), ALU.mult).then_inc(s_nx, 1)

            row = tiny[:, 208:224].rearrange("p (t h) -> p t h", t=TT)
            score_parts = ((0, logits[:, :, 0:P], P), (1, logits[:, :, P:WIN], SEQ))

            def row_stat(op):
                for t, v, n in score_parts:
                    i = dve.tensor_reduce(row[:, t, :], v, AX.X, op)
                own(i)

            def less_maximum():
                for t, v, n in score_parts:
                    i = dve.tensor_tensor(v, v, row[:, t, :].unsqueeze(2).broadcast_to([P, HEADS_A, n]), ALU.subtract)
                i.then_inc(s_arg, 1)

            def over_sum():
                own(dve.reciprocal(tiny[:, 208:224], tiny[:, 208:224]))
                for t, v, n in score_parts:
                    i = dve.tensor_tensor(v, v, row[:, t, :].unsqueeze(2).broadcast_to([P, HEADS_A, n]), ALU.mult)
                i.then_inc(s_nx, 1)

            def by_key(h):
                b = tr_bank()
                v = pv.up()
                if h >= SLOTS:
                    dve.wait_ge(s_pv, pv.back(SLOTS))
                dve.tensor_copy(prob[:, h % SLOTS], b[:, 0:WIN]).then_inc(s_td, 1)

            def attend_latent():
                def latent(j):
                    dve.wait_ge(s_pv, pv.back(HEADS_A - 2 - 2 * j if j == 3 else 1))
                    ad.up()
                    dve.tensor_copy(two_heads(j), AB[(ad.n - 1) % 4][:, :]).then_inc(s_ad, 1)

                by_key(0)
                by_key(1)
                for j in range(4):
                    if j < 3:
                        by_key(2 * j + 2)
                        latent(j)
                        by_key(2 * j + 3)
                    else:
                        latent(j)
                for j in range(2):
                    dve.wait_ge(s_th, th.up())
                    ab.up()
                    ad.up()
                    dst = mixT[:, 2, 1, 2 * j:2 * j + 2, :].rearrange("p k t -> p (k t)")
                    hi = mixT[:, 2, 0, 2 * j:2 * j + 2, :].rearrange("p k t -> p (k t)").bitcast(F32)
                    dve.tensor_tensor(dst, AB[(ad.n - 1) % 4][:, :], hi, ALU.subtract).then_inc(s_ad, 1)

            def two_heads(j):
                return (qlatA if j < 2 else qlatB)[:, 2 * (j % 2):2 * (j % 2) + 2, :].rearrange("p a t -> p (a t)")

            def branch(g, n, first=False, last=False):
                def read(t):
                    y, gt = xn[:, t, n * 512:(n + 1) * 512], gates[:, g, t, n * 512:(n + 1) * 512]
                    if first:
                        dve.tensor_tensor(y, LIN[t][:, :], gt, ALU.mult).then_inc(s_ld, 1)
                        ld.up()
                        return
                    dve.tensor_tensor(tmpy[:, t, :], LIN[t][:, :], gt, ALU.mult).then_inc(s_ld, 1)
                    dve.wait_ge(s_ld, ld.up())
                    i = dve.tensor_tensor(y, y, tmpy[:, t, :], ALU.add)
                    if last and t == 1:
                        i.then_inc(s_nx, 1)
                return read

            def residual(n):
                def read(t):
                    v = x[:, t, n * 512:(n + 1) * 512]
                    dve.tensor_tensor(v, LIN[t][:, :], v, ALU.add).then_inc(s_ld, 1)
                    dve.wait_ge(s_ld, ld.up())
                    if n == 1 and t == 1:
                        dve.memset(tc(1003), 0.0).then_inc(s_nx, 1)
                return read

            def glu(scale=None):
                lin.up()
                for t in range(TT):
                    dve.wait_ge(s_g, g.up())
                    if t == 1:
                        pos.up(4)
                    ld.up()
                    i = dve.scalar_tensor_tensor(he[:, t, :], LIN[t][:, GLU:2 * GLU], scale(t) if scale else tc(X_INV, t),
                                                 gbuf[:, t, :], ALU.mult, ALU.mult)
                    i.then_inc(s_ld, 1)

            def hidden_low():
                dve.wait_ge(s_th, th.up())
                tr.up()
                b = TR[(tr.n - 1) % 2]
                dve.tensor_tensor(heT[:, 1].rearrange("p k t -> p (k t)"), b[:, :],
                                  heT[:, 0].rearrange("p k t -> p (k t)").bitcast(F32), ALU.subtract).then_inc(s_td, 1)

            def feed_forward(name, groups):
                glu()
                with repeat(dve, name, groups - 1, counts, per):
                    hidden_low()
                    glu()
                    pos.up(2)
                hidden_low()
                dve.wait_ge(s_used, pos.up(2))
                for t in range(TT):
                    for n in range(2):
                        ad_done = dve.tensor_copy(x[:, t, n * 512:(n + 1) * 512], AB[2 * t + n][:, :])
                ad_done.then_inc(s_x, 1)
                dve.wait_ge(s_x, xr.up())

            def layer(l):
                dve.wait_ge(s_sm, smc.up(32))
                split(hT, KT, L_N1)
                x_stats()
                small_norms()
                dve.wait_ge(s_la, la.up(2))
                own(dve.memset(conv_in[:, :, 0:3], 0.0))
                for j in range(2):
                    b = tr_bank()
                    dve.tensor_copy(conv_in[:, 2 * j:2 * j + 2, 3:SEQ + 3],
                                    b[:, :].rearrange("p (a t) -> p a t", a=2)).then_inc(s_td, 1)
                dve.wait_ge(s_td, tr.back(0))
                conv(conv_out, conv_in, 4, L_CW)
                gate_logs()
                small_by_feature()
                for n in (4, 4, 4, 4, 1, 1, 4, 4, 4, 4, 4, 4, 4, 4):
                    unit(n)
                gate_rows()
                rotate((rq, 0, 4))
                index_scores()
                rotate((rk, 1024, 6))
                b = tr_bank()
                dve.tensor_copy(tiny[:, 184:192], b[:, 8:16]).then_inc(s_arg, 1)
                dve.tensor_copy(tiny[:, 176:184], b[:, 0:8]).then_inc(s_td, 1)
                dve.wait_ge(s_td, tr.back(0))
                exps.up()
                take(8)
                taken()
                for dst in (rqT[:, 0], rqT[:, 1]):
                    for j in range(2):
                        b = tr_bank()
                        dve.tensor_copy(dst[:, 2 * j:2 * j + 2, :].rearrange("p a t -> p (a t)"), b[:, :]).then_inc(s_td, 1)
                mlstm()
                dve.wait_ge(s_ad, ad.back(0))
                total = m_out[:, :, :, P:P + 1].rearrange("p t h a -> p t (h a)")
                own(dve.scalar_tensor_tensor(den, total, -1.0, total, ALU.mult, ALU.max))
                own(dve.tensor_tensor(den, den, em, ALU.max))
                own(dve.reciprocal(den, den))
                own(dve.tensor_tensor(m_out[:, :, :, 0:P], m_out[:, :, :, 0:P], spread(den), ALU.mult))
                dve.wait_ge(s_la, la.up(4))
                head_norm(m_out[:, :, :, 0:P], mo)
                retain()
                dve.wait_ge(s_ad, ad.back(0))
                dve.wait_ge(s_la, la.up(2))
                head_norm(heads(r_out), rg)
                for j in range(4):
                    b = ab_bank()
                    dst = (qlatA if j < 2 else qlatB)[:, j % 2:4:2, :]
                    dve.tensor_scalar(dst, b[:, :].rearrange("p (a t) -> p a t", a=2), 64 ** -0.5, None, ALU.mult).then_inc(s_ad, 1)
                dve.wait_ge(s_b, 64)
                for h in range(HEADS_A):
                    b = ab_bank()
                    i = dve.tensor_tensor(logits[:, h, :], b[:, 0:WIN], bias[:, h, :], ALU.add)
                    i.then_inc(s_ad, 1)
                dve.wait_ge(s_ad, ad.back(0))
                split(mixT[:, 0], 4, L_MN)
                split(mixT[:, 1], 4, L_RN)
                dve.wait_ge(s_la, la.up(8))
                own(dve.tensor_tensor(logits[:], logits[:], keep.unsqueeze(1).broadcast_to([P, HEADS_A, WIN]), ALU.add))
                unit(2, branch(0, 0, first=True))
                row_stat(ALU.max)
                unit(2, branch(0, 1, first=True))
                less_maximum()
                unit(2, branch(1, 0))
                dve.wait_ge(s_exp, exps.up())
                row_stat(ALU.add)
                unit(2, branch(1, 1))
                over_sum()
                unit(4)
                unit(4)
                attend_latent()
                dve.wait_ge(s_la, la.up(4))
                unit(2, branch(0, 0))
                unit(2, branch(0, 1, last=True))
                split(hT, KT)
                unit(4, residual(0))
                unit(4, residual(1))
                split(hT, KT, L_N2)
                x_stats()
                feed_forward("ff_dve", FF_GROUPS)

            def first_of(v, out, at):
                m = tn(at, TT, 1)
                own(dve.tensor_reduce(m, v, AX.X, ALU.max))
                own(dve.tensor_tensor(out, v, m.broadcast_to([P, TT, 4]), ALU.is_equal))
                own(dve.tensor_tensor(out, out, tn(772, 1, 4).broadcast_to([P, TT, 4]), ALU.mult))
                own(dve.tensor_reduce(tn(776, TT, 1), out, AX.X, ALU.max))
                own(dve.tensor_tensor(out, out, tn(776, TT, 1).broadcast_to([P, TT, 4]), ALU.is_equal))

            def route():
                for i in range(4):
                    own(dve.memset(tiny[:, 772 + i:773 + i], 4.0 - i))
                lg = tn(780, TT, 20)
                b = ab_bank()
                for t in range(TT):
                    i = dve.scalar_tensor_tensor(lg[:, t, :], b[:, 20 * t:20 * t + 20], tc(X_INV, t),
                                                 small[:, S_BR:S_BR + 20], ALU.mult, ALU.add)
                i.then_inc(s_ad, 1)
                dve.wait_ge(s_ad, ad.back(0))
                four = [P, TT, 4]
                gp, og, ei, o1, e2, o2, cig = (tn(832 + 8 * i, TT, 4) for i in range(7))
                pw, m1, m2, ex, w1, w2 = (tn(900 + 2 * i, TT, 1) for i in range(6))
                own(dve.tensor_reduce(m1, lg[:, :, 0:4], AX.X, ALU.max))
                dve.tensor_tensor(gp, lg[:, :, 0:4], m1.broadcast_to(four), ALU.subtract).then_inc(s_arg, 1)
                dve.wait_ge(s_exp, exps.up())
                own(dve.tensor_reduce(m1, gp, AX.X, ALU.add))
                own(dve.reciprocal(m1, m1))
                own(dve.tensor_tensor(gp, gp, m1.broadcast_to(four), ALU.mult))
                first_of(gp, og, 900)
                m = tn(920, TT, 16).rearrange("p t (g j) -> p t g j", g=4)
                own(dve.tensor_tensor(m, lg[:, :, 4:20].rearrange("p t (g j) -> p t g j", g=4),
                                      og.unsqueeze(3).broadcast_to([P, TT, 4, 4]), ALU.mult))
                own(dve.tensor_reduce(ei, m.rearrange("p t g j -> p t j g"), AX.X, ALU.add))
                first_of(ei, o1, 902)
                own(dve.scalar_tensor_tensor(e2, o1, -BIG, ei, ALU.mult, ALU.add))
                first_of(e2, o2, 904)
                own(dve.memset(tiny[:, 952:960], 0.0))
                dve.tensor_tensor(tn(952, TT, 4), m2.broadcast_to(four), m1.broadcast_to(four), ALU.subtract).then_inc(s_arg, 1)
                dve.wait_ge(s_exp, exps.up())
                ex = tn(952, TT, 4)[:, :, 0:1]
                own(dve.tensor_scalar(w1, ex, 1.0, None, ALU.add))
                own(dve.reciprocal(w1, w1))
                own(dve.tensor_tensor(w1, w1, pw, ALU.mult))
                own(dve.tensor_tensor(w2, w1, ex, ALU.mult))
                own(dve.tensor_tensor(o1, o1, w1.broadcast_to(four), ALU.mult))
                own(dve.tensor_tensor(o2, o2, w2.broadcast_to(four), ALU.mult))
                own(dve.tensor_tensor(cig, o1, o2, ALU.add))
                for t in range(TT):
                    i = dve.tensor_scalar(cig[:, t, :], cig[:, t, :], tc(X_INV, t), None, ALU.mult)
                own(i)
                own(dve.tensor_tensor(comb.rearrange("p t (g j) -> p t g j", g=4), og.unsqueeze(3).broadcast_to([P, TT, 4, 4]),
                                      cig.unsqueeze(2).broadcast_to([P, TT, 4, 4]), ALU.mult))

            def norm_rows(gain, dst):
                for t in range(TT):
                    i = squares(x[:, t, :], xn[:, t, :], D, t)
                own(i)
                rstd(2)
                for t in range(TT):
                    i = dve.scalar_tensor_tensor(dst[:, t, :], x[:, t, :], tc(32, t), gain, ALU.mult, ALU.mult)
                return i

            def second():
                dve.wait_ge(s_sm, smc.up(32))
                dve.wait_ge(s_sw, 1)
                dve.tensor_tensor(sw[:, 1, :], small[:, S_SW:S_END], sw[:, 0, :].bitcast(F32), ALU.subtract)
                dve.memset(conv2[:, :, 0:3], 0.0)
                norm_rows(gain1, x).then_inc(s_nx, 1)
                split(hT, KT, S_N1)
                x_stats()
                unit(4)
                b = ab_bank()
                f = tn(400, TT, 16)
                for t in range(TT):
                    i = dve.scalar_tensor_tensor(f[:, t, :], b[:, 16 * t:16 * t + 16], tc(X_INV, t),
                                                 small[:, S_DTB:S_DTB + 16], ALU.mult, ALU.add)
                i.then_inc(s_ad, 1)
                dve.wait_ge(s_ad, ad.back(0))
                log1p_exp_minus(tiny[:, 400:432], 32, (432, 464, 496, 528, 560, 592))
                own(dve.tensor_scalar(f, f, 0.0, None, ALU.max))
                own(dve.tensor_tensor(dt, f, tn(528, TT, 16), ALU.add))
                dve.wait_ge(s_exp, exps.up())
                own(dve.tensor_scalar(tiny[:, 720:736], tiny[:, 720:736], -1.0, None, ALU.mult))
                dve.tensor_tensor(da, dt, tiny[:, 720:736].unsqueeze(1).broadcast_to([P, TT, 16]), ALU.mult).then_inc(s_nx, 1)

                def conv_chunk(c):
                    for j in range(2):
                        b = tr_bank()
                        dve.tensor_copy(conv2[:, 2 * j:2 * j + 2, 3:SEQ + 3],
                                        b[:, :].rearrange("p (a t) -> p a t", a=2)).then_inc(s_td, 1)
                    dve.wait_ge(s_td, tr.back(0))
                    conv(xbcT[c], conv2, 4, S_CW, S_CB, 4 * c)

                unit(4)
                conv_chunk(0)
                unit(4)
                conv_chunk(1)
                unit(4)
                conv_chunk(2)
                for i in range(2):
                    unit(4)
                    for j in range(2):
                        b = tr_bank()
                        dve.tensor_copy(qkT2[:, i, 2 * j:2 * j + 2, :].rearrange("p a t -> p (a t)"), b[:, :]).then_inc(s_td, 1)
                unit(4)
                b = tr_bank()
                dve.tensor_copy(rows2[:, 0, :], b[0:16, 0:SEQ]).then_inc(s_td, 1)
                dve.wait_ge(s_td, tr.back(0))
                dve.tensor_tensor_scan(rows2[:, 1, :], ones[:], rows2[:, 0, :], 0.0, ALU.mult, ALU.add).then_inc(s_nx, 1)
                unit(4)
                b = tr_bank()
                dve.tensor_copy(cs, b[:, 0:32].rearrange("p (t n) -> p t n", t=TT)).then_inc(s_td, 1)
                for t in range(TT):
                    for i in range(2):
                        b = tr_bank()
                        dve.tensor_copy(xs[:, t, i * 512:(i + 1) * 512], b[:, :]).then_inc(s_td, 1)
                for g in range(2):
                    b = ab_bank()
                    dve.tensor_copy(cb[:, g, :], b[:, 0:WIN]).then_inc(s_ad, 1)
                dve.wait_ge(s_alibi, 16)
                for h in range(HEADS_A):
                    b = ab_bank()
                    dve.scalar_tensor_tensor(logits[:, h, :], b[:, 0:WIN], 64 ** -0.5, bias[:, h, :], ALU.mult,
                                             ALU.add).then_inc(s_ad, 1)
                dve.wait_ge(s_ad, ad.back(0))
                row_stat(ALU.max)
                less_maximum()

                def by_head(v):
                    return v.rearrange("p t (h d) -> p t h d", h=SSD_HEADS)

                def over(v):
                    return v.unsqueeze(3).broadcast_to([P, TT, SSD_HEADS, 64])

                for g in range(4):
                    for h in range(4 * g, 4 * g + 4):
                        b = ab_bank()
                        if h >= SLOTS:
                            dve.wait_ge(s_pp, h - SLOTS + 1)
                        dve.scalar_tensor_tensor(wexp[:, h % SLOTS, 0:SEQ], b[:, 0:SEQ], cs[:, 0, h:h + 1], mask,
                                                 ALU.subtract, ALU.add)
                        dve.scalar_tensor_tensor(wexp[:, h % SLOTS, SEQ:WIN], b[:, P:SEQ], cs[:, 1, h:h + 1], mask[:, 0:P],
                                                 ALU.subtract, ALU.add).then_inc(s_ad, 1)
                    if g == 0:
                        skip = small[:, S_DS:S_DS + 16].unsqueeze(1).broadcast_to([P, TT, 16])
                        dve.tensor_tensor(by_head(yb), by_head(xs), over(skip), ALU.mult)
                        dve.tensor_tensor(by_head(xdt), by_head(xs), over(dt), ALU.mult).then_inc(s_nx, 1)
                    for h in range(4 * g, 4 * g + 4):
                        dve.wait_ge(s_ex2, h + 1)
                        dve.tensor_tensor(prob[:, h % SLOTS], wexp[:, h % SLOTS], cb[:, h // 8, :], ALU.mult).then_inc(s_pp, 1)
                    unit(4)
                    pv.up(4)
                    dve.wait_ge(s_pv, pv.back(0))
                    ad.up()
                    yv = by_head(yb)[:, :, 4 * g:4 * g + 4, :]
                    src = AB[(ad.n - 1) % 4][:, :].rearrange("p (h t d) -> p t h d", h=4, t=TT)
                    dve.tensor_tensor(yv, src, yv, ALU.add).then_inc(s_ad, 1)
                dve.wait_ge(s_exp, exps.up())
                row_stat(ALU.add)
                over_sum()
                for h in range(HEADS_A):
                    by_key(h)
                for j in range(2):
                    dve.wait_ge(s_th, th.up())
                    ad.up()
                    dst = mixT[:, 2, 1, 2 * j:2 * j + 2, :].rearrange("p k t -> p (k t)")
                    hi = mixT[:, 2, 0, 2 * j:2 * j + 2, :].rearrange("p k t -> p (k t)").bitcast(F32)
                    dve.tensor_tensor(dst, AB[(ad.n - 1) % 4][:, :], hi, ALU.subtract).then_inc(s_ad, 1)
                dve.wait_ge(s_la, la.up(2 * 8))
                own(dve.tensor_tensor(yb, yb, xn[:], ALU.mult))
                for t in range(TT):
                    for g in range(2):
                        i = squares(yb[:, t, g * 512:(g + 1) * 512], xdt[:, t, g * 512:(g + 1) * 512], 512, 2 * t + g)
                own(i)
                rstd(4)
                for t in range(TT):
                    for g in range(2):
                        v = yb[:, t, g * 512:(g + 1) * 512]
                        i = dve.tensor_scalar(v, v, tc(32, 2 * t + g), None, ALU.mult)
                i.then_inc(s_nx, 1)
                dve.wait_ge(s_la, la.up(2 * 4))
                unit(2, branch(0, 0, first=True))
                unit(2, branch(0, 1, first=True))
                split(mixT8, KT, S_NS)
                unit(4, branch(1, 0))
                unit(4, branch(1, 1, last=True))
                split(hT, KT)
                unit(4, residual(0))
                unit(4, residual(1))
                split(hT, KT, S_N2)
                x_stats()
                route()
                glu(lambda t: comb[:, t, 0:1])
                with repeat(dve, "moe_dve", EXPERTS - 1, counts, per) as e:
                    for i in range(2):
                        hidden_low()
                        glu(lambda t: comb[:, t, bass.ds(e + i, 1)])
                        pos.up(2)
                hidden_low()
                glu(lambda t: comb[:, t, EXPERTS - 1:EXPERTS])
                pos.up(2)
                hidden_low()
                dve.wait_ge(s_used, pos.up(2))
                for t in range(TT):
                    for n in range(2):
                        i = dve.tensor_copy(x[:, t, n * 512:(n + 1) * 512], AB[2 * t + n][:, :])
                i.then_inc(s_x, 1)
                dve.wait_ge(s_x, xr.up())
                split(cqT, QK)
                split(hT, KT)
                unit(1)
                unit(1)
                for n in range(2):
                    unit(4)
                    dve.wait_ge(s_la, la.up(6 if n == 0 else 2))
                    pl = ple[:, :, n * 512:(n + 1) * 512]
                    own(dve.tensor_tensor(pl, pl, tmpg2[n], ALU.mult))
                    v = x[:, :, n * 512:(n + 1) * 512]
                    own(dve.tensor_tensor(v, v, pl, ALU.add))
                dve.wait_ge(s_sm, smc.up(32))
                norm_rows(gain2, xn).then_inc(s_x, 1)

            dve.wait_ge(s_cst, 64)
            dve.wait_ge(s_z, 1)
            for i in range(2 * HEADS_A):
                dve.wait_ge(s_bf, i + 1)
                j = dve.tensor_copy(windows[i % 2][:, (i // 2) * WIN:(i // 2 + 1) * WIN], TR[i % 2][:, 0:WIN])
                j.then_inc(s_bd, 1)
            own(dve.memset(tiny[:], 0.0))
            dve.tensor_copy(tiny[:, 1000:1001], tiny[:, 1:2]).then_inc(s_x, 1)
            dve.wait_ge(s_x, xr.up())
            with repeat(dve, "layers_dve", LAYERS, counts + [xr], per) as l:
                layer(l)
            second()


def split_rows(w):
    k, n = w.shape
    q = w.reshape(k // (QK * P), QK, P, n // QC, QC).transpose(3, 0, 2, 1, 4)
    return q.reshape(-1, P, QK * QC)


def glu_rows(g, u, d):
    groups = g.shape[1] // GLU
    gu = [split_rows(np.concatenate([g[:, i * GLU:(i + 1) * GLU], u[:, i * GLU:(i + 1) * GLU]], 1)) for i in range(groups)]
    dn = [split_rows(d[i * GLU:(i + 1) * GLU]) for i in range(groups)]
    out = [gu[0]]
    for i in range(1, groups):
        out += [gu[i], dn[i - 1]]
    return out + [dn[-1]]


def columns(v):
    return v.reshape(-1, P).T


def layer_stream(a, l):
    w = a["w_in"][l]
    at = np.cumsum([0, 256, 256, 512, 4, 4, 512, 256, 64, 8, 128, 512, 512, 512, 512, 1024, 1024, 1024])
    mq, mk, mv, mi, mf, mo, cq, kidx, widx, ckv, rq, rk, rv, rg, gm, ga, gr = (w[:, at[i]:at[i + 1]] for i in range(17))
    small = np.concatenate([cq, kidx, widx, mi, mf, np.zeros((D, 48), np.float32), ckv], 1)
    p = {n: a[n][l] for n in ("p_m", "p_a", "p_r")}
    parts = [split_rows(small), split_rows(np.concatenate([mq, mk], 1)), split_rows(mv), split_rows(rq),
             split_rows(a["a_wuq"][l]), split_rows(a["a_wuq_idx"][l]), split_rows(rk), split_rows(rv), split_rows(mo),
             split_rows(rg), split_rows(gm), split_rows(gr), split_rows(p["p_m"]), split_rows(p["p_r"]),
             split_rows(ga), split_rows(p["p_a"]), split_rows(a["w_out"][l])]
    return parts + glu_rows(a["w_gate"][l], a["w_up"][l], a["w_down"][l])


def second_stream(a):
    w = a["w_in_2"][0]
    at = np.cumsum([0, 512, 512, 512, 1024, 1536, 16, 1024, 1024])
    q, k, v, z, xbc, _, ga, gb = (w[:, at[i]:at[i + 1]] for i in range(8))
    wide = lambda n: np.concatenate(list(a[n][0]), 1)
    parts = [split_rows(m) for m in (xbc, q, k, v, z, ga, gb, a["w_out_a_2"][0], a["w_out_b_2"][0], a["w_out_2"][0])]
    parts += glu_rows(wide("w_gate_2"), wide("w_up_2"), np.concatenate(list(a["w_down_2"][0]), 0))
    return parts + [split_rows(a["w_ple_proj_2"][0]), split_rows(a["w_ple_gate_2"][0])]


def second_params(a):
    rep = lambda v: np.broadcast_to(v, (P, v.size))
    cw = a["conv_w_2"][0].reshape(4, 12, P).transpose(2, 1, 0).reshape(P, 48)
    dtw = a["w_in_2"][0][:, 4096:4112]
    sw = np.concatenate([dtw, a["w_rg_2"][0], a["w_re_2"][0]], 1).reshape(KT, P, 36).transpose(1, 0, 2).reshape(P, 8 * 36)
    return np.concatenate([columns(a["mix_norm_g_2"][0]), columns(a["ffn_norm_g_2"][0]), columns(a["ssd_norm_g_2"][0]), cw,
                           columns(a["conv_b_2"][0]), rep(a["dt_bias_2"][0]), rep(a["a_log_2"][0]), rep(a["d_skip_2"][0]),
                           rep(a["b_rg_2"][0]), rep(a["b_re_2"][0]), sw], 1)


def alibi_bias():
    i = np.arange(P)
    out = np.zeros((P, HEADS_A, WIN), np.float32)
    for t, c, n in ((0, 0, P), (1, P, SEQ)):
        dist = (t * P + i)[:, None] - np.arange(n)[None, :]
        for h in range(HEADS_A):
            out[:, h, c:c + n] = np.where(dist >= 0, -2.0 ** -(h + 1) * dist, -BIG)
    return out.reshape(P, HEADS_A * WIN)


def layer_params(a, l):
    rep = lambda v: np.broadcast_to(v, (P, v.size))
    cw = a["m_conv"][l].reshape(4, 4, P).transpose(2, 1, 0).reshape(P, 16)
    uk = a["a_wuk"][l].reshape(4, P, P).transpose(1, 0, 2).reshape(P, 512)
    uv = a["a_wuv"][l].transpose(1, 0, 2).reshape(P, 512)
    ki = np.concatenate([a["a_kidx_g"][l]] * 2)
    return np.concatenate([columns(a["norm1_g"][l]), columns(a["norm2_g"][l]), columns(a["a_qnorm_g"][l]), columns(ki),
                           columns(a["m_norm_g"][l]), columns(a["r_norm_g"][l]), cw, rep(a["a_kvnorm_g"][l]),
                           rep(a["m_ibias"][l]), rep(a["m_fbias"][l]), uk, uv], 1)


def constants():
    f = np.float32
    i = np.arange(P)
    pos = np.arange(SEQ)
    mask = np.where(pos[None, :] >= i[:, None], 0, -BIG).astype(f)
    qmask = np.where(i[None, :] <= i[:, None], 0, -BIG).astype(f)
    lg = np.log1p(-np.exp2(-5.0 - np.arange(4)))
    diff = pos[None, :] - i[:, None]
    ret = [np.where(diff >= 0, np.exp(np.maximum(diff, 0) * g) * P ** -0.5, 0).astype(f) for g in lg]
    ang = pos.astype(f)[:, None] * (f(10000.0) ** (-np.linspace(0, 1, 64).astype(f)))[None, :]
    by = lambda v: v.astype(f).reshape(TT, P, 64).transpose(1, 0, 2).reshape(P, 128)
    const = np.concatenate([np.eye(P, dtype=f), mask, qmask, *ret, by(np.cos(ang)), by(np.sin(ang))], 1)
    half = BUCKETS // 2
    onehot = np.zeros((BUCKETS, TT, WIN), f)
    for t in range(TT):
        for j in range(WIN):
            dist = t * P + P - 1 - j
            if dist >= 0:
                b = dist if dist < half else min(half + int(np.log(dist / half) / math.log(128 / half) * half), BUCKETS - 1)
                onehot[b, t, j] = 1
    return const, onehot


def kernel(**a):
    import concourse.bacc as bacc
    from concourse.bass_utils import run_bass_kernel_spmd

    a = {k: np.asarray(v) for k, v in a.items()}
    const, onehot = constants()
    second = second_params(a)
    quarters = []
    for l in range(LAYERS):
        quarters += layer_stream(a, l)
    quarters += second_stream(a)
    assert sum(len(v) for v in quarters) == TOTAL_Q
    arrays = {
        "stream": np.concatenate(quarters),
        "const": const,
        "small_in": np.stack([layer_params(a, l) for l in range(LAYERS)]
                             + [np.concatenate([second, np.zeros((P, L_END - S_END), np.float32)], 1)]),
        "x_in": np.ascontiguousarray(a["x"][0]),
        "onehot": onehot,
        "alibi": alibi_bias(),
        "gains": np.stack([np.broadcast_to(a[n], (P, D)) for n in ("final_norm_g", "final_norm_g_2")]),
        "p_in": np.ascontiguousarray(a["p_2"][0, 0]),
        "relb": np.ascontiguousarray(np.broadcast_to(a["rel_bias"][:, :, None], (BUCKETS, HEADS_A, P))),
    }
    per = {}
    for trial in range(2):
        nc = bacc.Bacc("TRN2", target_bir_lowering=False, num_devices=1, dynamic_dma_scratch_size=1024)
        t = {n: nc.dram_tensor(f"in_{n}", v.shape, F32, kind="ExternalInput").ap() for n, v in arrays.items()}
        scratch = nc.dram_tensor("bias_windows", [TT, P, HEADS_A * WIN], F32, kind="Internal").ap()
        out = nc.dram_tensor("out", [SEQ, D], F32, kind="ExternalOutput").ap()
        program(nc, t["stream"], t["const"], t["small_in"], t["x_in"], t["onehot"], t["relb"], scratch,
                t["alibi"], t["gains"], t["p_in"], out, per)
    r = run_bass_kernel_spmd(nc, [{f"in_{n}": v for n, v in arrays.items()}], core_ids=[0])
    return r.results[0]["out"][None]
```

```python
import math
from contextlib import ExitStack, contextmanager

import numpy as np

import concourse.bass as bass
from concourse import mybir

F32 = mybir.dt.float32
F32R = mybir.dt.float32r
ALU = mybir.AluOpType
ACT = mybir.ActivationFunctionType
AX = mybir.AxisListType

P = 128
SEQ = 256
TT = SEQ // P
D = 1024
KT = D // P
LAYERS = 2
EPS = 1e-6
QK = 2
QC = 512
RING = 3
BIG = 1e30
TAKEN = -3e38
HEADS_A = 8
WIN = SEQ + P
TOPK = 64
SLOTS = 4
SSD_HEADS = 16
BUCKETS = 32
GLU = 256
D_FF = 2816
FF_GROUPS = D_FF // GLU
EXPERTS = 16
MOE_FF = 512
MOE_GROUPS_PER_EXPERT = MOE_FF // GLU
LAYER_Q = 4 * 14 + 2 + 2 * 6 + 4 * 2 + 6 * FF_GROUPS
SECOND_Q = 4 * 12 + 2 * 2 + 4 * 2 + 4 * 2 + 6 * EXPERTS * MOE_GROUPS_PER_EXPERT + 2 + 4 * 2
TOTAL_Q = LAYERS * LAYER_Q + SECOND_Q

C_ID, C_MASK, C_QMASK, C_RET = 0, 128, 384, 512
C_COS, C_SIN, C_END = C_RET + 4 * SEQ, C_RET + 4 * SEQ + 128, C_RET + 4 * SEQ + 256
L_N1, L_N2, L_QN, L_KI, L_MN, L_RN, L_CW, L_KV, L_IB, L_UK, L_UV, L_END = (
    0, 8, 16, 18, 19, 23, 27, 43, 171, 179, 179 + 512, 179 + 1024)
(S_N1, S_N2, S_NS, S_CW, S_CB, S_DTB, S_AL, S_DS, S_BR, S_SW, S_G1, S_END) = (
    0, 8, 16, 24, 72, 84, 100, 116, 132, 152, 152 + 8 * 36, 160 + 8 * 36)


class Count:

    def __init__(self, sem):
        self.sem, self.reg, self.n = sem, 0, 0

    def up(self, k=1):
        self.n += k
        return self.reg + self.n

    def back(self, k):
        return self.reg + self.n - k


class Chain(Count):

    def __init__(self, sem, eng):
        super().__init__(sem)
        self.eng = eng

    def __call__(self, ins):
        ins.then_inc(self.sem, 1)
        self.eng.wait_ge(self.sem, self.up())


@contextmanager
def repeat(eng, name, trips, counts, per):
    with eng.Fori(0, trips) as i:
        saved = [(c, c.reg, c.n) for c in counts]
        for k, c in enumerate(counts):
            c.reg = c.reg + i * per.get((name, k), 6)
        yield i
    for k, (c, reg, n) in enumerate(saved):
        per[(name, k)] = c.n - n
        c.reg = reg
        c.n += (c.n - n) * (trips - 1)


def program(nc, stream, const, small_in, x_in, onehot, relb, scratch, alibi, gains, p_in, out, per):
    ctx = ExitStack()
    with ctx:
        def sb(name, shape, dt=F32):
            return ctx.enter_context(nc.sbuf_tensor(name, shape, dt))

        def sem(name):
            return ctx.enter_context(nc.semaphore(name))

        raw = sb("raw", [P, RING, QK * QC])
        w_hi = sb("w_hi", [P, RING, QK * QC], F32R)
        w_lo = sb("w_lo", [P, RING, QK * QC], F32R)
        cst = sb("cst", [P, C_END])
        ident = cst[:, C_ID:C_ID + P]
        mask = cst[:, C_MASK:C_MASK + SEQ]
        qmask = cst[:, C_QMASK:C_QMASK + P]
        ret_decay = cst[:, C_RET:C_RET + 4 * SEQ].rearrange("p (h t) -> p h t", h=4)
        cosv = cst[:, C_COS:C_COS + 128].rearrange("p (t d) -> p t d", t=TT)
        sinv = cst[:, C_SIN:C_SIN + 128].rearrange("p (t d) -> p t d", t=TT)
        small = sb("small", [P, L_END])
        x = sb("x", [P, TT, D])
        hT = sb("hT", [P, 2, KT, SEQ], F32R)
        xn = sb("xn", [P, TT, D])
        bias = sb("bias", [P, HEADS_A, WIN])
        mixT = sb("mixT", [P, 3, 2, 4, SEQ], F32R)
        heT = mixT[:, 0].rearrange("p a k t -> p (a k t)")[:, 0:2 * QK * SEQ].rearrange("p (a k t) -> p a k t", a=2, k=QK)
        logits = sb("logits", [P, HEADS_A, WIN])
        gates = sb("gates", [P, 2, TT, D])
        arena = sb("arena", [P, 14 * 1024 + 64])
        tiny = sb("tiny", [P, 1024])
        ones = sb("ones", [16, SEQ])
        zeros = sb("zeros", [16, P], F32R)
        wexp = sb("wexp", [P, SLOTS, WIN])
        prob = sb("prob", [P, SLOTS, WIN])
        sw = sb("sw", [P, 2, 8 * 36], F32R)
        rows2 = sb("rows2", [16, 2, SEQ])

        def ar(at, *shape):
            n = int(np.prod(shape))
            v = arena[:, at:at + n]
            if len(shape) == 2:
                return v.rearrange("p (a b) -> p a b", b=shape[1])
            if len(shape) == 3:
                return v.rearrange("p (a b c) -> p a b c", b=shape[1], c=shape[2])
            if len(shape) == 4:
                return v.rearrange("p (a b c d) -> p a b c d", b=shape[1], c=shape[2], d=shape[3])
            return v

        gates_flat = gates[:].rearrange("p g t d -> p (g t d)")
        windows = logits[0:HEADS_A].rearrange("p h w -> p (h w)")[:, 0:TT * WIN]
        relb_sb = arena[0:BUCKETS, 0:HEADS_A]
        onehot_sb = arena[0:BUCKETS, 1024:1024 + 2 * WIN].rearrange("p (t w) -> p t w", t=2)
        cqT = mixT[:, 2].rearrange("p a k t -> p (a k t)")[:, 0:2 * QK * SEQ].rearrange("p (a k t) -> p a k t", a=2, k=QK)
        gbuf, he = ar(0, TT, GLU), ar(TT * GLU, TT, GLU)
        K1 = 1024
        mqk_tok = ar(0, TT, 512)
        qkT = ar(0, 4, SEQ)
        conv_in = ar(K1, 4, SEQ + 3)
        m_out = ar(K1, TT, 4, 129)
        mv = ar(2 * K1 + 16, TT, 4, 129)
        sm = ar(3 * K1 + 64, TT, 512)
        A0 = 4 * K1 + 64
        rq = ar(A0, TT, 512)
        r_out = ar(A0, TT, 512)
        rk = ar(A0 + K1, TT, 512)
        rv = ar(A0 + 2 * K1, TT, 512)
        rg = ar(A0 + 3 * K1, TT, 512)
        mo = ar(A0 + 4 * K1, TT, 512)
        qT = ar(A0 + 5 * K1, 2, 4, SEQ)
        rqT = ar(A0 + 7 * K1, 2, 4, SEQ)
        kidxT = ar(A0 + 9 * K1 + 512, SEQ)
        ckvT = ar(A0 + 9 * K1 + 768, SEQ)
        conv_out = qkT
        tmpy = mo
        qlatA = ar(0, 4, SEQ)
        qlatB = ar(A0 + K1, 4, SEQ)

        def qlat(h):
            return (qlatA if h < 4 else qlatB)[:, h % 4, :]

        bank = [ctx.enter_context(nc.psum_tensor(f"bank{i}", [P, 512], F32)) for i in range(8)]
        LIN, TR, AB = bank[0:2], bank[2:4], bank[4:8]

        s_raw = [sem(f"raw_in{i}") for i in range(RING)]
        s_hi = sem("hi_done")
        s_lo = sem("lo_done")
        s_used = sem("quarter_used")
        s_lin = sem("lin_full")
        s_la = sem("lin_read_act")
        s_ld = sem("lin_read_dve")
        s_tr = sem("tr_full")
        s_th = sem("tr_hi")
        s_td = sem("tr_read")
        s_ab = sem("mix_full")
        s_ad = sem("mix_read")
        s_var = sem("var_ready")
        s_std = sem("std_ready")
        s_rs = sem("rms_ready")
        s_nx = sem("normed")
        s_arg = sem("exp_arg")
        s_ex2 = sem("decay_exp")
        s_pp = sem("head_weights")
        s_sw = sem("small_weights_hi")
        s_rot = sem("rotated")
        s_pv = sem("values_summed")
        s_bf, s_bd = sem("bias_full"), sem("bias_read")
        s_exp = sem("exp_done")
        s_act = sem("act_out")
        s_x = sem("x_ready")
        s_g = sem("glu_gate")
        s_sm = sem("small_in")
        s_alibi = sem("alibi_in")
        s_dist = sem("distances_in")
        s_cst = sem("const_in")
        s_b = sem("bias_moved")
        s_ch_d = sem("dve_chain")
        s_out = sem("out_written")
        s_z = sem("cleared")

        block = ctx.enter_context(nc.Block())

        @block.sync
        def _(sp):
            sp.dma_start(relb_sb, relb).then_inc(s_dist, 16)
            sp.dma_start(onehot_sb, onehot).then_inc(s_dist, 16)
            for i in range(RING):
                sp.dma_start(raw[:, i], stream[i]).then_inc(s_raw[i], 16)
            sp.dma_start(x[:], x_in.rearrange("(t p) d -> p t d", p=P)).then_inc(s_cst, 16)
            sp.dma_start(cst[:], const).then_inc(s_cst, 16)
            sp.dma_start(small[:], small_in[0]).then_inc(s_sm, 16)

            def load(r):
                for i in range(RING):
                    src = stream[r * RING + i]
                    sp.wait_ge(s_hi, r * RING + (i + 1 - RING))
                    sp.wait_ge(s_lo, r * RING + (i + 1 - RING))
                    sp.dma_start(raw[:, i], src).then_inc(s_raw[i], 16)

            for i in range(TT):
                load(1 + i)
                sp.wait_ge(s_bd, i + 1)
                sp.dma_start(scratch[i].rearrange("r (h w) -> h r w", h=HEADS_A),
                             windows[:, i * WIN:(i + 1) * WIN].unsqueeze(1).broadcast_to([HEADS_A, P, WIN])).then_inc(s_b, 16)
            load(1 + TT)
            sp.wait_ge(s_b, 16 * TT)
            sp.dma_start(bias[:, :, 0:P], bass.AP(scratch.tensor, P - 1, [[HEADS_A * WIN - 1, P], [WIN, HEADS_A], [1, P]])).then_inc(s_b, 16)
            load(2 + TT)
            sp.dma_start(bias[:, :, P:WIN], bass.AP(scratch.tensor, P * HEADS_A * WIN + P - 1,
                                                    [[HEADS_A * WIN - 1, P], [WIN, HEADS_A], [1, SEQ]])).then_inc(s_b, 16)
            with sp.Fori(3 + TT, TOTAL_Q // RING) as r:
                load(r)
            for t in range(TT):
                sp.wait_ge(s_x, 2 * (LAYERS + 2) + 1 + t)
                sp.dma_start(out[t * P:(t + 1) * P, :], xn[:, t, :]).then_inc(s_out, 16)
            sp.wait_ge(s_out, 16 * TT)

        tok = [ar(0, TT, 512), ar(K1, TT, 512)]
        yb = ar(0, TT, D)
        conv2 = ar(2 * K1, 4, SEQ + 3)
        xbcT = [ar(3 * K1 + 16 + i * K1, 4, SEQ) for i in range(3)]
        xs = ar(6 * K1 + 16, TT, D)
        xdt = ar(8 * K1 + 16, TT, D)
        qkT2 = ar(10 * K1 + 16, 2, 4, SEQ)
        v2 = ar(12 * K1 + 16, TT, 512)
        cb = ar(13 * K1 + 16, 2, WIN)
        mixT8 = mixT[:, 0:2].rearrange("p m a k t -> p (m a k t)").rearrange("p (a k t) -> p a k t", a=2, k=KT)
        bflat = bias[:].rearrange("p h w -> p (h w)")
        gain1 = gates_flat[:, 0:D]
        gain2 = bflat[:, 0:D]
        p_tok = bflat[:, D:D + 512].rearrange("p (t d) -> p t d", t=TT)
        ple = gates[:, 0]
        tmpg2 = [ar(0, TT, 512), ar(K1, TT, 512)]

        def tn(at, *shape):
            n = int(np.prod(shape))
            v = tiny[:, at:at + n]
            if len(shape) == 2:
                return v.rearrange("p (a b) -> p a b", b=shape[1])
            return v

        g16 = tn(64, TT, 16)
        gif = tn(96, TT, 8)
        acol, mcol = tn(176, TT, 4), tn(184, TT, 4)
        em = tn(192, TT, 4)
        den = tn(200, TT, 4)
        keep = tn(256, WIN)
        dt, da, cs = tn(624, TT, 16), tn(656, TT, 16), tn(688, TT, 16)
        X_INV = 1008
        comb = tn(740, TT, 16)
        lflat = logits[:].rearrange("p h w -> p (h w)")
        work = lflat[:, 0:WIN]
        relu_w = lflat[:, WIN:2 * WIN]
        best = lflat[:, 2 * WIN:2 * WIN + 8]
        rows = lflat[0:4, 1152:1152 + 5 * SEQ].rearrange("p (a b) -> p a b", b=SEQ)
        small_rows = lflat[0:32, 0:SEQ]
        xflat = xn[:].rearrange("p t d -> p (t d)")

        def heads(v):
            return v.rearrange("p t (h d) -> p t h d", h=4)

        @block.tensor
        def _(pe):
            lo, tr, ab = Count(s_lo), Count(s_td), Count(s_ad)
            la, ld, nx, rot = Count(s_la), Count(s_ld), Count(s_nx), Count(s_rot)
            counts = [lo, tr, ab, la, ld, nx, rot]
            free = {}

            def quarter():
                pe.wait_ge(s_lo, lo.up())
                s = (lo.n - 1) % RING
                return (w_hi[:, s, :].rearrange("p (k n) -> p k n", k=QK),
                        w_lo[:, s, :].rearrange("p (k n) -> p k n", k=QK))

            def claim(b, reader):
                if b in free:
                    c, n = free[b]
                    pe.wait_ge(c.sem, c.reg + n)
                c = la if reader == "act" else ld
                c.up()
                free[b] = (c, c.n)

            def product(lhs, nk, reader, between=None, feed=None, fed=False, each=None):
                if feed and not fed:
                    transposed(feed[0], KT // 2)
                for k0 in range(0, nk, QK):
                    if feed:
                        if k0 == QK:
                            feed[1]()
                        if 0 < k0 and k0 + QK < nk:
                            transposed(feed[0], QK, k0 + QK)
                        pe.wait_ge(s_td, tr.back(1 if k0 + QK < nk else 0))
                    hi, lw = quarter()
                    for t in range(TT):
                        if k0 == 0:
                            claim(t, reader)
                        for k in range(QK):
                            for n, (a, w) in enumerate(((0, hi), (1, hi), (0, lw))):
                                mm = pe.matmul(LIN[t][:, :], lhs[:, a, k0 + k, t * P:(t + 1) * P], w[:, k, :],
                                               start=(k0 + k == 0 and n == 0), stop=(k0 + k == nk - 1 and n == 2))
                        if t == 0 and k0 + QK == nk:
                            mm.then_inc(s_lin, 1)
                    mm.then_inc(s_used, 1)
                    if between and k0 + QK == nk // 2:
                        between()
                    if each:
                        each(k0 // QK)

            def tr_bank():
                f = tr.up()
                if tr.n > 2:
                    pe.wait_ge(s_td, f - 2)
                return TR[(tr.n - 1) % 2]

            def ab_bank():
                f = ab.up()
                if ab.n > 4:
                    pe.wait_ge(s_ad, f - 4)
                return AB[(ab.n - 1) % 4]

            def transposed(src, nk, first=0):
                for k0 in range(first, first + nk, 2):
                    b = tr_bank()
                    for k in range(2):
                        for t in range(TT):
                            mm = pe.transpose(b[:, k * SEQ + t * P:k * SEQ + (t + 1) * P], src(t, k0 + k), ident)
                    mm.then_inc(s_tr, 1)

            def scores(b, at, k, q):
                pe.matmul(b[:, at:at + SEQ], k[:, 0:P], q, start=True, stop=True, skip_group_check=True)
                return pe.matmul(b[:, at + SEQ:at + WIN], k[:, P:SEQ], q[:, P:SEQ], start=True, stop=True,
                                 skip_group_check=True)

            def weighted(b, at, n, w, v):
                pe.matmul(b[:, at:at + n], w[:, 0:P], v(0), start=True, stop=True, skip_group_check=True)
                pe.matmul(b[:, at + n:at + 2 * n], w[:, P:SEQ], v(0), start=True, stop=False, skip_group_check=True)
                return pe.matmul(b[:, at + n:at + 2 * n], w[:, SEQ:WIN], v(1), start=False, stop=True,
                                 skip_group_check=True)

            def x_cols(t, k):
                return x[:, t, k * P:(k + 1) * P]

            def y_cols(t, k):
                return xn[:, t, k * P:(k + 1) * P]

            def layer(l):
                pe.wait_ge(s_x, xr.up())
                product(hT, KT, "act", feed=(x_cols, lambda: pe.wait_ge(s_x, xr.up())))
                product(hT, KT, "act")

                def qk_by_feature():
                    pe.wait_ge(s_la, la.back(2))
                    transposed(lambda t, k: mqk_tok[:, t, k * P:(k + 1) * P], 4)

                product(hT, KT, "act", between=qk_by_feature)

                def small_by_feature():
                    pe.wait_ge(s_nx, nx.up())
                    transposed(lambda t, k: sm[:, t, k * P:(k + 1) * P], 4)

                product(hT, KT, "act", between=small_by_feature)
                pe.wait_ge(s_td, tr.back(1))
                for i in range(2):
                    hi, lw = quarter()
                    for f in range(4):
                        if f % 2 == 0:
                            claim(f // 2, "act")
                        for k in range(QK):
                            for n, (w, a) in enumerate(((hi, 0), (lw, 0), (hi, 1))):
                                mm = pe.matmul(LIN[f // 2][:, (f % 2) * SEQ:(f % 2 + 1) * SEQ], w[:, k, f * P:(f + 1) * P],
                                               cqT[:, a, k, :], start=(k == 0 and n == 0), stop=(k == QK - 1 and n == 2),
                                               skip_group_check=True)
                        if f == 1:
                            mm.then_inc(s_lin, 1)
                    mm.then_inc(s_used, 1)

                def gate_rows():
                    pe.wait_ge(s_nx, nx.up())
                    b = tr_bank()
                    for g in range(2):
                        for t in range(TT):
                            mm = pe.transpose(b[0:4, g * SEQ + t * P:g * SEQ + (t + 1) * P], gif[:, t, 4 * g:4 * g + 4], ident)
                    mm.then_inc(s_tr, 1)

                product(hT, KT, "act", between=gate_rows)
                pe.wait_ge(s_td, tr.back(1))
                for g in range(8):
                    b = ab_bank()
                    r = slice(64 * (g % 2), 64 * (g % 2) + 64)
                    pe.matmul(b[:, 0:P], qT[r, 1, g // 2, 0:P], kidxT[r, 0:P], start=True, stop=True, skip_group_check=True)
                    pe.matmul(b[:, P:WIN], qT[r, 1, g // 2, P:SEQ], kidxT[r, :], start=True, stop=True,
                              skip_group_check=True).then_inc(s_ab, 1)

                def gate_columns():
                    pe.wait_ge(s_nx, nx.up())
                    b = tr_bank()
                    for g, row in enumerate((0, 3)):
                        for t in range(TT):
                            mm = pe.matmul(b[:, 8 * g + 4 * t:8 * g + 4 * t + 4], rows[:, row, t * P:(t + 1) * P],
                                           ident[0:4, 0:4], start=True, stop=True, skip_group_check=True)
                    mm.then_inc(s_tr, 1)

                def rotated(src):
                    def turn():
                        pe.wait_ge(s_rot, rot.up())
                        transposed(lambda t, k: src[:, t, k * P:(k + 1) * P], 4)
                    return turn

                product(hT, KT, "act", between=gate_columns)
                product(hT, KT, "act", between=rotated(rq))
                product(hT, KT, "act", between=rotated(rk))
                for h in range(4):
                    pe.matmul(ab_bank()[:, 0:SEQ], ident[0:4, h:h + 1].to_broadcast([4, P]), rows[:, 2, :], start=True,
                              stop=True).then_inc(s_ab, 1)
                product(hT, KT, "act")
                pe.wait_ge(s_act, acts.up())

                def m_scores(h):
                    r = slice(64 * (h % 2), 64 * (h % 2) + 64)
                    scores(ab_bank(), 0, qkT[r, 2 + h // 2, :], qkT[r, h // 2, :]).then_inc(s_ab, 1)
                    return ab.back(0)

                weights = [m_scores(0)]
                for h in range(4):
                    if h < 3:
                        weights.append(m_scores(h + 1))
                    pe.wait_ge(s_ad, weights[h])
                    weighted(ab_bank(), 0, 129, prob[:, h % SLOTS], lambda s: mv[:, s, h, :]).then_inc(s_ab, 1)
                product(hT, KT, "act")
                pe.wait_ge(s_ad, ab.back(0))
                uk = small[:, L_UK:L_UK + 512].rearrange("p (a c) -> p a c", a=4)
                for j in range(4):
                    b = ab_bank()
                    r = slice(64 * (j % 2), 64 * (j % 2) + 64)
                    for i in range(2):
                        pair = 2 * (j // 2) + i
                        mm = pe.matmul(b[:, i * SEQ:(i + 1) * SEQ], uk[r, pair, :], qT[r, 0, pair, :], start=True, stop=True,
                                       skip_group_check=True)
                    mm.then_inc(s_ab, 1)

                def r_scores(h):
                    scores(ab_bank(), 0, rqT[:, 1, h, :], rqT[:, 0, h, :]).then_inc(s_ab, 1)
                    return ab.back(0)

                pe.wait_ge(s_td, tr.back(0))
                weights = [r_scores(0)]
                for h in range(4):
                    if h < 3:
                        weights.append(r_scores(h + 1))
                    pe.wait_ge(s_ad, weights[h])
                    weighted(ab_bank(), 0, P, prob[:, h % SLOTS], lambda s: rv[:, s, h * P:(h + 1) * P]).then_inc(s_ab, 1)
                product(hT, KT, "act")
                pe.wait_ge(s_ad, ab.back(0))
                for h in range(HEADS_A):
                    b = ab_bank()
                    pe.matmul(b[:, 0:P], qlat(h)[:, 0:P], ckvT[:, 0:P], start=True, stop=True, skip_group_check=True)
                    pe.matmul(b[:, P:WIN], qlat(h)[:, P:SEQ], ckvT, start=True, stop=True,
                              skip_group_check=True).then_inc(s_ab, 1)

                def m_by_feature():
                    pe.wait_ge(s_nx, nx.up())
                    transposed(lambda t, k: m_out[:, t, k, 0:P], 4)

                def r_by_feature():
                    pe.wait_ge(s_nx, nx.up())
                    transposed(lambda t, k: r_out[:, t, k * P:(k + 1) * P], 4)

                product(hT, KT, "act", between=m_by_feature)
                pe.wait_ge(s_td, tr.back(0))
                product(mixT[:, 0], 4, "dve", between=r_by_feature)
                product(mixT[:, 0], 4, "dve")
                pe.wait_ge(s_td, tr.back(0))
                product(mixT[:, 1], 4, "dve")
                values, latent_out = attention(latent=True)
                product(hT, KT, "act", each=lambda q: values(q - 1) if q else None)
                product(hT, KT, "act", each=lambda q: values(3 + q))

                def last_head():
                    values(HEADS_A - 1)
                    latent_out()

                product(mixT[:, 1], 4, "dve", between=last_head)
                pe.wait_ge(s_ad, ab.back(0))
                product(mixT[:, 2], 4, "dve")
                product(mixT[:, 2], 4, "dve", between=y_by_feature)
                product(hT, KT, "dve", feed=(y_cols, next_nx), fed=True)
                product(hT, KT, "dve")
                next_nx()
                product(hT, KT, "dve", feed=(x_cols, next_nx))
                seed()
                with repeat(pe, "ff_pe", FF_GROUPS - 1, counts, per):
                    hidden()
                    group()
                    down()
                hidden()
                down()

            def next_nx():
                pe.wait_ge(s_nx, nx.up())

            def y_by_feature():
                next_nx()
                transposed(y_cols, KT // 2)

            def attention(latent):
                held = []

                def turned(h):
                    b = tr_bank()
                    for i in range(3):
                        mm = pe.transpose(b[:, i * P:(i + 1) * P], logits[:, h, i * P:(i + 1) * P], ident)
                    mm.then_inc(s_tr, 1)

                def value(h):
                    pe.wait_ge(s_td, tr.back(1 if h < HEADS_A - 1 else 0))
                    p = prob[:, h % SLOTS]
                    if h % (2 if latent else 4) == 0:
                        held.append(ab_bank())
                    b = held[-1]
                    if latent:
                        o = b[:, (h % 2) * SEQ:(h % 2 + 1) * SEQ]
                        v = [sm[:, s, 384:512] for s in range(2)]
                    else:
                        o = b[64 * (h % 2):64 * (h % 2) + 64, (h // 2 % 2) * SEQ:(h // 2 % 2 + 1) * SEQ]
                        v = [v2[:, s, 64 * h:64 * h + 64] for s in range(2)]
                    pe.matmul(o, v[0], p[:, 0:SEQ], start=True, stop=False, skip_group_check=True)
                    mm = pe.matmul(o[:, P:SEQ], v[1], p[:, SEQ:WIN], start=False, stop=True, skip_group_check=True)
                    mm.then_inc(s_pv, 1)

                def step(q):
                    if q == 0:
                        next_nx()
                        turned(0)
                        turned(1)
                        return
                    value(q - 1)
                    if q + 1 < HEADS_A:
                        turned(q + 1)

                def out():
                    value(HEADS_A - 1)
                    if not latent:
                        return
                    uv = small[:, L_UV:L_UV + 512]
                    pe.wait_ge(s_ad, ab.back(0))
                    for j in range(2):
                        b = ab_bank()
                        for h in range(4 * j, 4 * j + 4):
                            mm = pe.matmul(b[64 * (h % 2):64 * (h % 2) + 64, (h // 2 % 2) * SEQ:(h // 2 % 2 + 1) * SEQ],
                                           uv[:, 64 * h:64 * h + 64], qlat(h), start=True, stop=True,
                                           skip_group_check=True)
                        mm.then_inc(s_ab, 1)

                return step, out

            def seed():
                pe.wait_ge(s_ad, ab.back(0))
                for b in AB:
                    pe.matmul(b[:, :], zeros[:], zeros[:, 0:1].to_broadcast([16, QC]), start=True, stop=False,
                              skip_group_check=True)

            def hidden():
                pe.wait_ge(s_ld, ld.back(0))
                b = tr_bank()
                for k in range(QK):
                    for t in range(TT):
                        mm = pe.transpose(b[:, k * SEQ + t * P:k * SEQ + (t + 1) * P], he[:, t, k * P:(k + 1) * P], ident)
                mm.then_inc(s_tr, 1)

            def group():
                product(hT, KT, "dve")

            def down():
                pe.wait_ge(s_td, tr.back(0))
                for n in range(2):
                    hi, lw = quarter()
                    for t in range(TT):
                        for k in range(QK):
                            for a, w in ((0, hi), (1, hi), (0, lw)):
                                mm = pe.matmul(AB[2 * t + n][:, :], heT[:, a, k, t * P:(t + 1) * P], w[:, k, :],
                                               start=False, stop=True, skip_group_check=True)
                    mm.then_inc(s_used, 1)

            def small_product(c0, n, feed=None):
                b = ab_bank()
                w = sw[:].rearrange("p a (k n) -> p a k n", k=KT)
                if feed:
                    transposed(feed[0], KT // 2)
                for k0 in range(0, KT, QK):
                    if feed:
                        if k0 == QK:
                            feed[1]()
                        if 0 < k0 and k0 + QK < KT:
                            transposed(feed[0], QK, k0 + QK)
                        pe.wait_ge(s_td, tr.back(1 if k0 + QK < KT else 0))
                    for k in range(k0, k0 + QK):
                        for i, (wa, a) in enumerate(((0, 0), (1, 0), (0, 1))):
                            mm = pe.matmul(b[0:n, 0:SEQ], w[:, wa, k, c0:c0 + n], hT[:, a, k, :],
                                           start=(k == 0 and i == 0), stop=(k == KT - 1 and i == 2))
                mm.then_inc(s_ab, 1)

            def small_columns(n):
                pe.wait_ge(s_ad, ab.back(0))
                b = ab_bank()
                for t in range(TT):
                    mm = pe.matmul(b[:, t * n:(t + 1) * n], small_rows[0:n, t * P:(t + 1) * P], ident[0:n, 0:n], start=True,
                                   stop=True, skip_group_check=True)
                mm.then_inc(s_ab, 1)

            def second():
                pe.wait_ge(s_x, xr.up())
                product(hT, KT, "act", feed=(x_cols, lambda: pe.wait_ge(s_x, xr.up())))
                pe.wait_ge(s_nx, nx.up())
                small_product(0, 16)

                def token_tiles(i):
                    def turn():
                        pe.wait_ge(s_la, la.back(2))
                        transposed(lambda t, k: tok[i][:, t, k * P:(k + 1) * P], 4)
                    return turn

                def dt_and_x():
                    small_columns(16)
                    token_tiles(0)()

                product(hT, KT, "act", between=dt_and_x)
                product(hT, KT, "act", between=token_tiles(1))
                product(hT, KT, "act", between=token_tiles(0))
                product(hT, KT, "act", between=token_tiles(1))
                product(hT, KT, "act", between=token_tiles(0))

                def decay_rows():
                    pe.wait_ge(s_nx, nx.up())
                    b = tr_bank()
                    for t in range(TT):
                        mm = pe.transpose(b[0:16, t * P:(t + 1) * P], da[:, t, :], ident)
                    mm.then_inc(s_tr, 1)

                def decay_columns():
                    pe.wait_ge(s_nx, nx.up())
                    b = tr_bank()
                    for t in range(TT):
                        mm = pe.matmul(b[:, t * 16:(t + 1) * 16], rows2[:, 1, t * P:(t + 1) * P], ident[0:16, 0:16], start=True,
                                       stop=True, skip_group_check=True)
                    mm.then_inc(s_tr, 1)

                product(hT, KT, "act", between=decay_rows)
                product(hT, KT, "act", between=decay_columns)
                pe.wait_ge(s_act, acts.up(3))
                for t in range(TT):
                    for i in range(2):
                        b = tr_bank()
                        for k in range(4):
                            mm = pe.transpose(b[:, k * P:(k + 1) * P], xbcT[i][:, k, t * P:(t + 1) * P], ident)
                        mm.then_inc(s_tr, 1)
                for g in range(2):
                    scores(ab_bank(), 0, xbcT[2][:, g, :], xbcT[2][:, 2 + g, :]).then_inc(s_ab, 1)
                pe.wait_ge(s_td, tr.back(4))
                for h in range(HEADS_A):
                    b = ab_bank()
                    r = slice(64 * (h % 2), 64 * (h % 2) + 64)
                    q, k = qkT2[r, 0, h // 2, :], qkT2[r, 1, h // 2, :]
                    pe.matmul(b[:, 0:P], q[:, 0:P], k[:, 0:P], start=True, stop=True, skip_group_check=True)
                    pe.matmul(b[:, P:WIN], q[:, P:SEQ], k, start=True, stop=True, skip_group_check=True).then_inc(s_ab, 1)

                for g in range(4):
                    for h in range(4 * g, 4 * g + 4):
                        pe.matmul(ab_bank()[:, 0:SEQ], ident[0:16, h:h + 1].to_broadcast([16, P]), rows2[:, 1, :], start=True,
                                  stop=True).then_inc(s_ab, 1)
                    product(hT, KT, "act")
                    b = ab_bank()
                    if g == 0:
                        pe.wait_ge(s_nx, nx.up())
                    for h in range(4 * g, 4 * g + 4):
                        pe.wait_ge(s_pp, pp.up())
                        weighted(b, P * (h % 4), 64, prob[:, h % SLOTS],
                                 lambda s: xdt[:, s, 64 * h:64 * h + 64]).then_inc(s_pv, 1)
                step, last = attention(latent=False)
                for h in range(HEADS_A):
                    step(h)
                last()
                pe.wait_ge(s_ad, ab.back(0))
                product(mixT[:, 2], 4, "dve")
                product(mixT[:, 2], 4, "dve")
                pe.wait_ge(s_nx, nx.up())
                product(mixT8, KT, "dve", feed=(lambda t, k: yb[:, t, k * P:(k + 1) * P], lambda: None))
                product(mixT8, KT, "dve", between=y_by_feature)
                product(hT, KT, "dve", feed=(y_cols, next_nx), fed=True)

                def p_by_feature():
                    pe.wait_ge(s_sm, 16 * (1 + 2 * LAYERS + 2))
                    transposed(lambda t, k: p_tok[:, t, k * P:(k + 1) * P], QK)

                product(hT, KT, "dve", between=p_by_feature)
                pe.wait_ge(s_td, tr.back(0))
                product(cqT, QK, "act")
                product(cqT, QK, "act")
                next_nx()
                small_product(16, 20, feed=(x_cols, next_nx))
                small_columns(20)
                seed()
                product(hT, KT, "dve")
                with repeat(pe, "moe_pe", EXPERTS - 1, counts, per):
                    for _ in range(2):
                        hidden()
                        group()
                        down()
                free.clear()
                hidden()
                group()
                down()
                hidden()
                down()
                pe.wait_ge(s_x, xr.up())
                product(hT, KT, "act", feed=(x_cols, lambda: pe.wait_ge(s_x, xr.up())))
                product(hT, KT, "act")

            acts, pp, xr = Count(s_act), Count(s_pp), Count(s_x)
            counts += [acts, xr]
            pe.wait_ge(s_dist, 32)
            for i in range(TT):
                pe.matmul(bank[i][0:HEADS_A, 0:WIN], relb_sb, onehot_sb[:, i, :], start=True, stop=True).then_inc(s_bf, 1)
            pe.wait_ge(s_bd, TT)
            pe.wait_ge(s_cst, 32)
            with repeat(pe, "layers_pe", LAYERS, counts, per) as l:
                free.clear()
                layer(l)
            free.clear()
            second()

        @block.scalar
        def _(act):
            hi = Count(s_hi)
            used, lin, tr, ab, raws = Count(s_used), Count(s_lin), Count(s_tr), Count(s_ab), [Count(s) for s in s_raw]
            var, arg, ad, rs, la, smc, pos = (Count(s_var), Count(s_arg), Count(s_ad), Count(s_rs), Count(s_la),
                                             Count(s_sm), Count(s_used))
            smc.n = -16
            counts = [hi, used, lin, tr, ab, *raws, var, arg, ad, rs, la, smc, pos]

            def high():
                if hi.n >= TOTAL_Q:
                    return
                s = hi.n % RING
                act.wait_ge(s_raw[s], raws[s].up(16))
                if hi.n >= RING:
                    act.wait_ge(s_used, used.up())
                hi.n += 1
                act.activation(w_hi[:, s, :], raw[:, s, :], ACT.Copy).then_inc(s_hi, 1)

            def unit(n, read=None, first=None, mid=None, feed=None, fed=False, early=None):
                if feed:
                    dst, gain = feed
                    if not fed:
                        split(dst, KT // 2, gain)
                    high()
                    split(dst, QK, gain, KT // 2)
                    high()
                    split(dst, QK, gain, KT // 2 + QK)
                    if early:
                        early()
                    made = 2
                else:
                    made = n // 2 if mid else 0
                    for _ in range(made):
                        high()
                    if mid:
                        mid()
                if read is None:
                    for _ in range(n - made):
                        high()
                    pos.up(n)
                    lin.up()
                    return
                for _ in range(n - 1 - made):
                    high()
                if first:
                    first()
                act.wait_ge(s_lin, lin.up())
                read(0).then_inc(s_la, 1)
                act.wait_ge(s_used, pos.up(n))
                read(1).then_inc(s_la, 1)
                high()

            def roots(n, at=0):
                act.wait_ge(s_var, var.up())
                act.activation(tiny[:, 16:16 + n], tiny[:, at:at + n], ACT.Sqrt).then_inc(s_std, 1)

            def split(dst, nk, gain=None, start=0):
                for k0 in range(start, start + nk, 2):
                    act.wait_ge(s_tr, tr.up())
                    b = TR[(tr.n - 1) % 2]
                    if gain is None:
                        act.activation(dst[:, 0, k0:k0 + 2, :].rearrange("p k t -> p (k t)"), b[:, :], ACT.Copy).then_inc(s_th, 1)
                    else:
                        for k in range(2):
                            i = act.activation(dst[:, 0, k0 + k, :], b[:, k * SEQ:(k + 1) * SEQ], ACT.Copy,
                                               scale=small[:, gain + k0 + k:gain + k0 + k + 1])
                        i.then_inc(s_th, 1)

            def exp(dst, src, scale=1.0, func=ACT.Exp):
                act.wait_ge(s_arg, arg.up())
                act.activation(dst, src, func, scale=scale).then_inc(s_exp, 1)

            def x_root():
                roots(2)
                act.wait_ge(s_rs, rs.up())

            def inv(t):
                return tiny[:, X_INV + t:X_INV + t + 1]

            def copy(dst, t):
                return act.activation(dst, LIN[t][:, :], ACT.Copy, scale=inv(t))

            def layer(l):
                act.wait_ge(s_sm, smc.up(32))
                unit(4, lambda t: copy(sm[:, t, :], t), early=x_root, feed=(hT, L_N1))
                unit(4, lambda t: copy(mqk_tok[:, t, :], t))
                roots(6)
                unit(4, lambda t: act.activation(mv[:, t, :, 0:P], LIN[t][:, :].rearrange("p (h d) -> p h d", h=4), ACT.Copy,
                                                 scale=inv(t)))
                act.wait_ge(s_arg, arg.up())
                act.activation(qkT.rearrange("p a t -> p (a t)"), conv_out.rearrange("p a t -> p (a t)"), ACT.Silu).then_inc(s_act, 1)
                exp(tn(128, 8), tn(112, 8), -1.0)
                exp(tn(144, 8), tn(136, 8), 1.0, ACT.Ln)
                tr.up(2)
                unit(4, lambda t: copy(rq[:, t, :], t), mid=lambda: split(cqT, 2, L_QN))
                tr.up()
                for i in range(2):
                    unit(1, lambda t: act.activation(qT[:, i, 2 * t:2 * t + 2, :].rearrange("p a t -> p (a t)"),
                                                     LIN[t][:, :], ACT.Copy))
                unit(4, lambda t: copy(rk[:, t, :], t))
                tr.up()
                unit(4, lambda t: copy(rv[:, t, :], t))
                tr.up()
                exp(tn(192, 8), tn(184, 8), -1.0)
                unit(4, lambda t: act.activation(mo[:, t, :], LIN[t][:, :], ACT.Sigmoid, scale=inv(t)))
                unit(4, lambda t: act.activation(rg[:, t, :], LIN[t][:, :], ACT.Silu, scale=inv(t)))
                tr.up(4)
                ad.up(8)

                def gate(g, n, **more):
                    unit(4, lambda t: act.activation(gates[:, g, t, n * 512:(n + 1) * 512], LIN[t][:, :], ACT.Sigmoid,
                                                     scale=inv(t)), **more)

                def decays():
                    for h in range(4):
                        act.wait_ge(s_ad, ad.up(1))
                        act.activation(wexp[:, h % SLOTS], wexp[:, h % SLOTS], ACT.Exp).then_inc(s_exp, 1)

                gate(0, 0, first=decays)
                ad.up(8)
                gate(0, 1, mid=lambda: roots(8))
                ad.up(4 + 8)
                gate(1, 0, mid=lambda: roots(8))
                ad.up(8)
                gate(1, 1, mid=lambda: split(mixT[:, 0], 4, L_MN))
                unit(2, mid=lambda: split(mixT[:, 1], 4, L_RN))
                exp(logits[:].rearrange("p h w -> p (h w)"), logits[:].rearrange("p h w -> p (h w)"))
                unit(2)
                unit(2)
                gate(0, 0)
                gate(0, 1)
                attend_latent()
                unit(2)
                unit(2)
                unit(2, mid=lambda: split(hT, KT // 2))
                unit(4, feed=(hT, None), fed=True)
                unit(4)
                feed_forward("ff_act", FF_GROUPS, l)

            def attend_latent():
                tr.up(HEADS_A)
                ad.up(4)
                ab.up(40)
                for j in range(2):
                    act.wait_ge(s_ab, ab.up())
                    dst = mixT[:, 2, 0, 2 * j:2 * j + 2, :].rearrange("p k t -> p (k t)")
                    act.activation(dst, AB[ad.n % 4][:, :], ACT.Copy).then_inc(s_th, 1)
                    ad.up()

            def glu(first=None, feed=None):
                if feed:
                    split(hT, KT // 2, feed)
                for i in range(3):
                    high()
                    if feed and i < 2:
                        split(hT, QK, feed, KT // 2 + QK * i)
                    if first and i == 1:
                        first()
                act.wait_ge(s_lin, lin.up())
                act.activation(gbuf[:, 0, :], LIN[0][:, 0:GLU], ACT.Silu, scale=inv(0)).then_inc(s_g, 1)
                act.wait_ge(s_used, pos.up(4))
                act.activation(gbuf[:, 1, :], LIN[1][:, 0:GLU], ACT.Silu, scale=inv(1)).then_inc(s_g, 1)
                high()

            def hidden_high():
                act.wait_ge(s_tr, tr.up())
                act.activation(heT[:, 0].rearrange("p k t -> p (k t)"), TR[(tr.n - 1) % 2][:, :], ACT.Copy).then_inc(s_th, 1)

            def feed_forward(name, groups, l):
                glu(first=x_root, feed=L_N2)
                act.dma_start(small[:], small_in[l + 1]).then_inc(s_sm, 16)
                act.dma_start(gain1, gains[0]).then_inc(s_sm, 16)
                with repeat(act, name, groups - 1, counts, per):
                    hidden_high()
                    glu()
                    high()
                    high()
                    pos.up(2)
                hidden_high()
                high()
                high()
                pos.up(2)

            def second():
                act.wait_ge(s_sm, smc.up(32))
                act.dma_start(bflat, alibi).then_inc(s_alibi, 16)
                act.activation(sw[:, 0, :], small[:, S_SW:S_G1], ACT.Copy).then_inc(s_sw, 1)
                act.wait_ge(s_arg, arg.up())

                def by_token(i):
                    return lambda t: copy(tok[i][:, t, :], t)

                def silu_conv(i):
                    act.wait_ge(s_arg, arg.up())
                    v = xbcT[i].rearrange("p a t -> p (a t)")
                    act.activation(v, v, ACT.Silu).then_inc(s_act, 1)

                def dt_logs():
                    exp(tn(464, 32), tn(432, 32), -1.0)
                    exp(tn(528, 32), tn(496, 32), 1.0, ACT.Ln)
                    act.activation(tiny[:, 720:736], small[:, S_AL:S_AL + 16], ACT.Exp).then_inc(s_exp, 1)

                unit(4, by_token(0), early=lambda: roots(2), first=x_root, feed=(hT, S_N1))
                unit(4, by_token(1), mid=dt_logs)
                unit(4, by_token(0), mid=lambda: silu_conv(0))
                unit(4, by_token(1), mid=lambda: silu_conv(1))
                unit(4, by_token(0), mid=lambda: silu_conv(2))
                unit(4, lambda t: copy(v2[:, t, :], t))
                for n in range(2):
                    unit(4, lambda t: act.activation(xn[:, t, n * 512:(n + 1) * 512], LIN[t][:, :], ACT.Silu, scale=inv(t)))
                tr.up(2 * 5 + 2 + 4)
                ad.up(2 + 2 + HEADS_A)
                lv = logits[:].rearrange("p h w -> p (h w)")

                def softmax_exp():
                    exp(lv, lv)
                    act.dma_start(gain2, gains[1]).then_inc(s_sm, 16)
                    act.dma_start(p_tok, p_in.rearrange("(t p) d -> p t d", p=P)).then_inc(s_sm, 16)

                for g in range(4):
                    for h in range(4 * g, 4 * g + 4):
                        act.wait_ge(s_ad, ad.up())
                        act.activation(wexp[:, h % SLOTS], wexp[:, h % SLOTS], ACT.Exp).then_inc(s_ex2, 1)
                    ad.up()
                    unit(4, lambda t: act.activation(gates[:, g // 2, t, (g % 2) * 512:(g % 2 + 1) * 512], LIN[t][:, :],
                                                     ACT.Sigmoid, scale=inv(t)), mid=softmax_exp if g == 1 else None)
                tr.up(HEADS_A)
                for j in range(2):
                    act.wait_ge(s_pv, LAYERS * HEADS_A + SSD_HEADS + 4 * (j + 1))
                    dst = mixT[:, 2, 0, 2 * j:2 * j + 2, :].rearrange("p k t -> p (k t)")
                    act.activation(dst, AB[ad.n % 4][:, :], ACT.Copy).then_inc(s_th, 1)
                    ad.up()
                roots(4)
                unit(2)
                unit(2)
                unit(4, feed=(mixT8, S_NS))
                unit(4, mid=lambda: split(hT, KT // 2))
                unit(4, feed=(hT, None), fed=True)
                unit(4, mid=lambda: split(cqT, QK))
                for n in range(2):
                    unit(1, lambda t: act.activation(ple[:, t, n * 512:(n + 1) * 512], LIN[t][:, :], ACT.Copy))
                split(hT, KT, S_N2)
                x_root()
                ad.up(2)
                for c in (832, 952):
                    exp(tiny[:, c:c + 8], tiny[:, c:c + 8])
                glu()
                with repeat(act, "moe_act", EXPERTS - 1, counts, per):
                    for _ in range(2):
                        hidden_high()
                        glu()
                        high()
                        high()
                        pos.up(2)
                hidden_high()
                glu()
                high()
                high()
                pos.up(2)
                hidden_high()
                high()
                high()
                pos.up(2)
                for n in range(2):
                    unit(4, lambda t: act.activation(tmpg2[n][:, t, :], LIN[t][:, :], ACT.Sigmoid),
                         feed=(hT, None) if n == 0 else None)
                roots(2)

            for _ in range(RING):
                high()
            with repeat(act, "layers_act", LAYERS, counts, per) as l:
                layer(l)
            second()

        @block.gpsimd
        def _(pool):
            nc.gpsimd.memset(ones[:], 1.0).then_inc(s_z, 1)
            pool.wait_ge(s_z, 1)
            nc.gpsimd.tensor_scalar(zeros[:], ones[:, 0:P], 0.0, None, ALU.mult)
            nc.gpsimd.memset(mv[:, :, :, P:P + 1], 1.0).then_inc(s_z, 1)
            with pool.Fori(0, TOTAL_Q // RING) as r:
                for i in range(RING):
                    pool.wait_ge(s_hi, r * RING + (i + 1))
                    nc.gpsimd.tensor_tensor(w_lo[:, i, :], raw[:, i, :], w_hi[:, i, :].bitcast(F32),
                                            ALU.subtract).then_inc(s_lo, 1)

        @block.vector
        def _(dve):
            lin, pos, tr, th, ab, ad, std, exps, la, ld, g, pv, xr = (
                Count(s_lin), Count(s_used), Count(s_tr), Count(s_th), Count(s_ab), Count(s_ad), Count(s_std),
                Count(s_exp), Count(s_la), Count(s_ld), Count(s_g), Count(s_pv), Count(s_x))
            smc, rs = Count(s_sm), Count(s_rs)
            own = Chain(s_ch_d, dve)
            smc.n = -16
            counts = [lin, pos, tr, th, ab, ad, std, exps, la, ld, g, pv, smc, rs, own]

            def unit(n, read=None):
                v = lin.up()
                if read is None:
                    pos.up(n)
                    return
                dve.wait_ge(s_lin, v)
                read(0)
                dve.wait_ge(s_used, pos.up(n))
                read(1)

            def col(at, i=0):
                return small[:, at + i:at + i + 1]

            def tc(at, i=0):
                return tiny[:, at + i:at + i + 1]

            def squares(v, junk, n, i):
                return dve.tensor_tensor_reduce(junk, v, v, 1.0 / n, 0.0, ALU.mult, ALU.add, tc(0, i))

            def rstd(n, to=32):
                v, s, r, t = (tiny[:, a:a + n] for a in (0, 16, 32, 48))
                dve.tensor_scalar(v, v, EPS, None, ALU.add).then_inc(s_var, 1)
                dve.wait_ge(s_std, std.up())
                own(dve.reciprocal(r, s))
                own(dve.tensor_tensor(t, r, r, ALU.mult))
                own(dve.tensor_tensor(t, t, v, ALU.mult))
                own(dve.tensor_scalar(t, t, -0.5, 1.5, ALU.mult, ALU.add))
                last = dve.tensor_tensor(tiny[:, to:to + n], r, t, ALU.mult)
                if to == 32:
                    own(last)
                return last

            def x_squares():
                for t in range(TT):
                    i = squares(x[:, t, :], xn[:, t, :], D, t)
                own(i)

            def x_stats(gain, then=None):
                split(hT, KT // 2, gain)
                x_squares()
                split(hT, KT // 2, gain, KT // 2)
                if then:
                    then()
                rstd(2, X_INV).then_inc(s_rs, 1)
                dve.wait_ge(s_rs, rs.up())

            def split(dst, nk, gain=None, start=0):
                for k0 in range(start, start + nk, 2):
                    dve.wait_ge(s_th, th.up())
                    tr.up()
                    b = TR[(tr.n - 1) % 2]
                    for k in range(2):
                        hi = dst[:, 0, k0 + k, :].bitcast(F32)
                        bk = b[:, k * SEQ:(k + 1) * SEQ]
                        if gain is None:
                            i = dve.tensor_tensor(dst[:, 1, k0 + k, :], bk, hi, ALU.subtract)
                        else:
                            i = dve.scalar_tensor_tensor(dst[:, 1, k0 + k, :], bk, col(gain, k0 + k), hi, ALU.mult, ALU.subtract)
                    i.then_inc(s_td, 1)

            def tr_bank():
                dve.wait_ge(s_tr, tr.up())
                return TR[(tr.n - 1) % 2]

            def ab_bank():
                ad.up()
                dve.wait_ge(s_ab, ab.up())
                return AB[(ad.n - 1) % 4]

            def log1p_exp_minus(f, n, exp_at):
                a, e, w, ln, d, z = (tiny[:, k:k + n] for k in exp_at)
                dve.scalar_tensor_tensor(a, f, -1.0, f, ALU.mult, ALU.max).then_inc(s_arg, 1)
                dve.wait_ge(s_exp, exps.up())
                dve.tensor_scalar(w, e, 1.0, None, ALU.add).then_inc(s_arg, 1)
                dve.wait_ge(s_exp, exps.up())
                own(dve.tensor_scalar(d, w, -1.0, None, ALU.add))
                own(dve.tensor_scalar(z, d, 0.0, None, ALU.is_equal))
                own(dve.tensor_tensor(d, d, z, ALU.add))
                own(dve.reciprocal(d, d))
                own(dve.tensor_tensor(ln, ln, e, ALU.mult))
                own(dve.tensor_tensor(ln, ln, d, ALU.mult))
                own(dve.tensor_tensor(z, z, e, ALU.mult))
                own(dve.tensor_tensor(ln, ln, z, ALU.add))

            def small_norms():
                dve.wait_ge(s_la, la.up(2))
                own(dve.tensor_copy(g16, sm[:, :, 320:336]))
                dve.tensor_scalar(g16[:, :, 0:8], g16[:, :, 0:8], 8 ** -0.5 * 64 ** -0.5, None, ALU.mult)
                for t in range(TT):
                    squares(sm[:, t, 0:256], xflat[:, 512 * t:512 * t + 256], 256, t)
                    squares(sm[:, t, 384:512], xflat[:, 512 * t + 256:512 * t + 384], P, 2 + t)
                own(dve.tensor_reduce(tiny[:, 52:54], sm[:, :, 256:320], AX.X, ALU.add))
                own(dve.tensor_scalar(tiny[:, 52:54], tiny[:, 52:54], 1.0 / 64, None, ALU.mult))
                for t in range(TT):
                    i = dve.tensor_scalar(sm[:, t, 256:320], sm[:, t, 256:320], tc(52, t), None, ALU.subtract)
                own(i)
                for t in range(TT):
                    i = squares(sm[:, t, 256:320], xflat[:, 64 * t:64 * t + 64], 64, 4 + t)
                own(i)
                rstd(6)
                for t in range(TT):
                    dve.tensor_scalar(sm[:, t, 0:256], sm[:, t, 0:256], tc(32, t), None, ALU.mult)
                    dve.scalar_tensor_tensor(sm[:, t, 384:512], sm[:, t, 384:512], tc(34, t), small[:, L_KV:L_KV + P],
                                             ALU.mult, ALU.mult)
                    dve.tensor_scalar(sm[:, t, 320:384], sm[:, t, 256:320], tc(36, t), None, ALU.mult)
                    i = dve.tensor_scalar(sm[:, t, 256:320], sm[:, t, 256:320], tc(36, t), None, ALU.mult)
                i.then_inc(s_nx, 1)

            def small_by_feature():
                split(cqT, 2, L_QN)
                b = tr_bank()
                dve.tensor_scalar(kidxT, b[:, 0:SEQ], col(L_KI), None, ALU.mult)
                dve.tensor_copy(ckvT, b[:, SEQ:2 * SEQ]).then_inc(s_td, 1)

            def gate_logs():
                ib = small[:, L_IB:L_IB + 8].rearrange("p (g h) -> p g h", g=2)
                fx = tn(120, TT, 4)
                dve.tensor_tensor(gif[:, :, 0:4], g16[:, :, 8:12], ib[:, 0:1, :].broadcast_to([P, TT, 4]), ALU.add)
                own(dve.tensor_tensor(fx, g16[:, :, 12:16], ib[:, 1:2, :].broadcast_to([P, TT, 4]), ALU.add))
                log1p_exp_minus(tiny[:, 120:128], 8, (112, 128, 136, 144, 152, 160))
                own(dve.tensor_scalar(fx, fx, 0.0, None, ALU.min))
                dve.tensor_tensor(gif[:, :, 4:8], fx, tn(144, TT, 4), ALU.subtract).then_inc(s_nx, 1)

            def conv(dst, src, tiles, taps, bias_at=None, f0=0):
                for j in range(4):
                    for f in range(tiles):
                        s, w = src[:, f, j:j + SEQ], col(taps, 4 * (f0 + f) + j)
                        if j == 0:
                            i = dve.tensor_scalar(dst[:, f, :], s, w, None if bias_at is None else col(bias_at, f0 + f),
                                                  ALU.mult, ALU.bypass if bias_at is None else ALU.add)
                        else:
                            i = dve.scalar_tensor_tensor(dst[:, f, :], s, w, dst[:, f, :], ALU.mult, ALU.add)
                    own(i)
                dve.memset(tc(1004), 0.0).then_inc(s_arg, 1)

            def gate_rows():
                dve.wait_ge(s_b, 32)
                b = tr_bank()
                dve.tensor_copy(rows[:, 0:2, :].rearrange("p a b -> p (a b)"), b[0:4, :]).then_inc(s_td, 1)
                dve.wait_ge(s_td, tr.back(0))
                own(dve.tensor_tensor_scan(rows[:, 4, :], ones[0:4, :], rows[:, 1, :], 0.0, ALU.mult, ALU.add))
                own(dve.tensor_tensor(rows[:, 0, :], rows[:, 0, :], rows[:, 4, :], ALU.subtract))
                own(dve.tensor_tensor_scan(rows[:, 1, :], ones[0:4, :], rows[:, 0, :], 0.0, ALU.mult, ALU.max))
                dve.tensor_scalar(rows[:, 2, :], rows[:, 1, :], -1.0, None, ALU.mult)
                dve.tensor_tensor(rows[:, 3, :], rows[:, 1, :], rows[:, 4, :], ALU.add).then_inc(s_nx, 1)

            def index_scores():
                for h in range(8):
                    b = ab_bank()
                    dst = work if h == 0 else relu_w
                    dve.tensor_scalar(dst[:, 0:P], b[:, 0:P], 0.0, g16[:, 0, h:h + 1], ALU.max, ALU.mult)
                    dve.tensor_scalar(dst[:, P:WIN], b[:, P:WIN], 0.0, g16[:, 1, h:h + 1], ALU.max, ALU.mult).then_inc(s_ad, 1)
                    dve.wait_ge(s_ad, ad.back(0))
                    if h:
                        own(dve.tensor_tensor(work, work, relu_w, ALU.add))
                dve.tensor_tensor(work[:, 0:P], work[:, 0:P], qmask, ALU.add)
                own(dve.tensor_tensor(work[:, SEQ:WIN], work[:, SEQ:WIN], qmask, ALU.add))

            def take(n):
                for _ in range(n):
                    for i, c in ((0, slice(0, P)), (1, slice(P, WIN))):
                        if i == 0:
                            dve.memset(tc(1001), 0.0)
                        j = dve.max(lflat[:, 2 * WIN + 8 * i:2 * WIN + 8 * i + 8], work[:, c])
                    own(j)
                    for i, c in ((0, slice(0, P)), (1, slice(P, WIN))):
                        if i == 0:
                            dve.memset(tc(1002), 0.0)
                        j = dve.match_replace(work[:, c], lflat[:, 2 * WIN + 8 * i:2 * WIN + 8 * i + 8], work[:, c], TAKEN)
                    own(j)

            def rotate(*which):
                cos4 = cosv.unsqueeze(2).broadcast_to([P, TT, 4, 64])
                sin4 = sinv.unsqueeze(2).broadcast_to([P, TT, 4, 64])
                for src, at, copied in which:
                    dve.wait_ge(s_la, la.up(copied))
                    x1, x2 = heads(src)[:, :, :, 0:64], heads(src)[:, :, :, 64:128]
                    t1, t2 = (xflat[:, a:a + 512].rearrange("p (t h d) -> p t h d", t=TT, h=4) for a in (at, at + 512))
                    dve.tensor_tensor(t1, x2, sin4, ALU.mult)
                    own(dve.tensor_tensor(t2, x1, sin4, ALU.mult))
                    dve.tensor_tensor(x1, x1, cos4, ALU.mult)
                    own(dve.tensor_tensor(x2, x2, cos4, ALU.mult))
                    dve.tensor_tensor(x1, x1, t1, ALU.subtract)
                    dve.tensor_tensor(x2, x2, t2, ALU.add).then_inc(s_rot, 1)

            def taken():
                own(dve.tensor_scalar(keep, work, TAKEN / 2, -BIG, ALU.is_gt, ALU.mult))
                dve.tensor_tensor(keep[:, 0:P], keep[:, 0:P], qmask, ALU.add)
                own(dve.tensor_tensor(keep[:, SEQ:WIN], keep[:, SEQ:WIN], qmask, ALU.add))

            def decay_args():
                for h in range(4):
                    b = ab_bank()
                    dve.scalar_tensor_tensor(wexp[:, h % SLOTS, 0:SEQ], b[:, 0:SEQ], acol[:, 0, h:h + 1], mask, ALU.add, ALU.add)
                    dve.scalar_tensor_tensor(wexp[:, h % SLOTS, SEQ:WIN], b[:, P:SEQ], acol[:, 1, h:h + 1], mask[:, 0:P],
                                             ALU.add, ALU.add).then_inc(s_ad, 1)

            def mlstm():
                def weights(h):
                    b = ab_bank()
                    dve.wait_ge(s_exp, exps.up())
                    dve.scalar_tensor_tensor(prob[:, h % SLOTS], b[:, 0:WIN], 64 ** -0.5, wexp[:, h % SLOTS], ALU.mult,
                                             ALU.mult).then_inc(s_ad, 1)

                weights(0)
                for h in range(4):
                    if h < 3:
                        weights(h + 1)
                    b = ab_bank()
                    dve.tensor_copy(m_out[:, :, h, :], b[:, 0:258].rearrange("p (t v) -> p t v", t=TT)).then_inc(s_ad, 1)

            def retain():
                def decayed(h):
                    b = ab_bank()
                    dve.tensor_tensor(prob[:, h % SLOTS, 0:SEQ], b[:, 0:SEQ], ret_decay[:, h, :], ALU.mult)
                    dve.tensor_tensor(prob[:, h % SLOTS, SEQ:WIN], b[:, SEQ:WIN], ret_decay[:, h, 0:P], ALU.mult).then_inc(s_ad, 1)

                decayed(0)
                for h in range(4):
                    if h < 3:
                        decayed(h + 1)
                    b = ab_bank()
                    dve.tensor_copy(r_out[:, :, h * P:(h + 1) * P], b[:, 0:SEQ].rearrange("p (t v) -> p t v", t=TT)).then_inc(s_ad, 1)

            def spread(v):
                return v.unsqueeze(3).broadcast_to([P, TT, 4, P])

            def head_norm(o, gate):
                sq = xflat[:, 0:1024].rearrange("p (t h d) -> p t h d", t=TT, h=4)
                mean, var, r = tn(56, TT, 4), tn(0, TT, 4), tn(32, TT, 4)
                own(dve.tensor_reduce(mean, o, AX.X, ALU.add))
                own(dve.tensor_scalar(mean, mean, 1.0 / P, None, ALU.mult))
                own(dve.tensor_tensor(o, o, spread(mean), ALU.subtract))
                own(dve.tensor_tensor(sq, o, o, ALU.mult))
                own(dve.tensor_reduce(var, sq, AX.X, ALU.add))
                own(dve.tensor_scalar(var, var, 1.0 / P, None, ALU.mult))
                rstd(8)
                own(dve.tensor_tensor(o, o, spread(r), ALU.mult))
                dve.tensor_tensor(o, o, heads(gate), ALU.mult).then_inc(s_nx, 1)

            row = tiny[:, 208:224].rearrange("p (t h) -> p t h", t=TT)
            score_parts = ((0, logits[:, :, 0:P], P), (1, logits[:, :, P:WIN], SEQ))

            def row_stat(op):
                for t, v, n in score_parts:
                    i = dve.tensor_reduce(row[:, t, :], v, AX.X, op)
                own(i)

            def less_maximum():
                for t, v, n in score_parts:
                    i = dve.tensor_tensor(v, v, row[:, t, :].unsqueeze(2).broadcast_to([P, HEADS_A, n]), ALU.subtract)
                i.then_inc(s_arg, 1)

            def over_sum():
                own(dve.reciprocal(tiny[:, 208:224], tiny[:, 208:224]))
                for t, v, n in score_parts:
                    i = dve.tensor_tensor(v, v, row[:, t, :].unsqueeze(2).broadcast_to([P, HEADS_A, n]), ALU.mult)
                i.then_inc(s_nx, 1)

            def by_key(h):
                b = tr_bank()
                v = pv.up()
                if h >= SLOTS:
                    dve.wait_ge(s_pv, pv.back(SLOTS))
                dve.tensor_copy(prob[:, h % SLOTS], b[:, 0:WIN]).then_inc(s_td, 1)

            def attend_latent():
                def latent(j):
                    dve.wait_ge(s_pv, pv.back(HEADS_A - 2 - 2 * j if j == 3 else 1))
                    ad.up()
                    dve.tensor_copy(two_heads(j), AB[(ad.n - 1) % 4][:, :]).then_inc(s_ad, 1)

                by_key(0)
                by_key(1)
                for j in range(4):
                    if j < 3:
                        by_key(2 * j + 2)
                        latent(j)
                        by_key(2 * j + 3)
                    else:
                        latent(j)
                for j in range(2):
                    dve.wait_ge(s_th, th.up())
                    ab.up()
                    ad.up()
                    dst = mixT[:, 2, 1, 2 * j:2 * j + 2, :].rearrange("p k t -> p (k t)")
                    hi = mixT[:, 2, 0, 2 * j:2 * j + 2, :].rearrange("p k t -> p (k t)").bitcast(F32)
                    dve.tensor_tensor(dst, AB[(ad.n - 1) % 4][:, :], hi, ALU.subtract).then_inc(s_ad, 1)

            def two_heads(j):
                return (qlatA if j < 2 else qlatB)[:, 2 * (j % 2):2 * (j % 2) + 2, :].rearrange("p a t -> p (a t)")

            def branch(g, n, first=False, last=False):
                def read(t):
                    y, gt = xn[:, t, n * 512:(n + 1) * 512], gates[:, g, t, n * 512:(n + 1) * 512]
                    if first:
                        dve.tensor_tensor(y, LIN[t][:, :], gt, ALU.mult).then_inc(s_ld, 1)
                        ld.up()
                        return
                    dve.tensor_tensor(tmpy[:, t, :], LIN[t][:, :], gt, ALU.mult).then_inc(s_ld, 1)
                    dve.wait_ge(s_ld, ld.up())
                    i = dve.tensor_tensor(y, y, tmpy[:, t, :], ALU.add)
                    if last and t == 1:
                        i.then_inc(s_nx, 1)
                return read

            def residual(n):
                def read(t):
                    v = x[:, t, n * 512:(n + 1) * 512]
                    dve.tensor_tensor(v, LIN[t][:, :], v, ALU.add).then_inc(s_ld, 1)
                    dve.wait_ge(s_ld, ld.up())
                    if t == 1:
                        dve.memset(tc(1003), 0.0).then_inc(s_nx, 1)
                return read

            def glu(scale=None):
                lin.up()
                for t in range(TT):
                    dve.wait_ge(s_g, g.up())
                    if t == 1:
                        pos.up(4)
                    ld.up()
                    i = dve.scalar_tensor_tensor(he[:, t, :], LIN[t][:, GLU:2 * GLU], scale(t) if scale else tc(X_INV, t),
                                                 gbuf[:, t, :], ALU.mult, ALU.mult)
                    i.then_inc(s_ld, 1)

            def hidden_low():
                dve.wait_ge(s_th, th.up())
                tr.up()
                b = TR[(tr.n - 1) % 2]
                dve.tensor_tensor(heT[:, 1].rearrange("p k t -> p (k t)"), b[:, :],
                                  heT[:, 0].rearrange("p k t -> p (k t)").bitcast(F32), ALU.subtract).then_inc(s_td, 1)

            def x_back():
                for n in range(2):
                    for t in range(TT):
                        v = x[:, t, n * 512:(n + 1) * 512]
                        i = dve.tensor_tensor(v, AB[2 * t + n][:, :], v, ALU.add)
                    i.then_inc(s_x, 1)
                dve.wait_ge(s_x, xr.up(2))

            def feed_forward(name, groups):
                glu()
                with repeat(dve, name, groups - 1, counts, per):
                    hidden_low()
                    glu()
                    pos.up(2)
                hidden_low()
                dve.wait_ge(s_used, pos.up(2))
                x_back()

            def layer(l):
                dve.wait_ge(s_sm, smc.up(32))
                x_stats(L_N1)
                small_norms()
                dve.wait_ge(s_la, la.up(2))
                own(dve.memset(conv_in[:, :, 0:3], 0.0))
                for j in range(2):
                    b = tr_bank()
                    dve.tensor_copy(conv_in[:, 2 * j:2 * j + 2, 3:SEQ + 3],
                                    b[:, :].rearrange("p (a t) -> p a t", a=2)).then_inc(s_td, 1)
                dve.wait_ge(s_td, tr.back(0))
                conv(conv_out, conv_in, 4, L_CW)
                gate_logs()
                small_by_feature()
                for n in (4, 4, 4, 4, 1, 1, 4, 4, 4, 4, 4, 4, 4, 4):
                    unit(n)
                gate_rows()
                rotate((rq, 0, 4))
                index_scores()
                rotate((rk, 1024, 6))
                b = tr_bank()
                dve.tensor_copy(tiny[:, 184:192], b[:, 8:16]).then_inc(s_arg, 1)
                dve.tensor_copy(tiny[:, 176:184], b[:, 0:8]).then_inc(s_td, 1)
                dve.wait_ge(s_td, tr.back(0))
                exps.up()
                take(TOPK // 8)
                taken()
                for dst in (rqT[:, 0], rqT[:, 1]):
                    for j in range(2):
                        b = tr_bank()
                        dve.tensor_copy(dst[:, 2 * j:2 * j + 2, :].rearrange("p a t -> p (a t)"), b[:, :]).then_inc(s_td, 1)
                decay_args()
                dve.wait_ge(s_b, 64)
                dve.wait_ge(s_ad, ad.back(0))
                own(dve.tensor_tensor(logits[:], bias[:], keep.unsqueeze(1).broadcast_to([P, HEADS_A, WIN]), ALU.add))
                mlstm()
                dve.wait_ge(s_ad, ad.back(0))
                total = m_out[:, :, :, P:P + 1].rearrange("p t h a -> p t (h a)")
                own(dve.scalar_tensor_tensor(den, total, -1.0, total, ALU.mult, ALU.max))
                own(dve.tensor_tensor(den, den, em, ALU.max))
                own(dve.reciprocal(den, den))
                own(dve.tensor_tensor(m_out[:, :, :, 0:P], m_out[:, :, :, 0:P], spread(den), ALU.mult))
                dve.wait_ge(s_la, la.up(4))
                head_norm(m_out[:, :, :, 0:P], mo)
                for j in range(4):
                    b = ab_bank()
                    dst = (qlatA if j < 2 else qlatB)[:, j % 2:4:2, :]
                    dve.tensor_scalar(dst, b[:, :].rearrange("p (a t) -> p a t", a=2), 64 ** -0.5, None, ALU.mult).then_inc(s_ad, 1)
                retain()
                dve.wait_ge(s_ad, ad.back(0))
                dve.wait_ge(s_la, la.up(2))
                head_norm(heads(r_out), rg)
                for h in range(HEADS_A):
                    b = ab_bank()
                    i = dve.tensor_tensor(logits[:, h, :], b[:, 0:WIN], logits[:, h, :], ALU.add)
                    i.then_inc(s_ad, 1)
                dve.wait_ge(s_ad, ad.back(0))
                split(mixT[:, 0], 4, L_MN)
                row_stat(ALU.max)
                less_maximum()
                split(mixT[:, 1], 4, L_RN)
                dve.wait_ge(s_la, la.up(8))
                unit(2, branch(0, 0, first=True))
                unit(2, branch(0, 1, first=True))
                dve.wait_ge(s_exp, exps.up())
                row_stat(ALU.add)
                unit(2, branch(1, 0))
                over_sum()
                unit(4)
                unit(4)
                attend_latent()
                unit(2, branch(1, 1))
                dve.wait_ge(s_la, la.up(4))
                unit(2, branch(0, 0, last=True))
                split(hT, KT // 2)
                unit(2, branch(0, 1, last=True))
                split(hT, KT // 2, None, KT // 2)
                unit(4, residual(0))
                unit(4, residual(1))
                x_stats(L_N2)
                feed_forward("ff_dve", FF_GROUPS)

            def first_of(v, out, at):
                m = tn(at, TT, 1)
                own(dve.tensor_reduce(m, v, AX.X, ALU.max))
                own(dve.tensor_tensor(out, v, m.broadcast_to([P, TT, 4]), ALU.is_equal))
                own(dve.tensor_tensor(out, out, tn(772, 1, 4).broadcast_to([P, TT, 4]), ALU.mult))
                own(dve.tensor_reduce(tn(776, TT, 1), out, AX.X, ALU.max))
                own(dve.tensor_tensor(out, out, tn(776, TT, 1).broadcast_to([P, TT, 4]), ALU.is_equal))

            def rows_in(n):
                b = ab_bank()
                dve.tensor_copy(small_rows[0:n], b[0:n, 0:SEQ]).then_inc(s_ad, 1)

            def route():
                for i in range(4):
                    own(dve.memset(tiny[:, 772 + i:773 + i], 4.0 - i))
                lg = tn(780, TT, 20)
                b = ab_bank()
                for t in range(TT):
                    i = dve.scalar_tensor_tensor(lg[:, t, :], b[:, 20 * t:20 * t + 20], tc(X_INV, t),
                                                 small[:, S_BR:S_BR + 20], ALU.mult, ALU.add)
                i.then_inc(s_ad, 1)
                dve.wait_ge(s_ad, ad.back(0))
                four = [P, TT, 4]
                gp, og, ei, o1, e2, o2, cig = (tn(832 + 8 * i, TT, 4) for i in range(7))
                pw, m1, m2, ex, w1, w2 = (tn(900 + 2 * i, TT, 1) for i in range(6))
                own(dve.tensor_reduce(m1, lg[:, :, 0:4], AX.X, ALU.max))
                dve.tensor_tensor(gp, lg[:, :, 0:4], m1.broadcast_to(four), ALU.subtract).then_inc(s_arg, 1)
                dve.wait_ge(s_exp, exps.up())
                own(dve.tensor_reduce(m1, gp, AX.X, ALU.add))
                own(dve.reciprocal(m1, m1))
                own(dve.tensor_tensor(gp, gp, m1.broadcast_to(four), ALU.mult))
                first_of(gp, og, 900)
                m = tn(920, TT, 16).rearrange("p t (g j) -> p t g j", g=4)
                own(dve.tensor_tensor(m, lg[:, :, 4:20].rearrange("p t (g j) -> p t g j", g=4),
                                      og.unsqueeze(3).broadcast_to([P, TT, 4, 4]), ALU.mult))
                own(dve.tensor_reduce(ei, m.rearrange("p t g j -> p t j g"), AX.X, ALU.add))
                first_of(ei, o1, 902)
                own(dve.scalar_tensor_tensor(e2, o1, -BIG, ei, ALU.mult, ALU.add))
                first_of(e2, o2, 904)
                own(dve.memset(tiny[:, 952:960], 0.0))
                dve.tensor_tensor(tn(952, TT, 4), m2.broadcast_to(four), m1.broadcast_to(four), ALU.subtract).then_inc(s_arg, 1)
                dve.wait_ge(s_exp, exps.up())
                ex = tn(952, TT, 4)[:, :, 0:1]
                own(dve.tensor_scalar(w1, ex, 1.0, None, ALU.add))
                own(dve.reciprocal(w1, w1))
                own(dve.tensor_tensor(w1, w1, pw, ALU.mult))
                own(dve.tensor_tensor(w2, w1, ex, ALU.mult))
                own(dve.tensor_tensor(o1, o1, w1.broadcast_to(four), ALU.mult))
                own(dve.tensor_tensor(o2, o2, w2.broadcast_to(four), ALU.mult))
                own(dve.tensor_tensor(cig, o1, o2, ALU.add))
                for t in range(TT):
                    i = dve.tensor_scalar(cig[:, t, :], cig[:, t, :], tc(X_INV, t), None, ALU.mult)
                own(i)
                own(dve.tensor_tensor(comb.rearrange("p t (g j) -> p t g j", g=4), og.unsqueeze(3).broadcast_to([P, TT, 4, 4]),
                                      cig.unsqueeze(2).broadcast_to([P, TT, 4, 4]), ALU.mult))

            def second():
                dve.wait_ge(s_sm, smc.up(32))
                g = small[:, S_N1:S_N1 + KT]
                dve.tensor_tensor(g, g, small[:, S_G1:S_G1 + KT], ALU.mult).then_inc(s_arg, 1)
                dve.memset(conv2[:, :, 0:3], 0.0)
                split(hT, KT // 2, S_N1)
                dve.wait_ge(s_sw, 1)
                dve.tensor_tensor(sw[:, 1, :], small[:, S_SW:S_G1], sw[:, 0, :].bitcast(F32), ALU.subtract).then_inc(s_nx, 1)
                x_squares()
                split(hT, QK, S_N1, KT // 2)
                for t in range(TT):
                    i = dve.tensor_tensor(xn[:, t, :], x[:, t, :], gain1, ALU.mult)
                own(i)
                split(hT, QK, S_N1, KT // 2 + QK)
                rstd(2)
                first_inv = tn(1010, TT, 1).rearrange("p t a -> p (t a)")
                own(dve.tensor_copy(first_inv, tiny[:, 32:34]))
                for t in range(TT):
                    i = squares(xn[:, t, :], x[:, t, :], D, t)
                own(i)
                own(dve.tensor_tensor(tiny[:, 0:2], tiny[:, 0:2], first_inv, ALU.mult))
                own(dve.tensor_tensor(tiny[:, 0:2], tiny[:, 0:2], first_inv, ALU.mult))
                rstd(2)
                dve.tensor_tensor(tiny[:, X_INV:X_INV + 2], tiny[:, 32:34], first_inv, ALU.mult).then_inc(s_rs, 1)
                dve.wait_ge(s_rs, rs.up())
                for t in range(TT):
                    dve.tensor_scalar(x[:, t, :], xn[:, t, :], first_inv[:, t:t + 1], None, ALU.mult)
                unit(4)
                rows_in(16)
                b = ab_bank()
                f = tn(400, TT, 16)
                for t in range(TT):
                    i = dve.scalar_tensor_tensor(f[:, t, :], b[:, 16 * t:16 * t + 16], tc(X_INV, t),
                                                 small[:, S_DTB:S_DTB + 16], ALU.mult, ALU.add)
                i.then_inc(s_ad, 1)
                dve.wait_ge(s_ad, ad.back(0))
                log1p_exp_minus(tiny[:, 400:432], 32, (432, 464, 496, 528, 560, 592))
                own(dve.tensor_scalar(f, f, 0.0, None, ALU.max))
                own(dve.tensor_tensor(dt, f, tn(528, TT, 16), ALU.add))
                dve.wait_ge(s_exp, exps.up())
                own(dve.tensor_scalar(tiny[:, 720:736], tiny[:, 720:736], -1.0, None, ALU.mult))
                dve.tensor_tensor(da, dt, tiny[:, 720:736].unsqueeze(1).broadcast_to([P, TT, 16]), ALU.mult).then_inc(s_nx, 1)

                def conv_chunk(c):
                    for j in range(2):
                        b = tr_bank()
                        dve.tensor_copy(conv2[:, 2 * j:2 * j + 2, 3:SEQ + 3],
                                        b[:, :].rearrange("p (a t) -> p a t", a=2)).then_inc(s_td, 1)
                    dve.wait_ge(s_td, tr.back(0))
                    conv(xbcT[c], conv2, 4, S_CW, S_CB, 4 * c)

                unit(4)
                conv_chunk(0)
                unit(4)
                conv_chunk(1)
                unit(4)
                conv_chunk(2)
                for i in range(2):
                    unit(4)
                    for j in range(2):
                        b = tr_bank()
                        dve.tensor_copy(qkT2[:, i, 2 * j:2 * j + 2, :].rearrange("p a t -> p (a t)"), b[:, :]).then_inc(s_td, 1)
                unit(4)
                b = tr_bank()
                dve.tensor_copy(rows2[:, 0, :], b[0:16, 0:SEQ]).then_inc(s_td, 1)
                dve.wait_ge(s_td, tr.back(0))
                dve.tensor_tensor_scan(rows2[:, 1, :], ones[:], rows2[:, 0, :], 0.0, ALU.mult, ALU.add).then_inc(s_nx, 1)
                unit(4)
                b = tr_bank()
                dve.tensor_copy(cs, b[:, 0:32].rearrange("p (t n) -> p t n", t=TT)).then_inc(s_td, 1)
                for t in range(TT):
                    for i in range(2):
                        b = tr_bank()
                        dve.tensor_copy(xs[:, t, i * 512:(i + 1) * 512], b[:, :]).then_inc(s_td, 1)
                for g in range(2):
                    b = ab_bank()
                    dve.tensor_copy(cb[:, g, :], b[:, 0:WIN]).then_inc(s_ad, 1)
                dve.wait_ge(s_alibi, 16)
                for h in range(HEADS_A):
                    b = ab_bank()
                    dve.scalar_tensor_tensor(logits[:, h, :], b[:, 0:WIN], 64 ** -0.5, bias[:, h, :], ALU.mult,
                                             ALU.add).then_inc(s_ad, 1)
                dve.wait_ge(s_ad, ad.back(0))

                def by_head(v):
                    return v.rearrange("p t (h d) -> p t h d", h=SSD_HEADS)

                def gate_z(i):
                    dve.wait_ge(s_ad, ad.back(0))
                    cols = slice(512 * i, 512 * (i + 1))
                    own(dve.tensor_tensor(yb[:, :, cols], yb[:, :, cols], xn[:, :, cols], ALU.mult))
                    for t in range(TT):
                        j = squares(yb[:, t, cols], xn[:, t, cols], 512, 2 * t + i)
                    own(j)

                def over(v):
                    return v.unsqueeze(3).broadcast_to([P, TT, SSD_HEADS, 64])

                dve.wait_ge(s_la, la.up(2 * 8))
                for g in range(4):
                    for h in range(4 * g, 4 * g + 4):
                        b = ab_bank()
                        if h >= SLOTS:
                            dve.wait_ge(s_pp, h - SLOTS + 1)
                        dve.scalar_tensor_tensor(wexp[:, h % SLOTS, 0:SEQ], b[:, 0:SEQ], cs[:, 0, h:h + 1], mask,
                                                 ALU.subtract, ALU.add)
                        dve.scalar_tensor_tensor(wexp[:, h % SLOTS, SEQ:WIN], b[:, P:SEQ], cs[:, 1, h:h + 1], mask[:, 0:P],
                                                 ALU.subtract, ALU.add).then_inc(s_ad, 1)
                    if g == 0:
                        skip = small[:, S_DS:S_DS + 16].unsqueeze(1).broadcast_to([P, TT, 16])
                        dve.tensor_tensor(by_head(yb), by_head(xs), over(skip), ALU.mult)
                        dve.tensor_tensor(by_head(xdt), by_head(xs), over(dt), ALU.mult).then_inc(s_nx, 1)
                    for h in range(4 * g, 4 * g + 4):
                        dve.wait_ge(s_ex2, h + 1)
                        dve.tensor_tensor(prob[:, h % SLOTS], wexp[:, h % SLOTS], cb[:, h // 8, :], ALU.mult).then_inc(s_pp, 1)
                    if g == 0:
                        row_stat(ALU.max)
                        less_maximum()
                    elif g == 2:
                        dve.wait_ge(s_exp, exps.up())
                        row_stat(ALU.add)
                    elif g == 3:
                        over_sum()
                    unit(4)
                    pv.up(4)
                    dve.wait_ge(s_pv, pv.back(0))
                    ad.up()
                    yv = by_head(yb)[:, :, 4 * g:4 * g + 4, :]
                    src = AB[(ad.n - 1) % 4][:, :].rearrange("p (h t d) -> p t h d", h=4, t=TT)
                    dve.tensor_tensor(yv, src, yv, ALU.add).then_inc(s_ad, 1)
                    if g == 1:
                        gate_z(0)
                for h in range(HEADS_A):
                    by_key(h)
                for j in range(2):
                    dve.wait_ge(s_th, th.up())
                    ad.up()
                    dst = mixT[:, 2, 1, 2 * j:2 * j + 2, :].rearrange("p k t -> p (k t)")
                    hi = mixT[:, 2, 0, 2 * j:2 * j + 2, :].rearrange("p k t -> p (k t)").bitcast(F32)
                    dve.tensor_tensor(dst, AB[(ad.n - 1) % 4][:, :], hi, ALU.subtract).then_inc(s_ad, 1)
                gate_z(1)
                rstd(4)
                for t in range(TT):
                    for g in range(2):
                        v = yb[:, t, g * 512:(g + 1) * 512]
                        i = dve.tensor_scalar(v, v, tc(32, 2 * t + g), None, ALU.mult)
                i.then_inc(s_nx, 1)
                dve.wait_ge(s_la, la.up(2 * 4))
                unit(2, branch(0, 0, first=True))
                unit(2, branch(0, 1, first=True))
                split(mixT8, KT, S_NS)
                unit(4, branch(1, 0, last=True))
                split(hT, KT // 2)
                unit(4, branch(1, 1, last=True))
                split(hT, KT // 2, None, KT // 2)
                unit(4, residual(0))
                split(cqT, QK)
                unit(4, residual(1))
                unit(1)
                unit(1)
                x_stats(S_N2, then=lambda: rows_in(20))
                route()
                glu(lambda t: comb[:, t, 0:1])
                with repeat(dve, "moe_dve", EXPERTS - 1, counts, per) as e:
                    for i in range(2):
                        hidden_low()
                        glu(lambda t: comb[:, t, bass.ds(e + i, 1)])
                        pos.up(2)
                hidden_low()
                glu(lambda t: comb[:, t, EXPERTS - 1:EXPERTS])
                pos.up(2)
                hidden_low()
                dve.wait_ge(s_used, pos.up(2))
                x_back()
                split(hT, KT)
                dve.wait_ge(s_la, la.up(4))
                for n in range(2):
                    for t in range(TT):
                        cols = slice(n * 512, (n + 1) * 512)
                        dve.wait_ge(s_la, la.up())
                        own(dve.tensor_tensor(ple[:, t, cols], ple[:, t, cols], tmpg2[n][:, t, :], ALU.mult))
                        own(dve.tensor_tensor(x[:, t, cols], x[:, t, cols], ple[:, t, cols], ALU.add))
                        own(squares(x[:, t, cols], xn[:, t, cols], D, 2 * n + t))
                own(dve.tensor_tensor(tiny[:, 0:2], tiny[:, 0:2], tiny[:, 2:4], ALU.add))
                dve.wait_ge(s_sm, smc.up(32))
                rstd(2)
                for t in range(TT):
                    dve.scalar_tensor_tensor(xn[:, t, :], x[:, t, :], tc(32, t), gain2, ALU.mult, ALU.mult).then_inc(s_x, 1)

            dve.wait_ge(s_z, 2)
            for i in range(TT):
                dve.wait_ge(s_bf, i + 1)
                dve.tensor_copy(windows[:, i * WIN:(i + 1) * WIN], bank[i][0:HEADS_A, 0:WIN]).then_inc(s_bd, 1)
            dve.wait_ge(s_cst, 32)
            for _ in range(2):
                dve.memset(tiny[:, 1000:1001], 0.0).then_inc(s_x, 1)
                dve.wait_ge(s_x, xr.up())
            with repeat(dve, "layers_dve", LAYERS, counts + [xr], per) as l:
                layer(l)
            second()


def split_rows(w):
    k, n = w.shape
    q = w.reshape(k // (QK * P), QK, P, n // QC, QC).transpose(3, 0, 2, 1, 4)
    return q.reshape(-1, P, QK * QC)


def glu_rows(g, u, d):
    groups = g.shape[1] // GLU
    gu = [split_rows(np.concatenate([g[:, i * GLU:(i + 1) * GLU], u[:, i * GLU:(i + 1) * GLU]], 1)) for i in range(groups)]
    dn = [split_rows(d[i * GLU:(i + 1) * GLU]) for i in range(groups)]
    out = [gu[0]]
    for i in range(1, groups):
        out += [gu[i], dn[i - 1]]
    return out + [dn[-1]]


def columns(v):
    return v.reshape(-1, P).T


def layer_stream(a, l):
    w = a["w_in"][l]
    at = np.cumsum([0, 256, 256, 512, 4, 4, 512, 256, 64, 8, 128, 512, 512, 512, 512, 1024, 1024, 1024])
    mq, mk, mv, mi, mf, mo, cq, kidx, widx, ckv, rq, rk, rv, rg, gm, ga, gr = (w[:, at[i]:at[i + 1]] for i in range(17))
    small = np.concatenate([cq, kidx, widx, mi, mf, np.zeros((D, 48), np.float32), ckv], 1)
    p = {n: a[n][l] for n in ("p_m", "p_a", "p_r")}
    pr = split_rows(p["p_r"])
    parts = [split_rows(small), split_rows(np.concatenate([mq, mk], 1)), split_rows(mv), split_rows(rq),
             split_rows(a["a_wuq"][l]), split_rows(a["a_wuq_idx"][l]), split_rows(rk), split_rows(rv), split_rows(mo),
             split_rows(rg), split_rows(gm), split_rows(gr), split_rows(p["p_m"]), pr[:len(pr) // 2],
             split_rows(ga), pr[len(pr) // 2:], split_rows(p["p_a"]), split_rows(a["w_out"][l])]
    return parts + glu_rows(a["w_gate"][l], a["w_up"][l], a["w_down"][l])


def second_stream(a):
    w = a["w_in_2"][0]
    at = np.cumsum([0, 512, 512, 512, 1024, 1536, 16, 1024, 1024])
    q, k, v, z, xbc, _, ga, gb = (w[:, at[i]:at[i + 1]] for i in range(8))
    wide = lambda n: np.concatenate(list(a[n][0]), 1)
    parts = [split_rows(m) for m in (xbc, q, k, v, z, ga, gb, a["w_out_a_2"][0], a["w_out_b_2"][0], a["w_out_2"][0])]
    parts.append(split_rows(a["w_ple_proj_2"][0]))
    parts += glu_rows(wide("w_gate_2"), wide("w_up_2"), np.concatenate(list(a["w_down_2"][0]), 0))
    return parts + [split_rows(a["w_ple_gate_2"][0])]


def second_params(a):
    rep = lambda v: np.broadcast_to(v, (P, v.size))
    cw = a["conv_w_2"][0].reshape(4, 12, P).transpose(2, 1, 0).reshape(P, 48)
    dtw = a["w_in_2"][0][:, 4096:4112]
    sw = np.concatenate([dtw, a["w_rg_2"][0], a["w_re_2"][0]], 1).reshape(KT, P, 36).transpose(1, 0, 2).reshape(P, 8 * 36)
    return np.concatenate([columns(a["mix_norm_g_2"][0]), columns(a["ffn_norm_g_2"][0]), columns(a["ssd_norm_g_2"][0]), cw,
                           columns(a["conv_b_2"][0]), rep(a["dt_bias_2"][0]), rep(a["a_log_2"][0]), rep(a["d_skip_2"][0]),
                           rep(a["b_rg_2"][0]), rep(a["b_re_2"][0]), sw, columns(a["final_norm_g"])], 1)


def alibi_bias():
    i = np.arange(P)
    out = np.zeros((P, HEADS_A, WIN), np.float32)
    for t, c, n in ((0, 0, P), (1, P, SEQ)):
        dist = (t * P + i)[:, None] - np.arange(n)[None, :]
        for h in range(HEADS_A):
            out[:, h, c:c + n] = np.where(dist >= 0, -2.0 ** -(h + 1) * dist, -BIG)
    return out.reshape(P, HEADS_A * WIN)


def layer_params(a, l):
    rep = lambda v: np.broadcast_to(v, (P, v.size))
    cw = a["m_conv"][l].reshape(4, 4, P).transpose(2, 1, 0).reshape(P, 16)
    uk = a["a_wuk"][l].reshape(4, P, P).transpose(1, 0, 2).reshape(P, 512)
    uv = a["a_wuv"][l].transpose(1, 0, 2).reshape(P, 512)
    ki = np.concatenate([a["a_kidx_g"][l]] * 2)
    return np.concatenate([columns(a["norm1_g"][l]), columns(a["norm2_g"][l]), columns(a["a_qnorm_g"][l]), columns(ki),
                           columns(a["m_norm_g"][l]), columns(a["r_norm_g"][l]), cw, rep(a["a_kvnorm_g"][l]),
                           rep(a["m_ibias"][l]), rep(a["m_fbias"][l]), uk, uv], 1)


def constants():
    f = np.float32
    i = np.arange(P)
    pos = np.arange(SEQ)
    mask = np.where(pos[None, :] >= i[:, None], 0, -BIG).astype(f)
    qmask = np.where(i[None, :] <= i[:, None], 0, -BIG).astype(f)
    lg = np.log1p(-np.exp2(-5.0 - np.arange(4)))
    diff = pos[None, :] - i[:, None]
    ret = [np.where(diff >= 0, np.exp(np.maximum(diff, 0) * g) * P ** -0.5, 0).astype(f) for g in lg]
    ang = pos.astype(f)[:, None] * (f(10000.0) ** (-np.linspace(0, 1, 64).astype(f)))[None, :]
    by = lambda v: v.astype(f).reshape(TT, P, 64).transpose(1, 0, 2).reshape(P, 128)
    const = np.concatenate([np.eye(P, dtype=f), mask, qmask, *ret, by(np.cos(ang)), by(np.sin(ang))], 1)
    half = BUCKETS // 2
    onehot = np.zeros((BUCKETS, TT, WIN), f)
    for t in range(TT):
        for j in range(WIN):
            dist = t * P + P - 1 - j
            if dist >= 0:
                b = dist if dist < half else min(half + int(np.log(dist / half) / math.log(128 / half) * half), BUCKETS - 1)
                onehot[b, t, j] = 1
    return const, onehot


def kernel(**a):
    import concourse.bacc as bacc
    from concourse.bass_utils import run_bass_kernel_spmd

    a = {k: np.asarray(v) for k, v in a.items()}
    const, onehot = constants()
    second = second_params(a)
    quarters = []
    for l in range(LAYERS):
        quarters += layer_stream(a, l)
    quarters += second_stream(a)
    assert sum(len(v) for v in quarters) == TOTAL_Q
    arrays = {
        "stream": np.concatenate(quarters),
        "const": const,
        "small_in": np.stack([layer_params(a, l) for l in range(LAYERS)]
                             + [np.concatenate([second, np.zeros((P, L_END - S_END), np.float32)], 1)]),
        "x_in": np.ascontiguousarray(a["x"][0]),
        "onehot": onehot,
        "alibi": alibi_bias(),
        "gains": np.stack([np.broadcast_to(a[n], (P, D)) for n in ("final_norm_g", "final_norm_g_2")]),
        "p_in": np.ascontiguousarray(a["p_2"][0, 0]),
        "relb": a["rel_bias"],
    }
    per = {}
    for trial in range(2):
        nc = bacc.Bacc("TRN2", target_bir_lowering=False, num_devices=1, dynamic_dma_scratch_size=1024)
        t = {n: nc.dram_tensor(f"in_{n}", v.shape, F32, kind="ExternalInput").ap() for n, v in arrays.items()}
        scratch = nc.dram_tensor("bias_windows", [TT, P, HEADS_A * WIN], F32, kind="Internal").ap()
        out = nc.dram_tensor("out", [SEQ, D], F32, kind="ExternalOutput").ap()
        program(nc, t["stream"], t["const"], t["small_in"], t["x_in"], t["onehot"], t["relb"], scratch,
                t["alibi"], t["gains"], t["p_in"], out, per)
    r = run_bass_kernel_spmd(nc, [{f"in_{n}": v for n, v in arrays.items()}], core_ids=[0])
    return r.results[0]["out"][None]
```
